# Optimizing a Trainium2 kernel written in Bass

```python
import jax, jax.numpy as jnp
from jax import lax
import numpy as np

D_MODEL = 1024
BATCH = 1
SEQ = 512
DEPTH = 1

RET_HEADS = D_MODEL // 256
RET_QK_DIM = D_MODEL
RET_V_DIM = 2 * D_MODEL
RET_HEAD_QK = RET_QK_DIM // RET_HEADS
RET_HEAD_V = RET_V_DIM // RET_HEADS
RET_CHUNK = 128
ROPE_BASE = 10000.0
GN_EPS = 1e-5
CONV_DIM = D_MODEL
CONV_WIDTH = 31
LN_EPS = 1e-5
RMS_EPS = 1e-6
IN_SPLITS = (RET_QK_DIM, RET_QK_DIM, RET_V_DIM, RET_V_DIM, CONV_DIM, CONV_DIM, CONV_DIM, D_MODEL, D_MODEL)
IN_WIDTH = sum(IN_SPLITS)


def rmsnorm(x, g):
    xf = x.astype(jnp.float32)
    y = xf * lax.rsqrt(jnp.mean(xf * xf, axis=-1, keepdims=True) + RMS_EPS)
    return (y * g.astype(jnp.float32)).astype(x.dtype)

def layernorm(x, g, b):
    xf = x.astype(jnp.float32)
    mu = jnp.mean(xf, axis=-1, keepdims=True)
    var = jnp.mean(jnp.square(xf - mu), axis=-1, keepdims=True)
    y = (xf - mu) * lax.rsqrt(var + LN_EPS)
    return (y * g.astype(jnp.float32) + b.astype(jnp.float32)).astype(x.dtype)

def head_groupnorm(o):
    of = o.astype(jnp.float32)
    mu = jnp.mean(of, axis=-1, keepdims=True)
    var = jnp.mean(jnp.square(of - mu), axis=-1, keepdims=True)
    return (of - mu) * lax.rsqrt(var + GN_EPS)

def rotary(t, positions):
    dh = t.shape[-1]
    half = dh // 2
    inv_freq = ROPE_BASE ** (-jnp.arange(half, dtype=jnp.float32) / half)
    ang = positions.astype(jnp.float32)[..., None] * inv_freq
    cos = jnp.cos(ang)[:, :, None, :]
    sin = jnp.sin(ang)[:, :, None, :]
    t1, t2 = t[..., :half], t[..., half:]
    return jnp.concatenate([t1 * cos - t2 * sin, t1 * sin + t2 * cos], axis=-1)

def retention_chunkwise(q, k, v):
    B, S, H, dk = q.shape
    dv = v.shape[-1]
    C = RET_CHUNK
    N = S // C
    log_g = jnp.log1p(-jnp.exp2(-5.0 - jnp.arange(H, dtype=jnp.float32)))
    idx = jnp.arange(C, dtype=jnp.float32)
    diff = idx[:, None] - idx[None, :]
    causal = diff >= 0
    decay_mask = jnp.where(causal, jnp.exp(log_g[:, None, None] * jnp.where(causal, diff, 0.0)), 0.0)
    xi = jnp.exp(log_g[:, None] * (idx + 1.0))
    zeta = jnp.exp(log_g[:, None] * (C - 1.0 - idx))
    g_chunk = jnp.exp(log_g * C)

    def to_chunks(t):
        return t.reshape(B, N, C, H, t.shape[-1]).transpose(1, 0, 3, 2, 4)

    def step(state, inp):
        qc, kc, vc = inp
        scores = jnp.einsum('bhid,bhjd->bhij', qc, kc) * decay_mask[None]
        inner = jnp.einsum('bhij,bhje->bhie', scores, vc)
        cross = jnp.einsum('bhid,bhde->bhie', qc, state) * xi[None, :, :, None]
        new_state = state * g_chunk[None, :, None, None] + jnp.einsum(
            'bhjd,bhje->bhde', kc * zeta[None, :, :, None], vc)
        return new_state, inner + cross

    state0 = jnp.zeros((B, H, dk, dv), jnp.float32)
    _, o = lax.scan(step, state0, (to_chunks(q), to_chunks(k), to_chunks(v)))
    return o.transpose(1, 0, 3, 2, 4).reshape(B, S, H, dv)

def causal_depthwise_conv(u, w, b):
    out = lax.conv_general_dilated(
        u, w[:, None, :].astype(u.dtype), window_strides=(1,),
        padding=[(CONV_WIDTH - 1, 0)],
        dimension_numbers=('NWC', 'WIO', 'NWC'),
        feature_group_count=u.shape[-1])
    return out + b.astype(u.dtype)

def first_inputs(seed: int = 0) -> dict:
    key = jax.random.key(seed)
    ks = jax.random.split(key, 16)
    f32 = jnp.float32
    x = jax.random.normal(ks[0], (BATCH, SEQ, D_MODEL), f32)
    c = jax.random.normal(ks[1], (BATCH, D_MODEL), f32)
    offsets = jax.random.randint(ks[2], (BATCH, 1), 0, 4096, dtype=jnp.int32)
    positions = offsets + jnp.arange(SEQ, dtype=jnp.int32)[None, :]
    w_ada = jax.random.normal(ks[3], (DEPTH, D_MODEL, 3 * D_MODEL), f32) * (0.1 * D_MODEL ** -0.5)
    b_ada = jax.random.normal(ks[4], (DEPTH, 3 * D_MODEL), f32) * 0.02
    pre_norm_g = 1.0 + 0.05 * jax.random.normal(ks[5], (DEPTH, D_MODEL), f32)
    w_in = jax.random.normal(ks[6], (DEPTH, D_MODEL, IN_WIDTH), f32) * D_MODEL ** -0.5
    conv_w = jax.random.normal(ks[7], (DEPTH, CONV_WIDTH, CONV_DIM), f32) * CONV_WIDTH ** -0.5
    conv_b = jax.random.normal(ks[8], (DEPTH, CONV_DIM), f32) * 0.02
    conv_ln_g = 1.0 + 0.05 * jax.random.normal(ks[9], (DEPTH, CONV_DIM), f32)
    conv_ln_b = jax.random.normal(ks[10], (DEPTH, CONV_DIM), f32) * 0.02
    w_ret_out = jax.random.normal(ks[11], (DEPTH, RET_V_DIM, D_MODEL), f32) * RET_V_DIM ** -0.5
    w_conv_out = jax.random.normal(ks[12], (DEPTH, CONV_DIM, D_MODEL), f32) * CONV_DIM ** -0.5
    w_out = jax.random.normal(ks[13], (DEPTH, D_MODEL, D_MODEL), f32) * D_MODEL ** -0.5
    post_norm_g = 1.0 + 0.05 * jax.random.normal(ks[14], (DEPTH, D_MODEL), f32)
    return {"x": x, "c": c, "positions": positions, "w_ada": w_ada, "b_ada": b_ada,
            "pre_norm_g": pre_norm_g, "w_in": w_in, "conv_w": conv_w, "conv_b": conv_b,
            "conv_ln_g": conv_ln_g, "conv_ln_b": conv_ln_b, "w_ret_out": w_ret_out,
            "w_conv_out": w_conv_out, "w_out": w_out, "post_norm_g": post_norm_g}

def first_block(x, c, positions, w_ada, b_ada, pre_norm_g, w_in, conv_w, conv_b,
              conv_ln_g, conv_ln_b, w_ret_out, w_conv_out, w_out, post_norm_g):
    B, S, _ = x.shape
    split_at = [int(v) for v in np.cumsum(IN_SPLITS)[:-1]]
    for l in range(DEPTH):
        mod = c @ w_ada[l] + b_ada[l]
        shift, scale, gate = jnp.split(mod, 3, axis=-1)
        h = rmsnorm(x, pre_norm_g[l]) * (1.0 + scale[:, None, :]) + shift[:, None, :]

        proj = h @ w_in[l]
        q, k, v, z_ret, u_val, u_gate, z_conv, g_a, g_b = jnp.split(proj, split_at, axis=-1)

        qh = rotary(q.reshape(B, S, RET_HEADS, RET_HEAD_QK).astype(jnp.float32), positions)
        kh = rotary(k.reshape(B, S, RET_HEADS, RET_HEAD_QK).astype(jnp.float32), positions) * RET_HEAD_QK ** -0.5
        vh = v.reshape(B, S, RET_HEADS, RET_HEAD_V).astype(jnp.float32)
        ret = head_groupnorm(retention_chunkwise(qh, kh, vh)).reshape(B, S, RET_V_DIM).astype(x.dtype)
        y_a = (ret * jax.nn.silu(z_ret)) @ w_ret_out[l]

        a = u_val * jax.nn.sigmoid(u_gate)
        a = causal_depthwise_conv(a, conv_w[l], conv_b[l])
        a = jax.nn.silu(layernorm(a, conv_ln_g[l], conv_ln_b[l]))
        y_b = (a * jax.nn.silu(z_conv)) @ w_conv_out[l]

        merged = jax.nn.sigmoid(g_a) * y_a + jax.nn.sigmoid(g_b) * y_b
        y = merged @ w_out[l]

        x = x + gate[:, None, :] * rmsnorm(y, post_norm_g[l])
    return x


MEM_LEN = 256
EPS = 1e-6
HEAD_DIM = 64
ATTN_WIDTH = D_MODEL // 2
ATTN_Q_HEADS = ATTN_WIDTH // HEAD_DIM
ATTN_KV_HEADS = 2
ATTN_REP = ATTN_Q_HEADS // ATTN_KV_HEADS
KV_WIDTH = ATTN_KV_HEADS * HEAD_DIM
WINDOW = 128
ATTN_BLOCK = 128
SGU_WIDTH = D_MODEL - ATTN_WIDTH
SGU_GROUP_DIM = 64
SGU_GROUPS = SGU_WIDTH // SGU_GROUP_DIM
SGU_CHUNK = 128
IN_WIDTH_2 = ATTN_WIDTH + 2 * KV_WIDTH + 2 * SGU_WIDTH
X_HEADS = 4
X_HEAD_DIM = D_MODEL // X_HEADS
N_GROUPS = 4
EXPERTS_PER_GROUP = 8
N_EXPERTS = N_GROUPS * EXPERTS_PER_GROUP
TOP_K = 2
D_EXPERT = D_MODEL // 2
MOE_BLOCK = 256


def rms_norm(x, gain):
    xf = x.astype(jnp.float32)
    y = xf * lax.rsqrt(jnp.mean(xf * xf, axis=-1, keepdims=True) + EPS)
    return (y * gain.astype(jnp.float32)).astype(x.dtype)

def sliding_window_attention(q, k, v, sinks):
    B, S = q.shape[:2]
    nb = S // ATTN_BLOCK
    qb = q.reshape(B, nb, ATTN_BLOCK, ATTN_KV_HEADS, ATTN_REP, HEAD_DIM).astype(jnp.float32)
    kb = k.reshape(B, nb, ATTN_BLOCK, ATTN_KV_HEADS, HEAD_DIM)
    vb = v.reshape(B, nb, ATTN_BLOCK, ATTN_KV_HEADS, HEAD_DIM)
    pad = ((0, 0), (1, 0), (0, 0), (0, 0), (0, 0))
    kwin = jnp.concatenate([jnp.pad(kb, pad)[:, :-1], kb], axis=2).astype(jnp.float32)
    vwin = jnp.concatenate([jnp.pad(vb, pad)[:, :-1], vb], axis=2).astype(jnp.float32)
    scores = jnp.einsum('bnqhrd,bnkhd->bnhrqk', qb, kwin) * (HEAD_DIM ** -0.5)
    qi = jnp.arange(ATTN_BLOCK)[:, None]
    kj = jnp.arange(2 * ATTN_BLOCK)[None, :]
    dist = qi + ATTN_BLOCK - kj
    band = (dist >= 0) & (dist < WINDOW)
    key_pos = jnp.arange(nb)[:, None, None] * ATTN_BLOCK + kj[None] - ATTN_BLOCK
    mask = band[None] & (key_pos >= 0)
    scores = jnp.where(mask[None, :, None, None], scores, jnp.finfo(jnp.float32).min)
    sink = sinks.astype(jnp.float32).reshape(ATTN_KV_HEADS, ATTN_REP)[None, None, :, :, None, None]
    m = jnp.maximum(jnp.max(scores, axis=-1, keepdims=True), sink)
    p = jnp.exp(scores - m)
    denom = jnp.sum(p, axis=-1, keepdims=True) + jnp.exp(sink - m)
    out = jnp.einsum('bnhrqk,bnkhd->bnqhrd', p / denom, vwin)
    return out.reshape(B, S, ATTN_WIDTH).astype(q.dtype)

def spatial_gating(u, v, sgu_norm, sgu_w, sgu_b):
    B, S = u.shape[:2]
    nc = S // SGU_CHUNK
    vc = rms_norm(v, sgu_norm).reshape(B, nc, SGU_CHUNK, SGU_GROUPS, SGU_GROUP_DIM)
    causal = jnp.tril(jnp.ones((SGU_CHUNK, SGU_CHUNK), dtype=bool))
    w = jnp.where(causal[None], sgu_w, jnp.zeros((), sgu_w.dtype))
    s = jnp.einsum('gij,bcjgd->bcigd', w, vc) + sgu_b.T[None, None, :, :, None]
    return u * s.reshape(B, S, SGU_WIDTH)

def memory_cross_attention(h, mem_n, w_cq, w_ck, w_cv, cq_norm, ck_norm, w_co):
    B, S = h.shape[:2]
    M = mem_n.shape[1]
    q = rms_norm((h @ w_cq).reshape(B, S, X_HEADS, X_HEAD_DIM), cq_norm)
    k = rms_norm((mem_n @ w_ck).reshape(B, M, X_HEADS, X_HEAD_DIM), ck_norm)
    v = (mem_n @ w_cv).reshape(B, M, X_HEADS, X_HEAD_DIM)
    scores = jnp.einsum('bshd,bmhd->bhsm', q.astype(jnp.float32), k.astype(jnp.float32)) * (X_HEAD_DIM ** -0.5)
    p = jax.nn.softmax(scores, axis=-1)
    out = jnp.einsum('bhsm,bmhd->bshd', p, v.astype(jnp.float32)).astype(h.dtype)
    return out.reshape(B, S, D_MODEL) @ w_co

def hierarchical_moe(h, w_router_group, w_router_expert, w1, w3, w2):
    B, S, D = h.shape
    T = B * S
    xt = h.reshape(T, D)
    xf = xt.astype(jnp.float32)
    p_group = jax.nn.softmax(xf @ w_router_group.astype(jnp.float32), axis=-1)
    g_idx = jnp.argmax(p_group, axis=-1)
    g_w = jnp.take_along_axis(p_group, g_idx[:, None], axis=1)[:, 0]
    local = jnp.einsum('td,gde->tge', xf, w_router_expert.astype(jnp.float32))
    local = jnp.take_along_axis(local, g_idx[:, None, None], axis=1)[:, 0]
    top_logit, top_idx = lax.top_k(local, TOP_K)
    gate = jax.nn.softmax(top_logit, axis=-1) * g_w[:, None]
    flat_e = (g_idx[:, None] * EXPERTS_PER_GROUP + top_idx).reshape(-1).astype(jnp.int32)
    flat_w = gate.reshape(-1)
    A = T * TOP_K
    order = jnp.argsort(flat_e)
    sorted_e = flat_e[order]
    counts = jnp.zeros((N_EXPERTS,), jnp.int32).at[flat_e].add(1)
    starts = jnp.cumsum(counts) - counts
    padded = (counts + MOE_BLOCK - 1) // MOE_BLOCK * MOE_BLOCK
    pad_end = jnp.cumsum(padded)
    pad_start = pad_end - padded
    dest = pad_start[sorted_e] + jnp.arange(A, dtype=jnp.int32) - starts[sorted_e]
    nb = -(-A // MOE_BLOCK) + N_EXPERTS
    P = nb * MOE_BLOCK
    slot_tok = jnp.full((P,), T, jnp.int32).at[dest].set((order // TOP_K).astype(jnp.int32))
    slot_w = jnp.zeros((P,), jnp.float32).at[dest].set(flat_w[order])
    block_e = jnp.minimum(jnp.searchsorted(pad_end, jnp.arange(nb, dtype=jnp.int32) * MOE_BLOCK, side='right'), N_EXPERTS - 1)
    x_pad = jnp.concatenate([xt, jnp.zeros((1, D), xt.dtype)], axis=0)
    xb = x_pad[slot_tok].reshape(nb, MOE_BLOCK, D)

    def run_block(args):
        xblk, e = args
        hid = jax.nn.silu(xblk @ w1[e]) * (xblk @ w3[e])
        return hid @ w2[e]

    yb = lax.map(run_block, (xb, block_e)).reshape(P, D)
    y = jnp.zeros((T + 1, D), jnp.float32).at[slot_tok].add(yb.astype(jnp.float32) * slot_w[:, None])[:T]
    return y.astype(h.dtype).reshape(B, S, D)

def second_inputs(seed: int = 0) -> dict:
    key = jax.random.key(seed)
    ks = jax.random.split(key, 32)
    f32 = jnp.float32
    nrm = lambda k, shape, s: jax.random.normal(k, shape, f32) * s
    gain = lambda k, n: 1.0 + 0.02 * jax.random.normal(k, (n,), f32)
    return {
        "x": nrm(ks[0], (BATCH, SEQ, D_MODEL), 1.0),
        "mem": nrm(ks[1], (BATCH, MEM_LEN, D_MODEL), 1.0),
        "norm_mix": gain(ks[2], D_MODEL),
        "w_in": nrm(ks[3], (D_MODEL, IN_WIDTH_2), D_MODEL ** -0.5),
        "q_norm": gain(ks[4], HEAD_DIM),
        "k_norm": gain(ks[5], HEAD_DIM),
        "attn_sinks": nrm(ks[6], (ATTN_Q_HEADS,), 0.5),
        "sgu_norm": gain(ks[7], SGU_WIDTH),
        "sgu_w": nrm(ks[8], (SGU_GROUPS, SGU_CHUNK, SGU_CHUNK), SGU_CHUNK ** -0.5),
        "sgu_b": 1.0 + nrm(ks[9], (SGU_GROUPS, SGU_CHUNK), 0.1),
        "out_norm_attn": gain(ks[10], ATTN_WIDTH),
        "out_norm_sgu": gain(ks[11], SGU_WIDTH),
        "w_out": nrm(ks[12], (D_MODEL, D_MODEL), D_MODEL ** -0.5),
        "norm_cross": gain(ks[13], D_MODEL),
        "norm_mem": gain(ks[14], D_MODEL),
        "w_cq": nrm(ks[15], (D_MODEL, D_MODEL), D_MODEL ** -0.5),
        "w_ck": nrm(ks[16], (D_MODEL, D_MODEL), D_MODEL ** -0.5),
        "w_cv": nrm(ks[17], (D_MODEL, D_MODEL), D_MODEL ** -0.5),
        "cq_norm": gain(ks[18], X_HEAD_DIM),
        "ck_norm": gain(ks[19], X_HEAD_DIM),
        "w_co": nrm(ks[20], (D_MODEL, D_MODEL), D_MODEL ** -0.5),
        "norm_ffn": gain(ks[21], D_MODEL),
        "w_router_group": nrm(ks[22], (D_MODEL, N_GROUPS), D_MODEL ** -0.5),
        "w_router_expert": nrm(ks[23], (N_GROUPS, D_MODEL, EXPERTS_PER_GROUP), D_MODEL ** -0.5),
        "w1": nrm(ks[24], (N_EXPERTS, D_MODEL, D_EXPERT), D_MODEL ** -0.5),
        "w3": nrm(ks[25], (N_EXPERTS, D_MODEL, D_EXPERT), D_MODEL ** -0.5),
        "w2": nrm(ks[26], (N_EXPERTS, D_EXPERT, D_MODEL), D_EXPERT ** -0.5),
    }

def second_block(x, mem, norm_mix, w_in, q_norm, k_norm, attn_sinks, sgu_norm, sgu_w, sgu_b,
              out_norm_attn, out_norm_sgu, w_out, norm_cross, norm_mem, w_cq, w_ck, w_cv,
              cq_norm, ck_norm, w_co, norm_ffn, w_router_group, w_router_expert, w1, w3, w2):
    B, S = x.shape[:2]
    mem_n = rms_norm(mem, norm_mem)
    for _ in range(DEPTH):
        h = rms_norm(x, norm_mix)
        proj = h @ w_in
        c0 = ATTN_WIDTH
        c1 = c0 + KV_WIDTH
        c2 = c1 + KV_WIDTH
        c3 = c2 + SGU_WIDTH
        q = rms_norm(proj[..., :c0].reshape(B, S, ATTN_Q_HEADS, HEAD_DIM), q_norm)
        k = rms_norm(proj[..., c0:c1].reshape(B, S, ATTN_KV_HEADS, HEAD_DIM), k_norm)
        v = proj[..., c1:c2].reshape(B, S, ATTN_KV_HEADS, HEAD_DIM)
        u = jax.nn.gelu(proj[..., c2:c3])
        g = jax.nn.gelu(proj[..., c3:])
        attn = sliding_window_attention(q, k, v, attn_sinks)
        sg = spatial_gating(u, g, sgu_norm, sgu_w, sgu_b)
        mixed = jnp.concatenate([rms_norm(attn, out_norm_attn), rms_norm(sg, out_norm_sgu)], axis=-1)
        x = x + mixed @ w_out
        x = x + memory_cross_attention(rms_norm(x, norm_cross), mem_n, w_cq, w_ck, w_cv, cq_norm, ck_norm, w_co)
        x = x + hierarchical_moe(rms_norm(x, norm_ffn), w_router_group, w_router_expert, w1, w3, w2)
    return x


def setup_inputs(seed=0):
    out = dict(first_inputs(seed))
    for name, value in second_inputs(seed + 1).items():
        if name != "x":
            out[name + "_2"] = value
    return out


def reference(
    x, c, positions, w_ada, b_ada, pre_norm_g, w_in, conv_w, conv_b, conv_ln_g, conv_ln_b,
    w_ret_out, w_conv_out, w_out, post_norm_g, mem_2, norm_mix_2, w_in_2, q_norm_2, k_norm_2,
    attn_sinks_2, sgu_norm_2, sgu_w_2, sgu_b_2, out_norm_attn_2, out_norm_sgu_2, w_out_2,
    norm_cross_2, norm_mem_2, w_cq_2, w_ck_2, w_cv_2, cq_norm_2, ck_norm_2, w_co_2, norm_ffn_2,
    w_router_group_2, w_router_expert_2, w1_2, w3_2, w2_2,
):
    x = first_block(
        x, c, positions, w_ada, b_ada, pre_norm_g, w_in, conv_w, conv_b, conv_ln_g, conv_ln_b,
        w_ret_out, w_conv_out, w_out, post_norm_g,
    )
    return second_block(
        x, mem_2, norm_mix_2, w_in_2, q_norm_2, k_norm_2, attn_sinks_2, sgu_norm_2, sgu_w_2,
        sgu_b_2, out_norm_attn_2, out_norm_sgu_2, w_out_2, norm_cross_2, norm_mem_2, w_cq_2,
        w_ck_2, w_cv_2, cq_norm_2, ck_norm_2, w_co_2, norm_ffn_2, w_router_group_2,
        w_router_expert_2, w1_2, w3_2, w2_2,
    )


_drawn_inputs = setup_inputs


def setup_inputs(seed=0):
    import zlib

    import numpy as np

    out = dict(_drawn_inputs(seed))
    spreads = {}
    factors = {'conv_b': 4.25,
     'conv_ln_g': 4.19,
     'conv_ln_b': 8.0,
     'post_norm_g': 3.744,
     'q_norm_2': 2.953,
     'attn_sinks_2': 4.419,
     'sgu_norm_2': 4.14,
     'out_norm_sgu_2': 2.86,
     'norm_cross_2': 6.414,
     'norm_mem_2': 5.247,
     'cq_norm_2': 5.503,
     'ck_norm_2': 5.935,
     'norm_ffn_2': 8.0}
    for name, (base, spread) in spreads.items():
        noise = np.random.default_rng([zlib.crc32(name.encode()), seed]).standard_normal(out[name].shape)
        drawn = base * np.exp(spread * noise) if base else spread * noise
        out[name] = __import__('jax').numpy.asarray(drawn.astype(out[name].dtype))
    for name, factor in factors.items():
        out[name] = (out[name] * factor).astype(out[name].dtype)
    return out
```

```python
from contextlib import ExitStack

import concourse.bass as bass
import numpy as np
from concourse import mybir

P = 128
S = 512
D = 1024
MT = S // P
KT = D // P
HEADS, HQK, HV = 4, 256, 512
TAPS = 31
WIN_COLS = (1024, 1024, 2048, 2048, 1024, 1024, 1024, 1024, 1024)
OFF_Q, OFF_K, OFF_V, OFF_Z, OFF_UV, OFF_UG, OFF_ZC, OFF_GA, OFF_GB = [
    sum(WIN_COLS[:n]) for n in range(len(WIN_COLS))]
MEM, MM = 256, 2
AH, AD = 8, 64
XH, XD = 4, 256
GROUPS, PER_GROUP = 4, 8
EXPERTS, FF = GROUPS * PER_GROUP, 512
SLOTS = 64
MAX_BLOCKS = (2 * S - EXPERTS) // SLOTS + EXPERTS + 1
RMS_EPS, GN_EPS, LN_EPS = 1e-6, 1e-5, 1e-5
NEG = -1e30
ARENA = 24300

F32 = mybir.dt.float32
F32R = mybir.dt.float32r
BF16 = mybir.dt.bfloat16
I32 = mybir.dt.int32
U32 = mybir.dt.uint32
ACT = mybir.ActivationFunctionType
ALU = mybir.AluOpType
AX = mybir.AxisListType

CONSTS = {}


def const_table():
    p = np.arange(P)
    inv_freq = (np.float32(10000.0) ** (-np.arange(HQK // 2, dtype=np.float32) / np.float32(HQK // 2)))
    dist = p[:, None] + P - np.arange(2 * P)[None, :]
    band = np.where((dist >= 0) & (dist < P), 0.0, NEG)
    first = np.where(np.arange(2 * P)[None, :] >= P, band, NEG)
    parts = [
        ("ident", np.eye(P)),
        ("before", (p[:, None] < p[None, :])),
        ("causalT", (p[:, None] <= p[None, :])),
        ("ones", np.ones((P, P))),
        ("mean", np.full((P, P), 1.0 / D)),
        ("iota", np.broadcast_to(np.arange(64), (P, 64))),
        ("token", p[:, None] + P * np.arange(MT)[None, :]),
        ("band", band),
        ("first", first),
        ("freq", inv_freq[:, None]),
    ]
    at = 0
    for name, a in parts:
        CONSTS[name] = (at, at + a.shape[1])
        at += a.shape[1]
    return np.concatenate([np.asarray(a, np.float32) for _, a in parts], axis=1)


def decay_table():
    log_g = np.log1p(-np.exp2(-5.0 - np.arange(HEADS)))
    diff = np.arange(S)[None, :] - np.arange(P)[:, None]
    d = np.where(diff >= 0, np.exp(log_g[:, None, None] * np.maximum(diff, 0)), 0.0)
    return (d * HQK ** -0.5).astype(np.float32)


const_table()


class Stage:

    def __init__(self, base, uses):
        self.base = list(base)
        self.places = [k % len(base) for k in range(uses)] if isinstance(uses, int) else list(uses)
        self.per = [self.places.count(b) for b in range(len(base))]

    def place(self, k):
        return self.places[k]

    def before(self, k, i=0):
        b = self.places[k]
        return i * self.per[b] + (self.base[b] + self.places[:k].count(b))


def stages(n, plan):
    base, out = [0] * n, {}
    for name, uses, steps in plan:
        out[name] = st = Stage(base, uses)
        base = [b + steps * p for b, p in zip(base, st.per)]
    return out


class Chain:

    def __init__(self, eng, sem):
        self.eng, self.sem, self.base, self.count = eng, sem, 0, 0

    def __call__(self, instruction):
        instruction.then_inc(self.sem, 1)
        self.count += 1

    def wait(self, but=0):
        self.eng.wait_ge(self.sem, self.base + (self.count - but))

    def enter(self, i, per):
        self.at, self.per = self.base + self.count, per
        self.base, self.count = i * per + self.at, 0

    def leave(self, steps):
        assert self.count == self.per, (self.count, self.per)
        self.base, self.count = (self.at + self.per * steps, 0) if steps else (None, 0)


BANK_PLAN = [
    ("columns", 1, 1), ("ada", 6, 1), ("hT", KT, 1), ("conv", 3, KT), ("ln", 2, 1),
    ("heads", 24, HEADS), ("mix", 4, KT), ("out", 8, 1),
    ("h2T", KT, 1), ("in2", 16, 1), ("qkT", 5, 1), ("attn", MT * 9, 1), ("sguw", 2, 1), ("sgu", 4, 1),
    ("mixT", KT, 1), ("out2", 8, 1),
    ("memT", 4, 1), ("xk", 4, 1), ("xv", 4, 1), ("xkT", 4, 1), ("hqT", KT, 1), ("xq", 8, 1), ("xqT", KT, 1),
    ("xs", 8, 1), ("xpT", 8, 1), ("xo", 8, 1), ("xout", 8, 1),
    ("h3T", KT, 1), ("route", 4, 1), ("moe0", (0, 3, 4, 5), 1), ("moe", 6, 1),
]
CHUNK_PLAN = [
    ("ada", 6, 1), ("conv", 3, KT), ("heads", 3, HEADS), ("mix", 3, KT), ("out", 2, 1), ("in2", 4, 1),
    ("out2", 2, 1), ("xk", 2, 1), ("xv", 2, 1), ("xq", 2, 1), ("xout", 2, 1), ("moe", 3, 1),
]
BLOCK2_COLS = 5


def build(nc, a, out):
    banks, chunks = stages(8, BANK_PLAN), stages(3, CHUNK_PLAN)
    ctx = ExitStack()
    with ctx:
        def sb(name, shape, dt=F32):
            return ctx.enter_context(nc.sbuf_tensor(name, shape, dt))

        def sem(name):
            return ctx.enter_context(nc.semaphore(name))

        ring = sb("ring", [P, 3, 4096])
        const = sb("const", [P, CONSTS["freq"][1]])
        cols = sb("cols", [P, KT, TAPS + 3 + 4])
        sgub = sb("sgub", [P, 8])
        actT = sb("actT", [P, KT, S])
        small = sb("small", [P, 512])
        arena = sb("arena", [P, ARENA])

        def cst(name, parts=P):
            lo, hi = CONSTS[name]
            return const[0:parts, lo:hi]

        ident = cst("ident")
        taken = [0]

        def carve(shape, at=None):
            n = int(np.prod(shape))
            lo = taken[0] if at is None else at
            assert lo + n <= ARENA, (lo, n)
            if at is None:
                taken[0] = lo + n
            v = arena[:, lo:lo + n]
            if len(shape) == 2:
                v = v.rearrange("p (a b) -> p a b", a=shape[0])
            if len(shape) == 3:
                v = v.rearrange("p (a b c) -> p a b c", a=shape[0], b=shape[1])
            return v

        def mini(lo, n):
            return small[:, lo:lo + n]

        gate_post = carve([D])
        cosT, sinT = carve([S]), carve([S])
        convT = carve([KT, S])
        zconvT = carve([KT, S])
        first_free = taken[0]
        taken[0] = D + 2 * S
        colrows = carve([D])[0:TAPS + 3 + 4, :]
        sgub_rows = carve([P])[0:8, :]
        pos_i = carve([S]).bitcast(I32)
        x0 = carve([MT, D])
        h0 = carve([MT, D])
        mod_scale, mod_shift = carve([D]), carve([D])
        pre_g, post_g = carve([D]), carve([D])
        c_rep = carve([KT, P])
        bada = carve([3 * D])
        angle, turns = carve([S]), carve([S])
        taken[0] = first_free
        apad = carve([TAPS - 1 + S])
        conv_acc = carve([2, S])
        sig_u, sig_z = carve([S]), carve([S])
        ln_sq = carve([2, S])
        ln_rstd, ln_std = carve([S]), carve([S])
        ln_y = carve([2, S])
        ln_s = carve([2, S])
        taken[0] = first_free - KT * S
        retT = carve([16, S])
        qk_rot = carve([4, S])
        v_tok = carve([MT, HV])
        z_tok = carve([MT, HV])
        decayed = carve([MT, S])
        rot = decayed
        sig_r = carve([2, S])
        norm_o = sig_r
        decay = carve([S])
        taken[0] = first_free + KT * S
        mergedT = carve([KT, S])
        part_a, part_b = carve([S]), carve([S])
        sig_a, sig_b = carve([S], at=D), carve([S], at=D + S)
        assert taken[0] <= ARENA - MT * D
        x = carve([MT, D], at=ARENA - MT * D)
        y_tok = carve([MT, D], at=first_free)
        squares = carve([D], at=first_free + MT * D)

        taken[0] = 0
        n_tok = carve([MT, D])
        sq_junk = carve([MT, 512])
        q_tok = carve([MT, 512])
        kv_tok = carve([MT, 256])
        u_tok = carve([MT, 512])
        g_tok = carve([MT, 512])
        attn_tok = carve([MT, 512])
        q_pair = attn_tok
        second_free = taken[0]
        qT = carve([4, S])
        kT = carve([P + S])
        s_tok = carve([AH, 2 * P], at=MT * D)
        p_tok = carve([AH, 2 * P], at=0)
        pT = carve([2 * AH, P], at=MT * D + MT * 512)
        sgu_w = carve([8, P], at=second_free)
        sgu_wT = carve([8, P], at=second_free + 8 * P)
        gain_rows = carve([AD + AD + 512 + 8], at=ARENA - MT * D - 648)
        qn_row, kn_row = gain_rows[:, 0:AD], gain_rows[:, AD:2 * AD]
        sgun_row, sink_row = gain_rows[:, 2 * AD:2 * AD + 512], gain_rows[:, 2 * AD + 512:]
        assert second_free + 4 * S + P + S <= ARENA - MT * D - 648
        taken[0] = MT * D
        mem = carve([MM, D])
        memT = carve([KT, MEM])
        xk_tok = carve([MM, D])
        xv_tok = carve([MM, D])
        xkT = carve([KT, MEM])
        xq_tok = carve([MT, D])
        cqn_row, ckn_row = carve([XD]), carve([XD])
        x_sq = carve([D])
        xqT = carve([KT, S], at=0)
        xp_tok = carve([MT, XH, MEM], at=MT * D)
        xpT = carve([KT, S], at=MT * D + 8 * D)
        xoT = carve([KT, S], at=0)
        h3_tok = carve([MT, D], at=0)
        taken[0] = MT * D
        ffn_row = carve([D])
        wr = carve([KT, GROUPS + EXPERTS])
        lg = carve([MT, 40])
        oh = carve([2 * MT, EXPERTS])
        ohs = carve([MT, EXPERTS])
        loc = carve([MT, 8])
        top = carve([MT, 8])
        ranks = carve([MT, EXPERTS])
        place_e = carve([MT, EXPERTS])
        e_tmp = carve([2 * MT, EXPERTS])
        slot_oh = carve([2 * MT, SLOTS])
        block_oh = carve([2 * MT, 64])
        expert_free = taken[0]
        xg = carve([D])
        sg_h, t_h, hid = carve([FF]), carve([FF]), carve([FF])
        y_blk = carve([D])
        combo = carve([4, D])
        assert taken[0] <= ARENA - MT * D
        top_i = sb("top_i", [P, MT, 8], U32)
        dest_i = sb("dest_i", [P, 4, 2 * MT], I32)
        parts = sb("parts", [P, 4, 2, 1024], F32R)
        xgT = sb("xgT", [P, 2, KT, SLOTS], F32R)
        hidT = sb("hidT", [P, 2, 4, SLOTS], F32R)
        mark_src = sb("mark_src", [P, P], BF16)
        slot_tok = sb("slot_tok", [SLOTS, 64], U32)
        idx = sb("idx", [SLOTS, 1], U32)
        plan_row = sb("plan_row", [1, 1 + P], I32)
        n_steps = sb("n_steps", [1, 1], I32)
        h3_rows = nc.dram_tensor("h3_rows", [S, D], F32).ap()
        y_rows = nc.dram_tensor("y_rows", [(MAX_BLOCKS + 2) * SLOTS, D], F32).ap()

        ps = ctx.enter_context(nc.psum_tensor("ps", [P, 8, 512], F32))

        bank_filled = [sem(f"bank{b}_filled") for b in range(8)]
        bank_drained = [sem(f"bank{b}_drained") for b in range(8)]
        weights_landed = [sem(f"weights{s}_landed") for s in range(3)]
        weights_used = [sem(f"weights{s}_used") for s in range(3)]
        const_in, cols_in, x_in, c_in, pos_in, rows_in = (sem(n) for n in (
            "const_in", "cols_in", "x_in", "c_in", "pos_in", "rows_in"))
        c_rep_ready, cols_ready, h0_ready, hT_ready = (sem(n) for n in (
            "c_rep_ready", "cols_ready", "h0_ready", "hT_ready"))
        act_own, dve_own, dve_moe = (sem(n) for n in ("act_own", "dve_own", "dve_moe"))
        sig_u_ready, sig_z_ready = sem("sig_u_ready"), sem("sig_z_ready")
        angles_ready, rotary_ready = sem("angles_ready"), sem("rotary_ready")
        conv_ready, sq_ready, sq_used, cen_ready = (sem(n) for n in (
            "conv_ready", "ln_sq_ready", "ln_sq_used", "centred"))
        ln_std_ready, ln_y_ready, ln_s_ready, gated_conv_ready = (sem(n) for n in (
            "ln_std_ready", "ln_y_ready", "ln_s_ready", "gated_conv_ready"))
        decay_in, decay_used = sem("decay_in"), sem("decay_used")
        qk_ready, v_ready, sig_r_ready, sig_r_used = (sem(n) for n in (
            "qk_ready", "v_ready", "sig_r_ready", "sig_r_used"))
        decayed_ready, var_ready, std_ready, ret_ready, retT_ready = (sem(n) for n in (
            "decayed_ready", "var_ready", "std_ready", "ret_ready", "retT_ready"))
        sig_ab_ready, merged_ready = sem("sig_ab_ready"), sem("merged_ready")
        y_ready, ms_ready, rms_ready, x_ready = (sem(n) for n in ("y_ready", "ms_ready", "rms_ready", "x_ready"))
        x_back, gains_in = sem("x_back"), sem("gains_in")
        row_ready, in2_ready, qk2_ready, qkT_ready = (sem(n) for n in (
            "rows_ready", "in2_ready", "qk2_ready", "qkT_ready"))
        smax_ready, p_ready, pT_ready, pv_done = (sem(n) for n in ("smax_ready", "p_ready", "pT_ready", "pv_done"))
        sguw_in, sguwT_ready, vc_ready, actT_ready = (sem(n) for n in (
            "sguw_in", "sguwT_ready", "vc_ready", "actT_ready"))
        mem_in, memT_ready, xkv_ready, xk_ready, xkT_ready = (sem(n) for n in (
            "mem_in", "memT_ready", "xkv_ready", "xk_ready", "xkT_ready"))
        xq_in, xq_ready, xqT_ready, xmax_ready, sink_exp, xp_ready, xpT_ready, xoT_ready = (sem(n) for n in (
            "xq_in", "xq_ready", "xqT_ready", "xmax_ready", "sink_exp", "xp_ready", "xpT_ready", "xoT_ready"))
        ffn_in, h3_stored, logits_ready, gexp_in, gexp_ready, texp_in, texp_ready = (sem(n) for n in (
            "ffn_in", "h3_stored", "logits_ready", "gexp_in", "gexp_ready", "texp_in", "texp_ready"))
        oh_ready, plan_col_ready, slot_oh_ready, plan_ready, slots_ready = (sem(n) for n in (
            "oh_ready", "plan_col_ready", "slot_oh_ready", "plan_ready", "slots_ready"))
        idx_ready, xg_in, xgT_hi, sg_h_ready, hid_ready, hidT_hi, y_blk_ready, y_stored = (sem(n) for n in (
            "idx_ready", "xg_in", "xgT_hi_ready", "sg_h_ready", "hid_ready", "hidT_hi_ready", "y_blk_ready", "y_stored"))
        half_landed = [sem(f"expert_half{n}_landed") for n in range(6)]
        piece_hi = sem("piece_hi_ready")
        piece_split = [sem(f"piece{n}_split") for n in range(12)]
        piece_used = [sem(f"parts{n}_used") for n in range(4)]
        combo_in = [sem(f"combo{n}_in") for n in range(4)]
        stats_settled, turn_may_start, idx_settled = (sem(n) for n in ("stats_settled", "turn_may_start", "idx_settled"))
        zero_ready, y_cleared = sem("zero_ready"), sem("y_cleared")
        combo_used, out_done = sem("combo_used"), sem("out_done")

        st_ms, st_rms, st_r = mini(0, 32), mini(32, 32), mini(64, 32)
        bn6, mv, st_std = mini(96, 24), mini(120, 8), mini(128, 4)
        gn_r = mini(132, 4)
        mx, nmx, den, sinkx = mini(136, 32), mini(168, 32), mini(200, 32), mini(232, 8)
        eps = mini(240, 3)
        gidx, gsum, gmax = mini(248, 4), mini(252, 4), mini(256, 4)
        gexp, gm8 = mini(260, 16), mini(276, 8)
        goh = mini(284, 16)
        eid, dl, w01, tden = mini(300, 8), mini(308, 4), mini(312, 8), mini(320, 4)
        cnt, nblk, incl, bstart = mini(324, 32), mini(356, 32), mini(388, 32), mini(420, 32)
        destf, blkf, inf_ = mini(452, 8), mini(460, 8), mini(468, 8)
        plan_col = mini(476, 1)
        c_col = mini(480, 8)
        e_one = mini(488, 4)

        def tiles(w):
            return w.rearrange("(t p) n -> p t n", p=P)

        def row(v, n=None):
            return v.rearrange("(o n) -> o n", o=1)

        x_v = a["x"][0].rearrange("(m p) d -> p m d", p=P)
        out_v = out[0].rearrange("(m p) d -> p m d", p=P)
        w_in = tiles(a["w_in"][0])
        w_ada = a["w_ada"][0].rearrange("(p t) n -> p t n", t=KT)

        block = ctx.enter_context(nc.Block())

        @block.sync
        def _(sp):
            def chunk(stage, j, halves, i=0):
                st = chunks[stage]
                s, n = st.place(j), st.before(j, i)
                if not (isinstance(n, int) and n == 0):
                    sp.wait_ge(weights_used[s], n)
                for dst, src in halves(ring[:, s, :]):
                    sp.dma_start(dst, src).then_inc(weights_landed[s], 16)

            def pair(r, src):
                k, n = src.shape[1], src.shape[2]
                v = r[:, 0:k * n].rearrange("p (k n) -> p k n", k=k)
                return [(v[:, 0:k // 2, :], src[:, 0:k // 2, :]), (v[:, k // 2:k, :], src[:, k // 2:k, :])]

            def both(r, one, two):
                k, n = one.shape[1], one.shape[2]
                v = r[:, 0:2 * k * n].rearrange("p (w k n) -> p w k n", w=2, k=k)
                return [(v[:, 0], one), (v[:, 1], two)]

            sp.dma_start(c_col, a["c"][0].rearrange("(p t) -> p t", t=KT)).then_inc(c_in, 16)
            sp.dma_start(const[:, :], a["const"]).then_inc(const_in, 16)
            sp.dma_start(bada[0:1, :], a["b_ada"]).then_inc(c_in, 16)
            sp.dma_start(x0, x_v).then_inc(x_in, 16)
            sp.dma_start(pre_g, a["pre_norm_g"].partition_broadcast(P)).then_inc(rows_in, 16)
            sp.dma_start(post_g, a["post_norm_g"].partition_broadcast(P)).then_inc(rows_in, 16)
            for j in range(3):
                g = (2, 3, 0, 1, 4, 5)[j]
                chunk("ada", j, lambda r: pair(r, w_ada[:, :, g * 512:(g + 1) * 512]))
            sp.dma_start(pos_i[:, :], a["positions"].partition_broadcast(P)).then_inc(pos_in, 16)
            per_feature = [a["conv_w"][0], a["conv_b"], a["conv_ln_g"], a["conv_ln_b"], row(a["norm_mix_2"]),
                           row(a["norm_cross_2"]), row(a["norm_mem_2"])]
            at = 0
            for v in per_feature:
                sp.dma_start(colrows[at:at + v.shape[0], :], v).then_inc(cols_in, 16)
                at += v.shape[0]
            sp.dma_start(colrows[at:at + 1, 0:512], row(a["out_norm_attn_2"])).then_inc(cols_in, 16)
            sp.dma_start(colrows[at:at + 1, 512:], row(a["out_norm_sgu_2"])).then_inc(cols_in, 16)
            sp.dma_start(sgub_rows[:, :], a["sgu_b_2"]).then_inc(cols_in, 16)
            for j in range(3, 6):
                g = (2, 3, 0, 1, 4, 5)[j]
                chunk("ada", j, lambda r: pair(r, w_ada[:, :, g * 512:(g + 1) * 512]))

            with sp.Fori(0, KT) as t:
                for j, off in enumerate((OFF_UV, OFF_UG, OFF_ZC)):
                    chunk("conv", j, lambda r: pair(r, w_in[:, :, bass.ds(off + t * P, P)]), t)
            with sp.Fori(0, HEADS) as h:
                sp.wait_ge(decay_used, (h + 1) * MT)
                sp.wait_ge(gated_conv_ready, KT)
                sp.dma_start(decay, a["decay"][bass.ds(h, 1), :, :].rearrange("o p n -> p (o n)")).then_inc(decay_in, 16)

                def qk(r):
                    v = r.rearrange("p (k n) -> p k n", k=KT)
                    return [(v[:, :, 0:HQK], w_in[:, :, bass.ds(OFF_Q + h * HQK, HQK)]),
                            (v[:, :, HQK:], w_in[:, :, bass.ds(OFF_K + h * HQK, HQK)])]
                chunk("heads", 0, qk, h)
                chunk("heads", 1, lambda r: pair(r, w_in[:, :, bass.ds(OFF_V + h * HV, HV)]), h)
                chunk("heads", 2, lambda r: pair(r, w_in[:, :, bass.ds(OFF_Z + h * HV, HV)]), h)
            w_ret, w_conv = tiles(a["w_ret_out"][0]), tiles(a["w_conv_out"][0])
            with sp.Fori(0, KT) as t:
                chunk("mix", 0, lambda r: pair(r, w_ret[:, :, bass.ds(t * P, P)]), t)
                chunk("mix", 1, lambda r: pair(r, w_conv[:, :, bass.ds(t * P, P)]), t)
                chunk("mix", 2, lambda r: both(r, w_in[:, :, bass.ds(OFF_GA + t * P, P)],
                                               w_in[:, :, bass.ds(OFF_GB + t * P, P)]), t)

            def project(stage, w, widths=None):
                at = 0
                for j, n in enumerate(widths or [512] * (w.shape[2] // 512)):
                    chunk(stage, j, lambda r: pair(r, w[:, :, at:at + n]))
                    at += n

            project("out", tiles(a["w_out"][0]))
            sp.wait_ge(retT_ready, HEADS * 4)
            sp.dma_start(x, x_v).then_inc(x_back, 16)
            project("in2", tiles(a["w_in_2"]), (512, 256, 512, 512))
            sp.wait_ge(x_ready, 1)
            for dst, v in ((qn_row, "q_norm_2"), (kn_row, "k_norm_2"), (sgun_row, "sgu_norm_2"), (sink_row, "attn_sinks_2")):
                sp.dma_start(dst, row(a[v]).partition_broadcast(P)).then_inc(gains_in, 16)
            project("out2", tiles(a["w_out_2"]))
            sp.wait_ge(pv_done, 1)
            sp.dma_start(sgu_w, a["sgu_w_2"].rearrange("g i j -> i g j")).then_inc(sguw_in, 16)
            sp.wait_ge(actT_ready, 2 * KT)
            sp.dma_start(mem, a["mem_2"][0].rearrange("(m p) d -> p m d", p=P)).then_inc(mem_in, 16)
            for dst, v in ((cqn_row, "cq_norm_2"), (ckn_row, "ck_norm_2")):
                sp.dma_start(dst, row(a[v]).partition_broadcast(P)).then_inc(mem_in, 16)
            for stage, w in (("xk", "w_ck_2"), ("xv", "w_cv_2"), ("xq", "w_cq_2"), ("xout", "w_co_2")):
                project(stage, tiles(a[w]))
            sp.wait_ge(x_ready, 3)
            sp.dma_start(ffn_row, row(a["norm_ffn_2"]).partition_broadcast(P)).then_inc(ffn_in, 16)
            sp.dma_start(wr[:, :, 0:GROUPS], tiles(a["w_router_group_2"])).then_inc(ffn_in, 16)
            for g in range(GROUPS):
                lo = GROUPS + g * PER_GROUP
                sp.dma_start(wr[:, :, lo:lo + PER_GROUP], tiles(a["w_router_expert_2"][g])).then_inc(ffn_in, 16)
            sp.wait_ge(zero_ready, 1)
            sp.dma_start(y_rows.rearrange("(k p) d -> p k d", p=P),
                         combo[:, 0:1, :].to_broadcast([P, (MAX_BLOCKS + 2) * SLOTS // P, D])).then_inc(y_cleared, 16)
            sp.wait_ge(row_ready, 3 * MT)
            sp.dma_start(h3_rows.rearrange("(m p) d -> p m d", p=P), h3_tok).then_inc(h3_stored, 16)

            sp.wait_ge(plan_ready, 2)
            steps = sp.snap(sp.value_load(n_steps[0:1, 0:1], min_val=2, max_val=MAX_BLOCKS + 1))
            w1, w3 = (a[n].rearrange("e (t p) f -> e p t f", p=P) for n in ("w1_2", "w3_2"))
            w2 = a["w2_2"].rearrange("e (t p) f -> e p t f", p=P)
            for j in range(3):
                sp.wait_ge(weights_used[j], chunks["moe"].before(j))
            with sp.Fori(0, steps) as b:
                e = sp.snap(sp.value_load(plan_row[0:1, bass.ds(b + 1, 1)], min_val=0, max_val=EXPERTS - 1))
                e_before = sp.snap(sp.value_load(plan_row[0:1, bass.ds(b, 1)], min_val=0, max_val=EXPERTS - 1))
                for j, (w, at) in enumerate(((w1, e), (w3, e), (w2, e_before))):
                    src = w[bass.ds(at, 1)].rearrange("o p t f -> p (o t) f")
                    for n, (dst, half) in enumerate(pair(ring[:, j, :], src)):
                        for c in range(2):
                            sp.wait_ge(piece_split[4 * j + 2 * n + c], b + 1)
                        sp.dma_start(dst, half).then_inc(half_landed[2 * j + n], 16)
            sp.wait_ge(x_ready, 3 + MT)
            sp.dma_start(out_v, x).then_inc(out_done, 16)
            sp.wait_ge(out_done, 16)

        @block.tensor
        def _(pe):
            def landed(stage, j, i=0):
                st = chunks[stage]
                pe.wait_ge(weights_landed[st.place(j)], (st.before(j, i) + 1) * 32)
                return ring[:, st.place(j), :]

            def bank(stage, k, i=0):
                st = banks[stage]
                n = st.before(k, i)
                if not (isinstance(n, int) and n == 0):
                    pe.wait_ge(bank_drained[st.place(k)], n)
                return ps[:, st.place(k), :]

            def filled(stage, k, last):
                last.then_inc(bank_filled[banks[stage].place(k)], 1)

            def product(o, lhs, rhs):
                for k, (l, r) in enumerate(zip(lhs, rhs)):
                    mm = pe.matmul(o, l, r, start=(k == 0), stop=(k == len(lhs) - 1))
                return mm

            def turn(stage, k, pieces, n=P, i=0):
                o = bank(stage, k, i)
                pe.nop().then_inc(turn_may_start, 1)
                for q, piece in enumerate(pieces):
                    rows = piece.shape[0]
                    f = int(np.prod(piece.shape[1:]))
                    mm = pe.transpose(o[0:f, q * n:q * n + rows], piece, ident[0:rows, 0:rows])
                filled(stage, k, mm)

            def project(stage, srcT, mtiles, widths, rows_wait=None):
                k = 0
                for j, n in enumerate(widths):
                    r = landed(stage, j)
                    w = r[:, 0:KT * n].rearrange("p (k n) -> p k n", k=KT)
                    for m in range(mtiles):
                        o = bank(stage, k)
                        mm = product(o[:, 0:n], [srcT[:, t, m * P:(m + 1) * P] for t in range(KT)],
                                     [w[:, t, :] for t in range(KT)])
                        mm.then_inc(bank_filled[banks[stage].place(k)], 1)
                        k += 1

            pe.wait_ge(const_in, 16)
            pe.wait_ge(cols_in, 16 * 10)
            nrow = TAPS + 7
            o = bank("columns", 0)
            for t in range(KT):
                pe.transpose(o[:, t * nrow:(t + 1) * nrow], colrows[:, t * P:(t + 1) * P], ident[0:nrow, 0:nrow])
            filled("columns", 0, pe.transpose(o[:, KT * nrow:KT * nrow + 8], sgub_rows[:, :], ident[0:8, 0:8]))

            pe.wait_ge(c_rep_ready, KT)
            pe.wait_ge(c_in, 32)
            for j in range(6):
                g = (2, 3, 0, 1, 4, 5)[j]
                w = landed("ada", j).rearrange("p (k n) -> p k n", k=KT)
                o = bank("ada", j)
                for t in range(KT):
                    pe.matmul(o, c_rep[:, t, :], w[:, t, :], start=(t == 0), stop=False)
                filled("ada", j, pe.matmul(o, cst("ones", 1), bada[0:1, g * 512:(g + 1) * 512], start=False, stop=True))

            pe.wait_ge(h0_ready, MT)
            for t in range(KT):
                turn("hT", t, [h0[:, m, t * P:(t + 1) * P] for m in range(MT)])

            pe.wait_ge(hT_ready, KT)
            hT = [actT[:, t, :] for t in range(KT)]
            with pe.Fori(0, KT) as i:
                for j in range(3):
                    w = landed("conv", j, i)[:, 0:KT * P].rearrange("p (k n) -> p k n", k=KT)
                    o = bank("conv", j, i)
                    filled("conv", j, product(o, [w[:, t, :] for t in range(KT)], hT))

            pe.wait_ge(conv_ready, KT)
            filled("ln", 0, product(bank("ln", 0), [cst("mean")] * KT, [convT[:, t, :] for t in range(KT)]))
            o = bank("ln", 1)
            for t in range(KT):
                pe.wait_ge(sq_ready, t + 1)
                mm = pe.matmul(o, cst("mean"), ln_sq[:, t % 2, :], start=(t == 0), stop=(t == KT - 1))
                if t < KT - 1:
                    mm.then_inc(sq_used, 1)
            filled("ln", 1, mm)

            with pe.Fori(0, HEADS) as h:
                w = landed("heads", 0, h).rearrange("p (k n) -> p k n", k=KT)
                for k in range(4):
                    filled("heads", k, product(bank("heads", k, h), [w[:, t, k * P:(k + 1) * P] for t in range(KT)], hT))
                for part in range(2):
                    w = landed("heads", 1 + part, h).rearrange("p (k n) -> p k n", k=KT)
                    for m in range(MT):
                        k = 4 + 4 * part + m
                        filled("heads", k, product(bank("heads", k, h),
                                                   [actT[:, t, m * P:(m + 1) * P] for t in range(KT)],
                                                   [w[:, t, :] for t in range(KT)]))
                pe.wait_ge(qk_ready, (h + 1) * 4)
                for j in range(MT):
                    o = bank("heads", 12 + j, h)[:, 0:S - j * P]
                    filled("heads", 12 + j, product(o, [qk_rot[:, 2 + c, j * P:(j + 1) * P] for c in range(2)],
                                                    [qk_rot[:, c, j * P:S] for c in range(2)]))
                pe.wait_ge(v_ready, (h + 1) * MT)
                pe.wait_ge(decayed_ready, (h + 1) * MT)
                for m in range(MT):
                    filled("heads", 16 + m, product(bank("heads", 16 + m, h),
                                                    [decayed[:, j, m * P:(m + 1) * P] for j in range(m + 1)],
                                                    [v_tok[:, j, :] for j in range(m + 1)]))
                pe.wait_ge(ret_ready, (h + 1) * MT)
                for e in range(4):
                    turn("heads", 20 + e, [z_tok[:, m, e * P:(e + 1) * P] for m in range(MT)], i=h)

            pe.wait_ge(retT_ready, HEADS * 4)
            pe.wait_ge(gated_conv_ready, KT)
            with pe.Fori(0, KT) as i:
                w = landed("mix", 0, i)[:, 0:16 * P].rearrange("p (k n) -> p k n", k=16)
                filled("mix", 0, product(bank("mix", 0, i), [w[:, t, :] for t in range(16)], [retT[:, t, :] for t in range(16)]))
                w = landed("mix", 1, i)[:, 0:KT * P].rearrange("p (k n) -> p k n", k=KT)
                filled("mix", 1, product(bank("mix", 1, i), [w[:, t, :] for t in range(KT)], [convT[:, t, :] for t in range(KT)]))
                w = landed("mix", 2, i)[:, 0:2 * KT * P].rearrange("p (w k n) -> p w k n", w=2, k=KT)
                for g in range(2):
                    filled("mix", 2 + g, product(bank("mix", 2 + g, i), [w[:, g, t, :] for t in range(KT)], hT))

            pe.wait_ge(merged_ready, KT)
            project("out", mergedT, MT, (512, 512))

            def turn_rows(stage, src, n):
                pe.wait_ge(row_ready, n * MT)
                for t in range(KT):
                    turn(stage, t, [src[:, m, t * P:(t + 1) * P] for m in range(MT)])

            turn_rows("h2T", n_tok, 1)
            pe.wait_ge(actT_ready, KT)
            project("in2", actT, MT, (512, 256, 512, 512))

            pe.wait_ge(qk2_ready, 2)
            for r in range(4):
                turn("qkT", r, [q_pair[:, m, r * P:(r + 1) * P] for m in range(MT)])
            turn("qkT", 4, [kv_tok[:, m, 0:P] for m in range(MT)])
            pe.wait_ge(qkT_ready, 5)
            for n in range(MT):
                u = 9 * n
                for v in range(2):
                    for rp in range(2):
                        o = bank("attn", u + 2 * v + rp).rearrange("p (a k) -> p a k", a=2)
                        for c in range(2):
                            mm = pe.matmul(o[:, c, :], qT[v * AD:(v + 1) * AD, 2 * rp + c, n * P:(n + 1) * P],
                                           kT[v * AD:(v + 1) * AD, n * P:(n + 2) * P], start=True, stop=True)
                        filled("attn", u + 2 * v + rp, mm)
                pe.wait_ge(p_ready, AH * (n + 1))
                for hp in range(4):
                    turn("attn", u + 4 + hp, [p_tok[:, 2 * hp + c, w * P:(w + 1) * P] for c in range(2) for w in range(2)])
                pe.wait_ge(pT_ready, 4 * (n + 1))
                o = bank("attn", u + 8)
                for hd in range(AH):
                    v = hd // 4
                    halves = (0, 1) if n else (1,)
                    for w in halves:
                        mm = pe.matmul(o[:, hd * AD:(hd + 1) * AD], pT[:, 2 * hd + w, :],
                                       kv_tok[:, n - 1 + w, P + v * AD:P + (v + 1) * AD],
                                       start=(w == halves[0]), stop=(w == 1))
                filled("attn", u + 8, mm)

            pe.wait_ge(sguw_in, 16)
            for c in range(2):
                turn("sguw", c, [sgu_w[:, 4 * c + g, :] for g in range(4)])
            pe.wait_ge(sguwT_ready, 2)
            pe.wait_ge(vc_ready, 1)
            for gp in range(4):
                o = bank("sgu", gp).rearrange("p (a c d) -> p a c d", a=2, c=MT)
                for c in range(2):
                    g = 2 * gp + c
                    mm = pe.matmul(o[:, c], sgu_wT[:, g, :], g_tok[:, :, g * AD:(g + 1) * AD], start=True, stop=True)
                filled("sgu", gp, mm)
            turn_rows("mixT", n_tok, 2)
            pe.wait_ge(actT_ready, 2 * KT)
            project("out2", actT, MT, (512, 512))

            pe.wait_ge(vc_ready, 1 + MM)
            for c in range(4):
                turn("memT", c, [mem[:, m, (2 * c + q) * P:(2 * c + q + 1) * P] for q in range(2) for m in range(MM)])
            pe.wait_ge(memT_ready, KT)
            project("xk", memT, MM, (512, 512))
            project("xv", memT, MM, (512, 512))
            pe.wait_ge(xk_ready, 1)
            for c in range(4):
                turn("xkT", c, [xk_tok[:, m, (2 * c + q) * P:(2 * c + q + 1) * P] for q in range(2) for m in range(MM)])
            pe.wait_ge(vc_ready, 1 + MM + MT)
            for t in range(KT):
                turn("hqT", t, [n_tok[:, m, t * P:(t + 1) * P] for m in range(MT)])
            pe.wait_ge(actT_ready, 3 * KT)
            project("xq", actT, MT, (512, 512))
            pe.wait_ge(xq_ready, MT)
            for t in range(KT):
                turn("xqT", t, [xq_tok[:, m, t * P:(t + 1) * P] for m in range(MT)])
            pe.wait_ge(xkT_ready, 4)
            pe.wait_ge(xqT_ready, KT)
            for m in range(MT):
                for hp in range(2):
                    o = bank("xs", 2 * m + hp).rearrange("p (a k) -> p a k", a=2)
                    for c in range(2):
                        hd = 2 * hp + c
                        mm = product(o[:, c, :], [xqT[:, 2 * hd + q, m * P:(m + 1) * P] for q in range(2)],
                                     [xkT[:, 2 * hd + q, :] for q in range(2)])
                    filled("xs", 2 * m + hp, mm)
            pe.wait_ge(xp_ready, MT * XH)
            for k in range(2 * XH):
                turn("xpT", k, [xp_tok[:, m, k // 2, (k % 2) * P:(k % 2 + 1) * P] for m in range(MT)])
            pe.wait_ge(xpT_ready, KT)
            for t in range(KT):
                filled("xo", t, product(bank("xo", t), [xv_tok[:, w, t * P:(t + 1) * P] for w in range(MM)],
                                        [xpT[:, 2 * (t // 2) + w, :] for w in range(MM)]))
            pe.wait_ge(xoT_ready, KT)
            project("xout", xoT, MT, (512, 512))

            turn_rows("h3T", h3_tok, 3)
            pe.wait_ge(actT_ready, 4 * KT)
            pe.wait_ge(ffn_in, 16 * (2 + GROUPS))
            o = bank("route", 0)
            nl = GROUPS + EXPERTS
            for m in range(MT):
                mm = product(o[:, m * nl:(m + 1) * nl], [actT[:, t, m * P:(m + 1) * P] for t in range(KT)],
                             [wr[:, t, :] for t in range(KT)])
            filled("route", 0, mm)
            pe.wait_ge(oh_ready, MT)
            o = bank("route", 1)
            for m in range(MT):
                product(o[:, m * EXPERTS:(m + 1) * EXPERTS], [cst("ones")] * m + [cst("before")],
                        [ohs[:, q, :] for q in range(m + 1)])
            mm = product(o[:, MT * EXPERTS:(MT + 1) * EXPERTS], [cst("ones")] * MT, [ohs[:, q, :] for q in range(MT)])
            filled("route", 1, mm)
            pe.wait_ge(plan_col_ready, 1)
            filled("route", 2, pe.transpose(bank("route", 2)[0:1, 0:P], plan_col, ident))
            pe.wait_ge(slot_oh_ready, 1)
            filled("route", 3, product(bank("route", 3)[0:SLOTS, 0:64], [slot_oh[:, q, :] for q in range(2 * MT)],
                                       [block_oh[:, q, :] for q in range(2 * MT)]))

            def mark(signal):
                pe.matmul(ps[:, 7, 0:1], mark_src[:, :], mark_src[:, 0:1], start=True, stop=True).then_inc(signal, 1)

            def split_product(o, lhs, rhs, start, stop):
                pe.matmul(o, lhs[1], rhs[0], start=start, stop=False)
                pe.matmul(o, lhs[0], rhs[1], start=False, stop=False)
                return pe.matmul(o, lhs[0], rhs[0], start=False, stop=stop)

            def turn_slots(stage, k, rows, n, i=0):
                o = bank(stage, k, i)
                pe.nop().then_inc(turn_may_start, 1)
                for q in range(n):
                    mm = pe.transpose(o[:, q * SLOTS:(q + 1) * SLOTS], rows[0:SLOTS, q * P:(q + 1) * P], ident[0:SLOTS, 0:SLOTS])
                filled(stage, k, mm)

            pe.wait_ge(plan_ready, 2)
            steps = pe.snap(pe.value_load(n_steps[0:1, 0:1], min_val=2, max_val=MAX_BLOCKS + 1))
            pe.wait_ge(bank_drained[7], banks["moe"].base[7])
            for q in range(4):
                mark(piece_used[q])
            pe.wait_ge(xg_in, 16)
            turn_slots("moe0", 0, xg, KT)
            for g in range(3):
                filled("moe0", 1 + g, pe.matmul(bank("moe0", 1 + g), ident, const[:, 0:512], start=True, stop=True))
            with pe.Fori(0, steps) as b:
                st = banks["moe"]
                for j in range(2):
                    o = bank("moe", 1 + j, b)[0:SLOTS, :]
                    if j == 0:
                        pe.wait_ge(bank_drained[st.place(0)], st.before(0, b))
                    for n in range(4):
                        pe.wait_ge(piece_split[4 * j + n], b + 2)
                        for c in range(2):
                            t = 2 * n + c
                            mm = split_product(o, [xgT[:, h, t, :] for h in range(2)],
                                               [parts[:, n, h, c * 512:(c + 1) * 512] for h in range(2)],
                                               n == 0 and c == 0, n == 3 and c == 1)
                        if n == 3:
                            filled("moe", 1 + j, mm)
                        mark(piece_used[n])
                pe.wait_ge(xg_in, (b + 2) * 16)
                turn_slots("moe", 0, xg, KT, b)
                ys = [bank("moe", 4 + g, b)[0:SLOTS, :] for g in range(2)]
                pe.wait_ge(bank_drained[st.place(3)], st.before(3, b))
                for n in range(4):
                    pe.wait_ge(piece_split[8 + n], b + 2)
                    for g in range(2):
                        mm = split_product(ys[g], [hidT[:, h, n, :] for h in range(2)],
                                           [parts[:, n, h, g * 512:(g + 1) * 512] for h in range(2)], n == 0, n == 3)
                        if n == 3:
                            filled("moe", 4 + g, mm)
                    mark(piece_used[n])
                pe.wait_ge(hid_ready, b + 1)
                turn_slots("moe", 3, hid, 4, b)

        @block.scalar
        def _(act):
            own = Chain(act, act_own)

            def full(stage, k, i=0):
                st = banks[stage]
                act.wait_ge(bank_filled[st.place(k)], st.before(k, i) + 1)
                return ps[:, st.place(k), :]

            def drained(stage, k, ins):
                ins.then_inc(bank_drained[banks[stage].place(k)], 1)

            def release(stage, j):
                act.nop().then_inc(weights_used[chunks[stage].place(j)], 1)

            def roots(n, src, dst, eps_col, scale=1.0):
                act.wait_ge(ms_ready, n)
                act.activation(dst, src, ACT.Sqrt, bias=eps[:, eps_col:eps_col + 1], scale=scale).then_inc(rms_ready, 1)

            roots(1, st_ms[:, 0:MT], st_rms[:, 0:MT], 0, 1.0 / D)
            act.wait_ge(angles_ready, 1)
            own(act.activation(sinT, angle, ACT.Sin))
            own(act.activation(cosT, turns, ACT.Sin))
            own.wait()
            act.nop().then_inc(rotary_ready, 1)
            for t in range(KT):
                act.copy(actT[:, t, :], full("hT", t)).then_inc(hT_ready, 1)
            act.wait_ge(hT_ready, KT)
            for t in range(KT):
                drained("hT", t, act.nop())

            with act.Fori(0, KT) as i:
                full("conv", 0, i)
                release("conv", 0)
                o = full("conv", 1, i)
                release("conv", 1)
                act.activation(sig_u, o, ACT.Sigmoid).then_inc(sig_u_ready, 1)
                act.wait_ge(sig_u_ready, i + 1)
                drained("conv", 1, act.nop())
                o = full("conv", 2, i)
                release("conv", 2)
                act.activation(sig_z, o, ACT.Sigmoid).then_inc(sig_z_ready, 1)

            for t in range(KT):
                act.wait_ge(cen_ready, t + 1)
                if t >= 2:
                    act.wait_ge(sq_used, t - 1)
                act.activation(ln_sq[:, t % 2, :], convT[:, t, :], ACT.Square).then_inc(sq_ready, 1)
            o = full("ln", 1)
            own(act.activation(ln_std, o, ACT.Sqrt, bias=eps[:, 2:3]))
            own.wait()
            drained("ln", 1, act.nop())
            act.nop().then_inc(ln_std_ready, 1)
            for t in range(KT):
                act.wait_ge(ln_y_ready, t + 1)
                if t >= 2:
                    act.wait_ge(gated_conv_ready, t - 1)
                g, bias = cols[:, t, TAPS + 1:TAPS + 2], cols[:, t, TAPS + 2:TAPS + 3]
                own(act.activation(ln_y[:, t % 2, :], ln_y[:, t % 2, :], ACT.Identity, bias=bias, scale=g))
                own.wait()
                act.activation(ln_s[:, t % 2, :], ln_y[:, t % 2, :], ACT.Sigmoid).then_inc(ln_s_ready, 1)

            with act.Fori(0, HEADS) as h:
                own.enter(h, 8)
                act.wait_ge(gated_conv_ready, KT)
                full("heads", 3, h)
                release("heads", 0)
                for m in range(MT):
                    o = full("heads", 4 + m, h)
                    if m == MT - 1:
                        release("heads", 1)
                    own(act.copy(v_tok[:, m, :], o))
                    own.wait()
                    act.nop().then_inc(v_ready, 1)
                    drained("heads", 4 + m, act.nop())
                for m in range(MT):
                    o = full("heads", 8 + m, h)
                    if m == MT - 1:
                        release("heads", 2)
                    if m >= 2:
                        act.wait_ge(sig_r_used, h * MT + (m - 1))
                    act.activation(sig_r[:, m % 2, :], o, ACT.Sigmoid).then_inc(sig_r_ready, 1)
                act.wait_ge(var_ready, h + 1)
                act.activation(st_std, mv.rearrange("p (m s) -> p m s", s=2)[:, :, 1], ACT.Sqrt,
                               bias=eps[:, 1:2]).then_inc(std_ready, 1)
                for e in range(4):
                    o = full("heads", 20 + e, h)
                    own(act.copy(retT[:, bass.ds(h * 4 + e, 1), :], o))
                    own.wait()
                    act.nop().then_inc(retT_ready, 1)
                    drained("heads", 20 + e, act.nop())
            own.leave(HEADS)

            with act.Fori(0, KT) as i:
                own.enter(i, 2)
                for j in range(2):
                    full("mix", j, i)
                    release("mix", j)
                for g, s in ((0, sig_a), (1, sig_b)):
                    o = full("mix", 2 + g, i)
                    if g:
                        release("mix", 2)
                    own(act.activation(s, o, ACT.Sigmoid))
                    own.wait()
                    act.nop().then_inc(sig_ab_ready, 1)
                    drained("mix", 2 + g, act.nop())
            own.leave(KT)

            def take(stage, k, dst, func=ACT.Copy, done=None, n=512, mtiles=None):
                o = full(stage, k)
                if mtiles and k % mtiles == mtiles - 1:
                    release(stage, k // mtiles)
                own(act.activation(dst, o[:, 0:n], func))
                own.wait()
                drained(stage, k, act.nop())
                if done is not None:
                    act.nop().then_inc(done, 1)

            act.wait_ge(retT_ready, HEADS * 4)
            for k in range(8):
                take("out", k, y_tok[:, k % MT, (k // MT) * 512:(k // MT + 1) * 512], done=y_ready, mtiles=MT)
            roots(2, st_ms[:, 0:MT], st_rms[:, 0:MT], 0, 1.0 / D)

            def take_T(stage, col):
                for t in range(KT):
                    o = full(stage, t)
                    kw = {} if col is None else {"scale": cols[:, t, col:col + 1]}
                    own(act.activation(actT[:, t, :], o, ACT.Copy, **kw))
                    own.wait()
                    drained(stage, t, act.nop())
                    act.nop().then_inc(actT_ready, 1)

            roots(3, st_ms[:, 0:MT], st_rms[:, 0:MT], 0, 1.0 / D)
            take_T("h2T", TAPS + 3)
            for k in range(16):
                j, m = k // MT, k % MT
                dst, n = ((q_tok, 512), (kv_tok, 256), (u_tok, 512), (g_tok, 512))[j]
                take("in2", k, dst[:, m, :], ACT.Gelu_apprx_tanh if j >= 2 else ACT.Copy, done=in2_ready, n=n, mtiles=MT)
            roots(4, st_ms[:, 0:32], st_rms[:, 0:32], 0, 1.0 / AD)
            roots(5, st_ms[:, 0:MT * 2], st_rms[:, 0:MT * 2], 0, 1.0 / AD)
            roots(6, st_ms[:, 0:MT], st_rms[:, 0:MT], 0, 1.0 / 512)
            for r in range(4):
                take("qkT", r, qT[:, r, :], done=qkT_ready)
            take("qkT", 4, kT[:, P:], done=qkT_ready)
            for n in range(MT):
                act.wait_ge(smax_ready, n + 1)
                if n:
                    act.wait_ge(pT_ready, 4 * n)
                for hd in range(AH):
                    act.activation(p_tok[:, hd, :], s_tok[:, hd, :], ACT.Exp, bias=nmx[:, hd:hd + 1],
                                   accum_out=den[:, hd:hd + 1]).then_inc(p_ready, 1)
                act.activation(sinkx, sinkx, ACT.Exp).then_inc(sink_exp, 1)
            roots(7, st_ms[:, 0:2 * MT], st_rms[:, 0:2 * MT], 0, 1.0 / 512)
            take_T("mixT", TAPS + 6)

            roots(8, st_ms[:, 0:MM], st_rms[:, 0:MM], 0, 1.0 / D)
            for c in range(4):
                o = full("memT", c).rearrange("p (q n) -> p q n", q=2)
                for q in range(2):
                    own(act.activation(memT[:, 2 * c + q, :], o[:, q, :], ACT.Copy, scale=cols[:, 2 * c + q, TAPS + 5:TAPS + 6]))
                own.wait()
                drained("memT", c, act.nop())
                for q in range(2):
                    act.nop().then_inc(memT_ready, 1)
            for stage, dst in (("xk", xk_tok), ("xv", xv_tok)):
                for k in range(4):
                    take(stage, k, dst[:, k % MM, (k // MM) * 512:(k // MM + 1) * 512], done=xkv_ready, mtiles=MM)
            roots(9, st_ms[:, 0:MM * XH], st_rms[:, 0:MM * XH], 0, 1.0 / XD)
            for c in range(4):
                take("xkT", c, xkT[:, 2 * c:2 * c + 2, :].rearrange("p q n -> p (q n)"), done=xkT_ready)
            roots(10, st_ms[:, 0:MT], st_rms[:, 0:MT], 0, 1.0 / D)
            take_T("hqT", TAPS + 4)
            for k in range(8):
                take("xq", k, xq_tok[:, k % MT, (k // MT) * 512:(k // MT + 1) * 512], done=xq_in, mtiles=MT)
            roots(11, st_ms[:, 0:MT * XH], st_rms[:, 0:MT * XH], 0, 1.0 / XD)
            for t in range(KT):
                take("xqT", t, xqT[:, t, :], done=xqT_ready)
            for m in range(MT):
                for hp in range(2):
                    act.wait_ge(xmax_ready, 2 * m + hp + 1)
                    o = full("xs", 2 * m + hp).rearrange("p (a k) -> p a k", a=2)
                    for c in range(2):
                        hd = m * XH + 2 * hp + c
                        own(act.activation(xp_tok[:, m, 2 * hp + c, :], o[:, c, :], ACT.Exp, bias=nmx[:, hd:hd + 1],
                                           accum_out=den[:, hd:hd + 1]))
                    own.wait()
                    drained("xs", 2 * m + hp, act.nop())
                act.nop().then_inc(xq_in, 1)
            for k in range(8):
                take("xpT", k, xpT[:, k, :], done=xpT_ready)
            for t in range(KT):
                take("xo", t, xoT[:, t, :], done=xoT_ready)

            roots(12, st_ms[:, 0:MT], st_rms[:, 0:MT], 0, 1.0 / D)
            take_T("h3T", None)
            act.wait_ge(gexp_in, 1)
            act.activation(gexp, gexp, ACT.Exp).then_inc(gexp_ready, 1)
            act.wait_ge(texp_in, 1)
            act.activation(dl, dl, ACT.Exp).then_inc(texp_ready, 1)
            act.wait_ge(plan_ready, 2)
            steps = act.snap(act.value_load(n_steps[0:1, 0:1], min_val=2, max_val=MAX_BLOCKS + 1))
            act.wait_ge(y_cleared, 16)
            act.nop().then_inc(y_stored, 16)

            def high(n, b):
                j = n // 4
                act.wait_ge(half_landed[2 * j + n % 4 // 2], (b + 1) * 16)
                act.wait_ge(piece_used[n % 4], b * 3 + (n // 4 + 1))
                act.copy(parts[:, n % 4, 0, :], ring[:, j, n % 4 * 1024:(n % 4 + 1) * 1024]).then_inc(piece_hi, 1)

            def store_rows(b):
                st = banks["moe"]
                act.wait_ge(y_stored, (b + 1) * 16)
                for g in range(2):
                    act.wait_ge(bank_filled[st.place(4 + g)], st.before(4 + g, b))
                    own(act.copy(y_blk[0:SLOTS, g * 512:(g + 1) * 512], ps[0:SLOTS, st.place(4 + g), :]))
                own.wait()
                for g in range(2):
                    drained("moe", 4 + g, act.nop())
                act.dma_start(y_rows[bass.ds(b * SLOTS, SLOTS), :], y_blk[0:SLOTS, :]).then_inc(y_stored, 16)

            act.copy(xgT[:, 0].rearrange("p t n -> p (t n)"), full("moe0", 0)).then_inc(xgT_hi, 1)
            with act.Fori(0, steps) as b:
                own.enter(b, 2)
                for n in range(4):
                    high(n, b)
                store_rows(b)
                st = banks["moe"]
                act.wait_ge(bank_filled[st.place(3)], st.before(3, b))
                act.copy(hidT[:, 0].rearrange("p t n -> p (t n)"), ps[:, st.place(3), 0:4 * SLOTS]).then_inc(hidT_hi, 1)
                for n in range(4, 8):
                    high(n, b)
                act.activation(sg_h[0:SLOTS, :], full("moe", 1, b)[0:SLOTS, :], ACT.Sigmoid).then_inc(sg_h_ready, 1)
                for n in range(8, 12):
                    high(n, b)
                o = full("moe", 0, b)
                act.copy(xgT[:, 0].rearrange("p t n -> p (t n)"), o).then_inc(xgT_hi, 1)
            own.base = act.snap(steps * own.per + own.at)
            own.count = 0
            store_rows(steps)
            act.wait_ge(y_stored, steps * 16 + 32)
            act.nop().then_inc(y_blk_ready, 1)

        @block.vector
        def _(dve):
            own = Chain(dve, dve_own)

            def full(stage, k, i=0):
                st = banks[stage]
                dve.wait_ge(bank_filled[st.place(k)], st.before(k, i) + 1)
                return ps[:, st.place(k), :]

            def drained(stage, k, ins):
                ins.then_inc(bank_drained[banks[stage].place(k)], 1)

            def mean_squares(srcs, dst, junk, ready_n=None):
                for m, s in enumerate(srcs):
                    own(dve.tensor_tensor_reduce(out=junk, in0=s, in1=s, scale=1.0, scalar=0.0, op0=ALU.mult,
                                                 op1=ALU.add, accum_out=dst[:, m:m + 1]))
                    own.wait()
                dve.nop().then_inc(ms_ready, 1)

            def head_squares(src, groups, width, dst, junk):
                own(dve.tensor_tensor(junk, src, src, ALU.mult))
                own.wait()
                own(dve.tensor_reduce(dst, junk.rearrange("p (g d) -> p g d", d=width), AX.X, ALU.add))
                own.wait()

            def reciprocals(n, cnt_):
                dve.wait_ge(rms_ready, n)
                own(dve.reciprocal(st_r[:, 0:cnt_], st_rms[:, 0:cnt_]))
                own.wait()

            for n, v in enumerate((RMS_EPS, GN_EPS, LN_EPS)):
                own(dve.memset(eps[:, n:n + 1], v))
            own(dve.memset(mark_src[:, :], 0.0))
            dve.wait_ge(const_in, 16)
            dve.wait_ge(c_in, 32)
            for t in range(KT):
                dve.tensor_scalar(c_rep[:, t, :], cst("ones"), c_col[:, t:t + 1], None, ALU.mult).then_inc(c_rep_ready, 1)
            dve.wait_ge(x_in, 16)
            own.wait()
            mean_squares([x0[:, m, :] for m in range(MT)], st_ms, h0[:, 0, :])

            dve.wait_ge(pos_in, 16)
            own(dve.tensor_copy(angle, pos_i[:, :]))
            own.wait()
            own(dve.tensor_scalar(angle, angle, cst("freq"), None, ALU.mult))
            own.wait()
            magic = float(1.5 * 2 ** 23)
            own(dve.tensor_scalar(turns, angle, float(1 / (2 * np.pi)), magic, ALU.mult, ALU.add))
            own.wait()
            own(dve.tensor_scalar(turns, turns, magic, None, ALU.subtract))
            own.wait()
            left = 2 * np.pi
            for bits in (5, 13, None):
                part = float(np.float32(left)) if bits is None else float(np.floor(left * 2 ** bits) / 2 ** bits)
                left -= part
                own(dve.scalar_tensor_tensor(out=angle, in0=turns, scalar=-part, in1=angle, op0=ALU.mult, op1=ALU.add))
                own.wait()
            lim = 3.1415925
            own(dve.tensor_scalar(angle, angle, lim, -lim, ALU.min, ALU.max))
            own.wait()
            own(dve.scalar_tensor_tensor(out=turns, in0=angle, scalar=-1.0, in1=angle, op0=ALU.mult, op1=ALU.max))
            own.wait()
            own(dve.tensor_scalar(turns, turns, -1.0, float(np.pi / 2), ALU.mult, ALU.add))
            own.wait()
            dve.nop().then_inc(angles_ready, 1)

            full("columns", 0)
            o = ps[:, 0, :]
            nrow = TAPS + 7
            own(dve.tensor_copy(cols[:, :, :], o[:, 0:KT * nrow].rearrange("p (t r) -> p t r", t=KT)))
            own(dve.tensor_copy(sgub[:, :], o[:, KT * nrow:KT * nrow + 8]))
            own.wait()
            drained("columns", 0, dve.nop())

            dve.wait_ge(rows_in, 32)
            def release(stage, j):
                dve.nop().then_inc(weights_used[chunks[stage].place(j)], 1)

            for j in range(6):
                o = full("ada", j)
                release("ada", j)
                half = slice((j % 2) * 512, (j % 2) * 512 + 512)
                if j < 2:
                    own(dve.scalar_tensor_tensor(out=mod_scale[:, half], in0=o, scalar=1.0, in1=pre_g[:, half],
                                                 op0=ALU.add, op1=ALU.mult))
                elif j < 4:
                    own(dve.tensor_copy(mod_shift[:, half], o))
                else:
                    own(dve.tensor_tensor(gate_post[:, half], o, post_g[:, half], ALU.mult))
                own.wait()
                drained("ada", j, dve.nop())
                if j == 3:
                    reciprocals(1, MT)
                    for m in range(MT):
                        own(dve.scalar_tensor_tensor(out=h0[:, m, :], in0=x0[:, m, :], scalar=st_r[:, m:m + 1],
                                                     in1=mod_scale, op0=ALU.mult, op1=ALU.mult))
                    own.wait()
                    for m in range(MT):
                        dve.tensor_tensor(h0[:, m, :], h0[:, m, :], mod_shift, ALU.add).then_inc(h0_ready, 1)

            dve.wait_ge(h0_ready, MT)
            dve.wait_ge(hT_ready, KT)
            dve.wait_ge(rotary_ready, 1)
            own(dve.memset(apad[:, 0:TAPS - 1], 0.0))
            own.wait()
            with dve.Fori(0, KT) as i:
                own.enter(i, 2 + TAPS + 1)
                o = full("conv", 0, i)
                dve.wait_ge(sig_u_ready, i + 1)
                own(dve.tensor_tensor(apad[:, TAPS - 1:], o, sig_u, ALU.mult))
                own.wait()
                drained("conv", 0, dve.nop())
                dve.wait_ge(sig_z_ready, i + 1)
                own(dve.tensor_tensor(zconvT[:, bass.ds(i, 1), :], full("conv", 2, i), sig_z, ALU.mult))
                own.wait()
                drained("conv", 2, dve.nop())
                col = cols[:, bass.ds(i, 1), :].rearrange("p o r -> p (o r)")
                for j in range(TAPS):
                    acc = conv_acc[:, j % 2, :]
                    if j == 0:
                        own(dve.tensor_scalar(acc, apad[:, 0:S], col[:, 0:1], col[:, TAPS:TAPS + 1], ALU.mult, ALU.add))
                    elif j == 1:
                        own(dve.tensor_scalar(acc, apad[:, 1:1 + S], col[:, 1:2], None, ALU.mult))
                    else:
                        own.wait(1)
                        own(dve.scalar_tensor_tensor(out=acc, in0=apad[:, j:j + S], scalar=col[:, j:j + 1], in1=acc,
                                                     op0=ALU.mult, op1=ALU.add))
                own.wait()
                own(dve.tensor_tensor(convT[:, bass.ds(i, 1), :], conv_acc[:, 0, :], conv_acc[:, 1, :], ALU.add))
                own.wait()
                dve.nop().then_inc(conv_ready, 1)
            own.leave(KT)

            o = full("ln", 0)
            for t in range(KT):
                own(dve.tensor_tensor(convT[:, t, :], convT[:, t, :], o, ALU.subtract))
                own.wait()
                dve.nop().then_inc(cen_ready, 1)
            drained("ln", 0, dve.nop())
            dve.wait_ge(ln_std_ready, 1)
            own(dve.reciprocal(ln_rstd, ln_std))
            own.wait()
            for t in range(KT + 1):
                if t < KT:
                    if t >= 2:
                        dve.wait_ge(gated_conv_ready, t - 1)
                    dve.tensor_tensor(ln_y[:, t % 2, :], convT[:, t, :], ln_rstd, ALU.mult).then_inc(ln_y_ready, 1)
                if t:
                    q = t - 1
                    dve.wait_ge(ln_s_ready, q + 1)
                    own(dve.tensor_tensor(convT[:, q, :], ln_y[:, q % 2, :], ln_s[:, q % 2, :], ALU.mult))
                    own.wait()
                    dve.tensor_tensor(convT[:, q, :], convT[:, q, :], zconvT[:, q, :], ALU.mult).then_inc(gated_conv_ready, 1)

            dve.wait_ge(gated_conv_ready, KT)
            dve.nop().then_inc(decay_used, MT)
            with dve.Fori(0, HEADS) as h:
                own.enter(h, 12 + 5 * MT + 1)
                for part in range(2):
                    t1, t2 = full("heads", 2 * part, h), full("heads", 2 * part + 1, h)
                    own(dve.tensor_tensor(rot[:, 0, :], t1, cosT, ALU.mult))
                    own(dve.tensor_tensor(rot[:, 1, :], t2, sinT, ALU.mult))
                    own(dve.tensor_tensor(rot[:, 2, :], t1, sinT, ALU.mult))
                    own(dve.tensor_tensor(rot[:, 3, :], t2, cosT, ALU.mult))
                    own.wait()
                    for q in range(2):
                        drained("heads", 2 * part + q, dve.nop())
                    own(dve.tensor_tensor(qk_rot[:, 2 * part, :], rot[:, 0, :], rot[:, 1, :], ALU.subtract))
                    own(dve.tensor_tensor(qk_rot[:, 2 * part + 1, :], rot[:, 2, :], rot[:, 3, :], ALU.add))
                    own.wait()
                    for q in range(2):
                        dve.nop().then_inc(qk_ready, 1)
                for m in range(MT):
                    o = full("heads", 8 + m, h)
                    dve.wait_ge(sig_r_ready, h * MT + m + 1)
                    own(dve.tensor_tensor(z_tok[:, m, :], o, sig_r[:, m % 2, :], ALU.mult))
                    own.wait()
                    dve.nop().then_inc(sig_r_used, 1)
                    drained("heads", 8 + m, dve.nop())
                dve.wait_ge(decay_in, (h + 1) * 16)
                for j in range(MT):
                    o = full("heads", 12 + j, h)
                    own(dve.tensor_tensor(decayed[:, j, j * P:S], o[:, 0:S - j * P], decay[:, 0:S - j * P], ALU.mult))
                    own.wait()
                    dve.nop().then_inc(decayed_ready, 1)
                    dve.nop().then_inc(decay_used, 1)
                    drained("heads", 12 + j, dve.nop())
                for m in range(MT):
                    own(dve.bn_stats(bn6[:, 6 * m:6 * m + 6], full("heads", 16 + m, h)))
                own.wait()
                dve.nop().then_inc(stats_settled, 1)
                for m in range(MT):
                    own(dve.bn_aggr(mv[:, 2 * m:2 * m + 2], bn6[:, 6 * m:6 * m + 6]))
                own.wait()
                dve.nop().then_inc(var_ready, 1)
                dve.wait_ge(std_ready, h + 1)
                own(dve.reciprocal(gn_r, st_std))
                own.wait()
                for m in range(MT):
                    o = ps[:, banks["heads"].place(16 + m), :]
                    if m >= 2:
                        dve.wait_ge(ret_ready, h * MT + (m - 1))
                    own(dve.tensor_scalar(norm_o[:, m % 2, :], o, mv[:, 2 * m:2 * m + 1], gn_r[:, m:m + 1],
                                          ALU.subtract, ALU.mult))
                    own.wait()
                    drained("heads", 16 + m, dve.nop())
                    dve.tensor_tensor(z_tok[:, m, :], norm_o[:, m % 2, :], z_tok[:, m, :], ALU.mult).then_inc(ret_ready, 1)
            own.leave(HEADS)

            with dve.Fori(0, KT) as i:
                own.enter(i, 3)
                dve.wait_ge(sig_ab_ready, (i + 1) * 2)
                own(dve.tensor_tensor(part_a, full("mix", 0, i), sig_a, ALU.mult))
                own(dve.tensor_tensor(part_b, full("mix", 1, i), sig_b, ALU.mult))
                own.wait()
                for g in range(2):
                    drained("mix", g, dve.nop())
                own(dve.tensor_tensor(mergedT[:, bass.ds(i, 1), :], part_a, part_b, ALU.add))
                own.wait()
                dve.nop().then_inc(merged_ready, 1)
            own.leave(KT)

            dve.wait_ge(y_ready, 8)
            mean_squares([y_tok[:, m, :] for m in range(MT)], st_ms, squares)
            reciprocals(2, MT)
            dve.wait_ge(x_back, 16)
            for m in range(MT):
                own(dve.scalar_tensor_tensor(out=y_tok[:, m, :], in0=y_tok[:, m, :], scalar=st_r[:, m:m + 1],
                                             in1=gate_post, op0=ALU.mult, op1=ALU.mult))
            own.wait()
            for m in range(MT):
                own(dve.tensor_tensor(x[:, m, :], x[:, m, :], y_tok[:, m, :], ALU.add))
            own.wait()
            dve.nop().then_inc(x_ready, 1)

            def norm_rows(n, dst, done, junk, gain=None):
                mean_squares([x[:, m, :] for m in range(MT)], st_ms, junk)
                reciprocals(n, MT)
                for m in range(MT):
                    if gain is None:
                        dve.tensor_scalar(dst[:, m, :], x[:, m, :], st_r[:, m:m + 1], None, ALU.mult).then_inc(done, 1)
                    else:
                        dve.scalar_tensor_tensor(out=dst[:, m, :], in0=x[:, m, :], scalar=st_r[:, m:m + 1], in1=gain,
                                                 op0=ALU.mult, op1=ALU.mult).then_inc(done, 1)

            norm_rows(3, n_tok, row_ready, sq_junk[:, 0:2, :].rearrange("p m d -> p (m d)"))

            dve.wait_ge(gains_in, 64)
            dve.wait_ge(in2_ready, 16)
            dve.wait_ge(row_ready, MT)
            flat = lambda v: v.rearrange("p m d -> p (m d)")
            head_squares(flat(q_tok), 32, AD, st_ms[:, 0:32], flat(sq_junk))
            dve.nop().then_inc(ms_ready, 1)
            reciprocals(4, 32)

            def head_scale(v, nheads, width):
                r = st_r[:, 0:nheads].unsqueeze(2).to_broadcast([P, nheads, width])
                own(dve.tensor_tensor(v, v, r, ALU.mult))
                own.wait()

            def head_gain(v, nheads, gain, scale, width):
                g = gain.unsqueeze(1).to_broadcast([P, nheads, width])
                own(dve.scalar_tensor_tensor(out=v, in0=v, scalar=scale, in1=g, op0=ALU.mult, op1=ALU.mult))
                own.wait()

            head_scale(q_tok.rearrange("p m (h d) -> p (m h) d", d=AD), 32, AD)
            for m in range(MT):
                for v in range(2):
                    heads = q_tok[:, m, v * 256:(v + 1) * 256].rearrange("p (r d) -> p r d", d=AD)
                    pairs = q_pair[:, m, :].rearrange("p (r v d) -> p r v d", r=4, v=2)[:, :, v, :]
                    own(dve.scalar_tensor_tensor(out=pairs, in0=heads, scalar=AD ** -0.5,
                                                 in1=qn_row.unsqueeze(1).to_broadcast([P, 4, AD]),
                                                 op0=ALU.mult, op1=ALU.mult))
            own.wait()
            dve.nop().then_inc(qk2_ready, 1)
            for m in range(MT):
                own(dve.tensor_tensor(sq_junk[:, m, 0:P], kv_tok[:, m, 0:P], kv_tok[:, m, 0:P], ALU.mult))
            own.wait()
            for m in range(MT):
                own(dve.tensor_reduce(st_ms[:, 2 * m:2 * m + 2], sq_junk[:, m, 0:P].rearrange("p (g d) -> p g d", d=AD),
                                      AX.X, ALU.add))
            own.wait()
            dve.nop().then_inc(ms_ready, 1)
            reciprocals(5, 8)
            for m in range(MT):
                for v in range(2):
                    k = kv_tok[:, m, v * AD:(v + 1) * AD]
                    own(dve.scalar_tensor_tensor(out=k, in0=k, scalar=st_r[:, 2 * m + v:2 * m + v + 1], in1=kn_row,
                                                 op0=ALU.mult, op1=ALU.mult))
            own(dve.memset(kT[:, 0:P], 0.0))
            own.wait()
            dve.nop().then_inc(qk2_ready, 1)
            mean_squares([g_tok[:, m, :] for m in range(MT)], st_ms, sq_junk[:, 0, :])
            reciprocals(6, MT)
            for m in range(MT):
                own(dve.scalar_tensor_tensor(out=g_tok[:, m, :], in0=g_tok[:, m, :], scalar=st_r[:, m:m + 1], in1=sgun_row,
                                             op0=ALU.mult, op1=ALU.mult))
            own.wait()
            dve.nop().then_inc(vc_ready, 1)

            for n in range(MT):
                mask = cst("band" if n else "first").unsqueeze(1).to_broadcast([P, 2, 2 * P])
                if n:
                    dve.wait_ge(p_ready, AH * n)
                for q in range(4):
                    o = full("attn", 9 * n + q).rearrange("p (a k) -> p a k", a=2)
                    own(dve.tensor_tensor(s_tok[:, 2 * q:2 * q + 2, :], o, mask, ALU.add))
                    own.wait()
                    drained("attn", 9 * n + q, dve.nop())
                own(dve.tensor_reduce(mx[:, 0:AH], s_tok, AX.X, ALU.max))
                own.wait()
                own(dve.tensor_tensor(mx[:, 0:AH], mx[:, 0:AH], sink_row, ALU.max))
                own.wait()
                own(dve.tensor_scalar(nmx[:, 0:AH], mx[:, 0:AH], -1.0, None, ALU.mult))
                own(dve.tensor_tensor(sinkx, sink_row, mx[:, 0:AH], ALU.subtract))
                own.wait()
                dve.nop().then_inc(smax_ready, 1)
                dve.wait_ge(sink_exp, n + 1)
                dve.wait_ge(p_ready, AH * (n + 1))
                own(dve.tensor_tensor(den[:, 0:AH], den[:, 0:AH], sinkx, ALU.add))
                own.wait()
                own(dve.reciprocal(mx[:, 8:16], den[:, 0:AH]))
                for hp in range(4):
                    own(dve.tensor_copy(pT[:, 4 * hp:4 * hp + 4, :].rearrange("p a k -> p (a k)"), full("attn", 9 * n + 4 + hp)))
                    own.wait()
                    drained("attn", 9 * n + 4 + hp, dve.nop())
                    dve.nop().then_inc(pT_ready, 1)
                o = full("attn", 9 * n + 8).rearrange("p (h d) -> p h d", d=AD)
                own(dve.tensor_tensor(attn_tok[:, n, :].rearrange("p (h d) -> p h d", d=AD), o,
                                      mx[:, 8:16].unsqueeze(2).to_broadcast([P, AH, AD]), ALU.mult))
                own.wait()
                drained("attn", 9 * n + 8, dve.nop())
            dve.nop().then_inc(pv_done, 1)

            for c in range(2):
                o = full("sguw", c).rearrange("p (g i) -> p g i", g=4)
                own(dve.tensor_tensor(sgu_wT[:, 4 * c:4 * c + 4, :], o, cst("causalT").unsqueeze(1).to_broadcast([P, 4, P]), ALU.mult))
                own.wait()
                drained("sguw", c, dve.nop())
                dve.nop().then_inc(sguwT_ready, 1)
            for gp in range(4):
                o = full("sgu", gp).rearrange("p (a c d) -> p a c d", a=2, c=MT)
                for c in range(2):
                    g = 2 * gp + c
                    u = u_tok[:, :, g * AD:(g + 1) * AD]
                    own(dve.scalar_tensor_tensor(out=u, in0=o[:, c], scalar=sgub[:, g:g + 1], in1=u, op0=ALU.add, op1=ALU.mult))
                own.wait()
                drained("sgu", gp, dve.nop())
            mean_squares([attn_tok[:, m, :] for m in range(MT)] + [u_tok[:, m, :] for m in range(MT)], st_ms, sq_junk[:, 0, :])
            reciprocals(7, 2 * MT)
            dve.wait_ge(actT_ready, KT)
            for m in range(MT):
                own(dve.tensor_scalar(n_tok[:, m, 0:512], attn_tok[:, m, :], st_r[:, m:m + 1], None, ALU.mult))
                own.wait()
                dve.tensor_scalar(n_tok[:, m, 512:], u_tok[:, m, :], st_r[:, MT + m:MT + m + 1], None, ALU.mult).then_inc(row_ready, 1)

            def add_out(stage):
                for k in range(8):
                    v = x[:, k % MT, (k // MT) * 512:(k // MT + 1) * 512]
                    o = full(stage, k)
                    if k % MT == MT - 1:
                        release(stage, k // MT)
                    own(dve.tensor_tensor(v, o, v, ALU.add))
                    own.wait()
                    drained(stage, k, dve.nop())
                dve.nop().then_inc(x_ready, 1)

            add_out("out2")

            dve.wait_ge(mem_in, 48)
            mean_squares([mem[:, m, :] for m in range(MM)], st_ms, x_sq)
            reciprocals(8, MM)
            for m in range(MM):
                own(dve.tensor_scalar(mem[:, m, :], mem[:, m, :], st_r[:, m:m + 1], None, ALU.mult))
                own.wait()
                dve.nop().then_inc(vc_ready, 1)
            dve.wait_ge(xkv_ready, 4)
            for m in range(MM):
                head_squares(xk_tok[:, m, :], XH, XD, st_ms[:, XH * m:XH * (m + 1)], x_sq)
            dve.nop().then_inc(ms_ready, 1)
            reciprocals(9, MM * XH)
            head_scale(xk_tok.rearrange("p m (h d) -> p (m h) d", d=XD), MM * XH, XD)
            head_gain(xk_tok.rearrange("p m (h d) -> p (m h) d", d=XD), MM * XH, ckn_row, 1.0, XD)
            dve.nop().then_inc(xk_ready, 1)
            norm_rows(10, n_tok, vc_ready, x_sq)
            dve.wait_ge(xq_in, 8)
            for m in range(MT):
                head_squares(xq_tok[:, m, :], XH, XD, st_ms[:, XH * m:XH * (m + 1)], x_sq)
            dve.nop().then_inc(ms_ready, 1)
            reciprocals(11, MT * XH)
            head_scale(xq_tok.rearrange("p m (h d) -> p (m h) d", d=XD), MT * XH, XD)
            head_gain(xq_tok.rearrange("p m (h d) -> p (m h) d", d=XD), MT * XH, cqn_row, XD ** -0.5, XD)
            for m in range(MT):
                dve.nop().then_inc(xq_ready, 1)
            for m in range(MT):
                for hp in range(2):
                    hd = m * XH + 2 * hp
                    o = full("xs", 2 * m + hp).rearrange("p (a k) -> p a k", a=2)
                    own(dve.tensor_reduce(mx[:, hd:hd + 2], o, AX.X, ALU.max))
                    own.wait()
                    own(dve.tensor_scalar(nmx[:, hd:hd + 2], mx[:, hd:hd + 2], -1.0, None, ALU.mult))
                    own.wait()
                    dve.nop().then_inc(xmax_ready, 1)
            for m in range(MT):
                dve.wait_ge(xq_in, 8 + m + 1)
                own(dve.reciprocal(mx[:, m * XH:(m + 1) * XH], den[:, m * XH:(m + 1) * XH]))
                own.wait()
                for hd in range(XH):
                    v = xp_tok[:, m, hd, :]
                    dve.tensor_scalar(v, v, mx[:, m * XH + hd:m * XH + hd + 1], None, ALU.mult).then_inc(xp_ready, 1)
            add_out("xout")

            dve.wait_ge(ffn_in, 16 * (2 + GROUPS))
            own(dve.memset(lg[:, :, GROUPS:8], -3.0e38))
            norm_rows(12, h3_tok, row_ready, xg, gain=ffn_row)
            o = full("route", 0)[:, 0:MT * (GROUPS + EXPERTS)].rearrange("p (m e) -> p m e", m=MT)
            own(dve.tensor_copy(lg[:, :, 0:GROUPS], o[:, :, 0:GROUPS]))
            own(dve.tensor_copy(lg[:, :, 8:], o[:, :, GROUPS:]))
            own.wait()
            drained("route", 0, dve.nop())
            for m in range(MT):
                own(dve.max(top[:, m, :], lg[:, m, 0:8]))
                own.wait()
                own(dve.max_index(top_i[:, m, :], top[:, m, :], lg[:, m, 0:8]))
                own.wait()
                own(dve.tensor_copy(gidx[:, m:m + 1], top_i[:, m, 0:1]))
                own(dve.tensor_scalar(gexp[:, 4 * m:4 * m + 4], lg[:, m, 0:GROUPS], top[:, m, 0:1], None, ALU.subtract))
                own.wait()
                own(dve.tensor_scalar(goh[:, 4 * m:4 * m + 4], cst("iota")[:, 0:GROUPS], gidx[:, m:m + 1], None, ALU.is_equal))
            own.wait()
            dve.nop().then_inc(gexp_in, 1)
            for g in range(GROUPS):
                for m in range(MT):
                    src, sel = lg[:, m, 8 + 8 * g:16 + 8 * g], goh[:, 4 * m + g:4 * m + g + 1]
                    if g == 0:
                        own(dve.tensor_scalar(loc[:, m, :], src, sel, None, ALU.mult))
                    else:
                        own(dve.scalar_tensor_tensor(out=loc[:, m, :], in0=src, scalar=sel, in1=loc[:, m, :],
                                                     op0=ALU.mult, op1=ALU.add))
                own.wait()
            for m in range(MT):
                own(dve.max(top[:, m, :], loc[:, m, :]))
            own.wait()
            for m in range(MT):
                own(dve.max_index(top_i[:, m, :], top[:, m, :], loc[:, m, :]))
            own(dve.tensor_tensor(dl, top[:, :, 1], top[:, :, 0], ALU.subtract))
            own.wait()
            dve.nop().then_inc(texp_in, 1)
            for q in range(2):
                own(dve.tensor_copy(eid[:, q * MT:(q + 1) * MT], top_i[:, :, q]))
            own.wait()
            for q in range(2):
                own(dve.scalar_tensor_tensor(out=eid[:, q * MT:(q + 1) * MT], in0=gidx, scalar=float(PER_GROUP),
                                             in1=eid[:, q * MT:(q + 1) * MT], op0=ALU.mult, op1=ALU.add))
            own.wait()
            for c in range(2 * MT):
                own(dve.tensor_scalar(oh[:, c, :], cst("iota")[:, 0:EXPERTS], eid[:, c:c + 1], None, ALU.is_equal))
            own.wait()
            for m in range(MT):
                dve.tensor_tensor(ohs[:, m, :], oh[:, m, :], oh[:, MT + m, :], ALU.add).then_inc(oh_ready, 1)
            dve.wait_ge(gexp_ready, 1)
            own(dve.tensor_reduce(gsum, gexp.rearrange("p (m g) -> p m g", g=GROUPS), AX.X, ALU.add))
            dve.wait_ge(texp_ready, 1)
            own(dve.tensor_scalar(tden, dl, 1.0, None, ALU.add))
            own.wait()
            own(dve.tensor_tensor(tden, tden, gsum, ALU.mult))
            own.wait()
            own(dve.reciprocal(w01[:, 0:MT], tden))
            own.wait()
            own(dve.tensor_tensor(w01[:, MT:], w01[:, 0:MT], dl, ALU.mult))
            o = full("route", 1)
            own(dve.tensor_copy(ranks.rearrange("p m e -> p (m e)"), o[:, 0:MT * EXPERTS]))
            own(dve.tensor_copy(cnt, o[:, MT * EXPERTS:(MT + 1) * EXPERTS]))
            own.wait()
            drained("route", 1, dve.nop())
            own(dve.tensor_scalar(nblk, cnt, 0.0, None, ALU.is_gt))
            own.wait()
            for j in range(1, S // SLOTS):
                own(dve.scalar_tensor_tensor(out=nblk, in0=cnt, scalar=float(j * SLOTS), in1=nblk, op0=ALU.is_gt, op1=ALU.add))
                own.wait()
            own(dve.tensor_tensor_scan(incl, cst("ones")[:, 0:EXPERTS], nblk, 0.0, ALU.mult, ALU.add))
            own.wait()
            own(dve.tensor_tensor(bstart, incl, nblk, ALU.subtract))
            own(dve.tensor_scalar(n_steps[:, :], incl[0:1, EXPERTS - 1:EXPERTS], 1.0, None, ALU.add))
            own(dve.tensor_scalar(e_tmp[:, 0, :], incl, cst("token")[:, 0:1], 0.0, ALU.is_le, ALU.add, accum_out=plan_col))
            own.wait()
            own(dve.tensor_scalar(plan_col, plan_col, float(EXPERTS - 1), None, ALU.min))
            own.wait()
            dve.nop().then_inc(plan_col_ready, 1)
            dve.nop().then_inc(plan_ready, 1)
            for m in range(MT):
                own(dve.scalar_tensor_tensor(out=place_e[:, m, :], in0=bstart, scalar=float(SLOTS), in1=ranks[:, m, :],
                                             op0=ALU.mult, op1=ALU.add))
            own.wait()
            for q in range(2):
                own(dve.tensor_tensor(e_tmp[:, q * MT:(q + 1) * MT, :], oh[:, q * MT:(q + 1) * MT, :], place_e, ALU.mult))
            own.wait()
            own(dve.tensor_reduce(destf, e_tmp, AX.X, ALU.add))
            own.wait()
            own(dve.tensor_copy(dest_i[:, 0, :], destf))
            own(dve.tensor_scalar(dest_i[:, 3, :], destf, float(2 * SLOTS), None, ALU.add))
            own.wait()
            own(dve.tensor_scalar(dest_i[:, 1, :], dest_i[:, 0, :], SLOTS.bit_length() - 1, None, ALU.logical_shift_right))
            own(dve.tensor_scalar(dest_i[:, 2, :], dest_i[:, 0, :], SLOTS - 1, None, ALU.bitwise_and))
            own.wait()
            own(dve.tensor_copy(blkf, dest_i[:, 1, :]))
            own(dve.tensor_copy(inf_, dest_i[:, 2, :]))
            own.wait()
            for c in range(2 * MT):
                own(dve.tensor_scalar(slot_oh[:, c, :], cst("iota")[:, 0:SLOTS], inf_[:, c:c + 1], None, ALU.is_equal))
                own(dve.tensor_scalar(block_oh[:, c, :], cst("iota"), blkf[:, c:c + 1],
                                      cst("token")[:, c % MT:c % MT + 1], ALU.is_equal, ALU.mult))
            own.wait()
            dve.nop().then_inc(slot_oh_ready, 1)
            own(dve.memset(plan_row[:, 0:1], 0))
            own(dve.tensor_copy(plan_row[:, 1:], full("route", 2)[0:1, 0:P]))
            own.wait()
            drained("route", 2, dve.nop())
            dve.nop().then_inc(plan_ready, 1)
            own(dve.tensor_copy(slot_tok[:, :], full("route", 3)[0:SLOTS, 0:64]))
            own.wait()
            drained("route", 3, dve.nop())
            dve.nop().then_inc(slots_ready, 1)

            steps = dve.snap(dve.value_load(n_steps[0:1, 0:1], min_val=2, max_val=MAX_BLOCKS + 1))
            moe = Chain(dve, dve_moe)

            def low(n, b):
                dve.wait_ge(piece_hi, b * 12 + (n + 1))
                dve.tensor_tensor(parts[:, n % 4, 1, :], ring[:, n // 4, n % 4 * 1024:(n % 4 + 1) * 1024],
                                  parts[:, n % 4, 0, :].bitcast(F32), ALU.subtract).then_inc(piece_split[n], 1)

            def rest(stage, k, dst, o, i=0):
                n = dst.shape[2] * dst.shape[3]
                d = [dst[:, h].rearrange("p t n -> p (t n)") for h in range(2)]
                drained(stage, k, dve.tensor_tensor(d[1], o[:, 0:n], d[0].bitcast(F32), ALU.subtract))

            for n in range(12):
                dve.nop().then_inc(piece_split[n], 1)
            dve.wait_ge(xgT_hi, 1)
            rest("moe0", 0, xgT, full("moe0", 0))
            with dve.Fori(0, steps) as b:
                moe.enter(b, 2)
                for n in (0, 1, 2):
                    low(n, b)
                dve.wait_ge(hidT_hi, b + 1)
                rest("moe", 3, hidT, ps[:, banks["moe"].place(3), :])
                for n in (4, 5, 6):
                    low(n, b)
                dve.wait_ge(sg_h_ready, b + 1)
                moe(dve.tensor_tensor(t_h[0:SLOTS, :], full("moe", 1, b)[0:SLOTS, :], sg_h[0:SLOTS, :], ALU.mult))
                moe.wait()
                drained("moe", 1, dve.nop())
                for n in (8, 9, 10):
                    low(n, b)
                moe(dve.tensor_tensor(hid[0:SLOTS, :], full("moe", 2, b)[0:SLOTS, :], t_h[0:SLOTS, :], ALU.mult))
                moe.wait()
                drained("moe", 2, dve.nop())
                dve.nop().then_inc(hid_ready, 1)
                o = full("moe", 0, b)
                dve.wait_ge(xgT_hi, b + 2)
                rest("moe", 0, xgT, o, b)
            moe.leave(None)
            for c in range(2 * MT):
                q, m = c % 2, c // 2
                dve.wait_ge(combo_in[c % 4], 16 * (c // 4 + 1))
                if q:
                    dve.wait_ge(combo_used, c)
                ins = dve.scalar_tensor_tensor(out=x[:, m, :], in0=combo[:, c % 4, :], scalar=w01[:, q * MT + m:q * MT + m + 1],
                                               in1=x[:, m, :], op0=ALU.mult, op1=ALU.add)
                ins.then_inc(combo_used, 1)
                if q:
                    dve.wait_ge(combo_used, c + 1)
                    dve.nop().then_inc(x_ready, 1)

        @block.gpsimd
        def _(pool):
            pool.wait_ge(x_ready, 3)
            pool.memset(combo[:, 0, :], 0.0).then_inc(zero_ready, 1)
            pool.wait_ge(h3_stored, 16)
            pool.wait_ge(slots_ready, 1)
            steps = pool.snap(pool.value_load(n_steps[0:1, 0:1], min_val=2, max_val=MAX_BLOCKS + 1))

            def gather(b):
                pool.tensor_copy(idx[:, :], slot_tok[:, bass.ds(b, 1)]).then_inc(idx_ready, 1)
                pool.wait_ge(idx_ready, b + 1)
                pool.nop().then_inc(idx_settled, 1)
                pool.indirect_dma_start(xg[0:SLOTS, :], None, h3_rows,
                                        bass.IndirectOffsetOnAxis(ap=idx[:, 0:1], axis=0)).then_inc(xg_in, 16)

            gather(0)
            with pool.Fori(0, steps) as b:
                st = banks["moe"]
                pool.wait_ge(bank_filled[st.place(0)], st.before(0, b))
                gather(b + 1)
                for n in (3, 7, 11):
                    pool.wait_ge(piece_hi, b * 12 + (n + 1))
                    pool.tensor_tensor(parts[:, n % 4, 1, :], ring[:, n // 4, n % 4 * 1024:(n % 4 + 1) * 1024],
                                       parts[:, n % 4, 0, :].bitcast(F32), ALU.subtract).then_inc(piece_split[n], 1)
            pool.wait_ge(y_blk_ready, 1)
            for c in range(2 * MT):
                q, m = c % 2, c // 2
                if c >= 4:
                    pool.wait_ge(combo_used, c - 3)
                pool.indirect_dma_start(combo[:, c % 4, :], None, y_rows, bass.IndirectOffsetOnAxis(
                    ap=dest_i[:, 3, q * MT + m:q * MT + m + 1].bitcast(U32), axis=0)).then_inc(combo_in[c % 4], 16)


_INS = ["x", "c", "positions", "w_ada", "b_ada", "pre_norm_g", "w_in", "conv_w", "conv_b", "conv_ln_g", "conv_ln_b",
        "w_ret_out", "w_conv_out", "w_out", "post_norm_g", "mem_2", "norm_mix_2", "w_in_2", "q_norm_2", "k_norm_2",
        "attn_sinks_2", "sgu_norm_2", "sgu_w_2", "sgu_b_2", "out_norm_attn_2", "out_norm_sgu_2", "w_out_2",
        "norm_cross_2", "norm_mem_2", "w_cq_2", "w_ck_2", "w_cv_2", "cq_norm_2", "ck_norm_2", "w_co_2", "norm_ffn_2",
        "w_router_group_2", "w_router_expert_2", "w1_2", "w3_2", "w2_2"]


def kernel(**inputs):
    import concourse.bacc as _bacc
    from concourse.bass_utils import run_bass_kernel_spmd as _run

    nc = _bacc.Bacc("TRN2", target_bir_lowering=False, num_devices=1)
    arrays = {name: np.ascontiguousarray(inputs[name]) for name in _INS}
    arrays["const"], arrays["decay"] = const_table(), decay_table()
    args = {name: nc.dram_tensor(f"in_{name}", v.shape, mybir.dt.from_np(v.dtype), kind="ExternalInput").ap()
            for name, v in arrays.items()}
    out = nc.dram_tensor("out_0", (1, S, D), F32, kind="ExternalOutput").ap()
    build(nc, args, out)
    r = _run(nc, [{f"in_{k}": v for k, v in arrays.items()}], core_ids=[0])
    return r.results[0]["out_0"]
```

```python
from contextlib import ExitStack

import concourse.bass as bass
import numpy as np
from concourse import mybir

P = 128
S = 512
D = 1024
MT = S // P
KT = D // P
HEADS, HQK, HV = 4, 256, 512
TAPS = 31
WIN_COLS = (1024, 1024, 2048, 2048, 1024, 1024, 1024, 1024, 1024)
OFF_Q, OFF_K, OFF_V, OFF_Z, OFF_UV, OFF_UG, OFF_ZC, OFF_GA, OFF_GB = [
    sum(WIN_COLS[:n]) for n in range(len(WIN_COLS))]
MEM, MM = 256, 2
AH, AD = 8, 64
XH, XD = 4, 256
GROUPS, PER_GROUP = 4, 8
EXPERTS, FF = GROUPS * PER_GROUP, 512
SLOTS = 64
MAX_BLOCKS = (2 * S - EXPERTS) // SLOTS + EXPERTS + 1
RMS_EPS, GN_EPS, LN_EPS = 1e-6, 1e-5, 1e-5
NEG = -1e30
ARENA = 21740

F32 = mybir.dt.float32
F32R = mybir.dt.float32r
BF16 = mybir.dt.bfloat16
I32 = mybir.dt.int32
U32 = mybir.dt.uint32
ACT = mybir.ActivationFunctionType
ALU = mybir.AluOpType
AX = mybir.AxisListType

CONSTS = {}


def const_table():
    p = np.arange(P)
    inv_freq = (np.float32(10000.0) ** (-np.arange(HQK // 2, dtype=np.float32) / np.float32(HQK // 2)))
    dist = p[:, None] + P - np.arange(2 * P)[None, :]
    band = np.where((dist >= 0) & (dist < P), 0.0, NEG)
    first = np.where(np.arange(2 * P)[None, :] >= P, band, NEG)
    parts = [
        ("ident", np.eye(P)),
        ("before", (p[:, None] < p[None, :])),
        ("causalT", (p[:, None] <= p[None, :])),
        ("ones", np.ones((P, P))),
        ("mean", np.full((P, P), 1.0 / D)),
        ("iota", np.broadcast_to(np.arange(64), (P, 64))),
        ("token", p[:, None] + P * np.arange(MT)[None, :]),
        ("band", band),
        ("first", first),
        ("freq", inv_freq[:, None]),
    ]
    at = 0
    for name, a in parts:
        CONSTS[name] = (at, at + a.shape[1])
        at += a.shape[1]
    return np.concatenate([np.asarray(a, np.float32) for _, a in parts], axis=1)


def decay_table():
    log_g = np.log1p(-np.exp2(-5.0 - np.arange(HEADS)))
    diff = np.arange(S)[None, :] - np.arange(P)[:, None]
    d = np.where(diff >= 0, np.exp(log_g[:, None, None] * np.maximum(diff, 0)), 0.0)
    return (d * HQK ** -0.5).astype(np.float32)


const_table()


class Stage:

    def __init__(self, base, uses):
        self.base = list(base)
        self.places = [k % len(base) for k in range(uses)] if isinstance(uses, int) else list(uses)
        self.per = [self.places.count(b) for b in range(len(base))]

    def place(self, k):
        return self.places[k]

    def before(self, k, i=0):
        b = self.places[k]
        return i * self.per[b] + (self.base[b] + self.places[:k].count(b))


def stages(n, plan):
    base, out = [0] * n, {}
    for name, uses, steps in plan:
        out[name] = st = Stage(base, uses)
        base = [b + steps * p for b, p in zip(base, st.per)]
    return out


class Chain:

    def __init__(self, eng, sem):
        self.eng, self.sem, self.base, self.count = eng, sem, 0, 0

    def __call__(self, instruction):
        instruction.then_inc(self.sem, 1)
        self.count += 1

    def wait(self, but=0):
        self.eng.wait_ge(self.sem, self.base + (self.count - but))

    def enter(self, i, per):
        self.at, self.per = self.base + self.count, per
        self.base, self.count = i * per + self.at, 0

    def leave(self, steps):
        assert self.count == self.per, (self.count, self.per)
        self.base, self.count = (self.at + self.per * steps, 0) if steps else (None, 0)


BANK_PLAN = [
    ("ada", 6, 1), ("columns", 1, 1), ("hT", KT, 1), ("conv", 5, KT), ("ln", 2, 1),
    ("qk0", 4, 1), ("heads", 24, HEADS - 1), ("head_last", 20, 1), ("mix", 2, KT), ("out", 8, 1),
    ("h2T", KT, 1), ("in2", 16, 1), ("qkT", 5, 1), ("attn", MT * 9, 1), ("sguw", 2, 1), ("sgu", 4, 1),
    ("mixT", KT, 1), ("out2", 8, 1),
    ("memT", 4, 1), ("xk", 4, 1), ("xv", 4, 1), ("hqT", KT, 1), ("xkT", 4, 1), ("xq", 8, 1), ("xqT", KT, 1),
    ("xs", 8, 1), ("xpT", 8, 1), ("xo", 8, 1), ("xout", 8, 1),
    ("h3T", KT, 1), ("route", 4, 1), ("moe0", (0, 3, 4, 5), 1), ("moe", 6, 1),
]
CHUNK_PLAN = [
    ("ada", 6, 1), ("conv", 3, KT), ("qk0", 1, 1), ("heads", (1, 2, 0), HEADS - 1), ("head_last", (1, 2), 1),
    ("mix", 3, KT), ("out", 2, 1), ("in2", 4, 1),
    ("out2", 2, 1), ("xk", 2, 1), ("xv", 2, 1), ("xq", 2, 1), ("xout", 2, 1), ("moe", 3, 1),
]
PIECE_PLAN = [
    ("conv", (0, 1, 2, 3, 1), KT), ("qk0", 4, 1), ("heads", 12, HEADS - 1), ("head_last", 8, 1), ("in2", 14, 1), ("out2", 8, 1), ("xq", 8, 1),
    ("xout", 8, 1), ("moe", 12, 1),
]
BLOCK2_COLS = 5


def build(nc, a, out):
    banks, chunks, pieces = stages(7, BANK_PLAN), stages(3, CHUNK_PLAN), stages(4, PIECE_PLAN)
    ctx = ExitStack()
    with ctx:
        def sb(name, shape, dt=F32):
            return ctx.enter_context(nc.sbuf_tensor(name, shape, dt))

        def sem(name):
            return ctx.enter_context(nc.semaphore(name))

        ring = sb("ring", [P, 3, 4096])
        const = sb("const", [P, CONSTS["freq"][1]])
        cols = sb("cols", [P, KT, TAPS + 3 + 4])
        sgub = sb("sgub", [P, 8])
        act_parts = sb("act_parts", [P, 2 * KT * S], F32R)
        actT = act_parts[:, :].rearrange("p (h t n) -> p h t n", h=2, t=KT)
        xgT = act_parts[:, 0:2 * KT * SLOTS].rearrange("p (h t n) -> p h t n", h=2, t=KT)
        hidT = act_parts[:, 2 * KT * SLOTS:2 * (KT + 4) * SLOTS].rearrange("p (h t n) -> p h t n", h=2, t=4)
        parts = sb("parts", [P, 4, 2, 1024], F32R)
        small = sb("small", [P, 512])
        arena = sb("arena", [P, ARENA])

        def cst(name, parts=P):
            lo, hi = CONSTS[name]
            return const[0:parts, lo:hi]

        ident = cst("ident")
        taken = [0]

        def carve(shape, at=None):
            n = int(np.prod(shape))
            lo = taken[0] if at is None else at
            assert lo + n <= ARENA, (lo, n)
            if at is None:
                taken[0] = lo + n
            v = arena[:, lo:lo + n]
            if len(shape) == 2:
                v = v.rearrange("p (a b) -> p a b", a=shape[0])
            if len(shape) == 3:
                v = v.rearrange("p (a b c) -> p a b c", a=shape[0], b=shape[1])
            return v

        def mini(lo, n):
            return small[:, lo:lo + n]

        gate_post = carve([D])
        cosT, sinT = carve([S]), carve([S])
        convT = carve([KT, S])
        zconvT = carve([KT, S])
        first_free = taken[0]
        taken[0] = D + 2 * S
        colrows = carve([D])[0:TAPS + 3 + 4, :]
        sgub_rows = carve([P])[0:8, :]
        pos_i = carve([S]).bitcast(I32)
        x0 = carve([MT, D])
        h0 = carve([MT, D])
        mod_scale, mod_shift = carve([D]), carve([D])
        pre_g, post_g = carve([D]), carve([D])
        c_rep = carve([KT, P])
        bada = carve([3 * D])
        angle, turns = carve([S]), carve([S])
        taken[0] = first_free
        apad = carve([TAPS - 1 + S])
        conv_acc = carve([2, S])
        sig_u, sig_z = carve([S]), carve([S])
        ln_sq = carve([2, S])
        ln_rstd, ln_std = carve([S]), carve([S])
        ln_y = carve([2, S])
        ln_s = carve([2, S])
        sig_g = carve([2, S])
        taken[0] = first_free - 2 * KT * S
        retT = carve([16, S])
        qk_rot = carve([4, S])
        v_tok = carve([MT, HV])
        z_tok = carve([MT, HV])
        decayed = carve([MT, S])
        rot = decayed
        sig_r = carve([2, S])
        norm_o = sig_r
        decay = carve([S])
        zeros = carve([D])
        taken[0] = first_free
        conv_backT = carve([KT, S])
        mergedT = carve([KT, S])
        part_a, part_b = carve([S]), carve([S])
        sig_ab = carve([2, S], at=D)
        x = carve([MT, D], at=ARENA - MT * D)
        y_tok = carve([MT, D], at=first_free)
        x0_early = carve([D], at=MT * D)
        squares = carve([D], at=MT * D + D)
        OUT_TILES = (1, 2, 3, 0)

        taken[0] = 0
        n_tok = carve([MT, D])
        sq_junk = carve([MT, 512])
        q_tok = carve([MT, 512])
        kv_tok = carve([MT, 256])
        u_tok = carve([MT, 512])
        g_tok = carve([MT, 512])
        attn_tok = carve([MT, 512])
        q_pair = attn_tok
        second_free = taken[0]
        qT = carve([4, S])
        kT = carve([P + S], at=2 * D)
        s_tok = [carve([AH, 2 * P], at=MT * D), carve([AH, 2 * P], at=0)]
        pT = carve([2 * AH, P], at=MT * D + MT * 512)
        sgu_w = carve([8, P], at=second_free)
        sgu_wT = carve([8, P], at=second_free + 8 * P)
        gain_rows = carve([AD + AD + 512 + 8], at=2 * D + P + S)
        qn_row, kn_row = gain_rows[:, 0:AD], gain_rows[:, AD:2 * AD]
        sgun_row, sink_row = gain_rows[:, 2 * AD:2 * AD + 512], gain_rows[:, 2 * AD + 512:]
        assert second_free + 4 * S <= ARENA - MT * D
        taken[0] = MT * D
        mem = carve([MM, D])
        memT = carve([KT, MEM])
        xv_tok = carve([MM, D])
        xk_tok = carve([MM, D])
        xkT = carve([KT, MEM])
        cqn_row, ckn_row = carve([XD]), carve([XD])
        x_sq = carve([D])
        assert taken[0] <= ARENA - MT * D
        xq_tok = carve([MT, D], at=MT * D)
        xqT = carve([KT, S], at=0)
        xp_tok = carve([MT, XH, MEM], at=MT * D)
        xpT = carve([KT, S], at=MT * D + 6 * D)
        h3_tok = carve([MT, D], at=0)
        taken[0] = MT * D
        ffn_row = carve([D])
        wr = carve([KT, GROUPS + EXPERTS])
        lg = carve([MT, 40])
        oh = carve([2 * MT, EXPERTS])
        ohs = carve([MT, EXPERTS])
        loc = carve([MT, 8])
        top = carve([MT, 8])
        ranks = carve([MT, EXPERTS])
        place_e = carve([MT, EXPERTS])
        e_tmp = carve([2 * MT, EXPERTS])
        slot_oh = carve([2 * MT, SLOTS])
        block_oh = carve([2 * MT, 64])
        expert_free = taken[0]
        h3T = carve([KT, S], at=expert_free)
        xg = carve([D])
        sg_h, t_h, hid = carve([FF]), carve([FF]), carve([FF])
        y_blk = carve([D])
        taken[0] = expert_free + KT * S
        combo = carve([4, D])
        assert taken[0] <= ARENA - MT * D
        top_i = sb("top_i", [P, MT, 8], U32)
        dest_i = sb("dest_i", [P, 4, 2 * MT], I32)
        mark_src = sb("mark_src", [P, P], BF16)
        slot_tok = sb("slot_tok", [SLOTS, 64], U32)
        idx = sb("idx", [SLOTS, 1], U32)
        plan_row = sb("plan_row", [1, 1 + P], I32)
        n_steps = sb("n_steps", [1, 1], I32)
        conv_dram = nc.dram_tensor("conv_dram", [P, KT, S], F32).ap()
        gates_dram = nc.dram_tensor("gates_dram", [KT, P, 2, S], F32).ap()
        h3_rows = nc.dram_tensor("h3_rows", [S, D], F32).ap()
        y_rows = nc.dram_tensor("y_rows", [(MAX_BLOCKS + 2) * SLOTS, D], F32).ap()

        ps = ctx.enter_context(nc.psum_tensor("ps", [P, 8, 512], F32))

        bank_filled = [sem(f"bank{b}_filled") for b in range(7)]
        bank_drained = [sem(f"bank{b}_drained") for b in range(7)]
        weights_landed = [sem(f"weights{s}_landed") for s in range(3)]
        weights_used = [sem(f"weights{s}_used") for s in range(3)]
        const_in, cols_in, x_in, c_in, pos_in, rows_in = (sem(n) for n in (
            "const_in", "cols_in", "x_in", "c_in", "pos_in", "rows_in"))
        c_rep_ready, h0_ready = sem("c_rep_ready"), sem("h0_ready")
        act_own, dve_own, dve_moe = (sem(n) for n in ("act_own", "dve_own", "dve_moe"))
        sig_u_ready, sig_z_ready = sem("sig_u_ready"), sem("sig_z_ready")
        angles_ready, rotary_ready = sem("angles_ready"), sem("rotary_ready")
        conv_ready, sq_ready, sq_used, cen_ready = (sem(n) for n in (
            "conv_ready", "ln_sq_ready", "ln_sq_used", "centred"))
        ln_std_ready, ln_y_ready, ln_s_ready, gated_conv_ready = (sem(n) for n in (
            "ln_std_ready", "ln_y_ready", "ln_s_ready", "gated_conv_ready"))
        decay_in, decay_used = sem("decay_in"), sem("decay_used")
        qk_ready, v_ready, sig_r_ready, sig_r_used = (sem(n) for n in (
            "qk_ready", "v_ready", "sig_r_ready", "sig_r_used"))
        decayed_ready, var_ready, std_ready, ret_ready, retT_ready = (sem(n) for n in (
            "decayed_ready", "var_ready", "std_ready", "ret_ready", "retT_ready"))
        gates_stored, gates_in, gates_used, merged_ready = (sem(n) for n in (
            "gates_stored", "gates_in", "gates_used", "merged_ready"))
        y_ready, ms_ready, rms_ready, x_ready = (sem(n) for n in ("y_ready", "ms_ready", "rms_ready", "x_ready"))
        x_back, gains_in = sem("x_back"), sem("gains_in")
        row_ready, in2_ready, qk2_ready, qkT_ready = (sem(n) for n in (
            "rows_ready", "in2_ready", "qk2_ready", "qkT_ready"))
        smax_ready, p_ready, pT_ready, pv_done = (sem(n) for n in ("smax_ready", "p_ready", "pT_ready", "pv_done"))
        sguw_in, sguwT_ready, vc_ready, actT_ready = (sem(n) for n in (
            "sguw_in", "sguwT_ready", "vc_ready", "actT_ready"))
        mem_in, memT_ready, xkv_ready, xk_ready, xkT_ready = (sem(n) for n in (
            "mem_in", "memT_ready", "xkv_ready", "xk_ready", "xkT_ready"))
        xq_in, xq_ready, xqT_ready, xmax_ready, sink_exp, xp_ready, xpT_ready = (sem(n) for n in (
            "xq_in", "xq_ready", "xqT_ready", "xmax_ready", "sink_exp", "xp_ready", "xpT_ready"))
        ffn_in, h3_stored, gexp_in, gexp_ready, texp_in, texp_ready = (sem(n) for n in (
            "ffn_in", "h3_stored", "gexp_in", "gexp_ready", "texp_in", "texp_ready"))
        oh_ready, plan_col_ready, slot_oh_ready, plan_ready, slots_ready = (sem(n) for n in (
            "oh_ready", "plan_col_ready", "slot_oh_ready", "plan_ready", "slots_ready"))
        idx_ready, xg_in, xgT_hi, sg_h_ready, hid_ready, hidT_hi, y_blk_ready, y_stored = (sem(n) for n in (
            "idx_ready", "xg_in", "xgT_hi_ready", "sg_h_ready", "hid_ready", "hidT_hi_ready", "y_blk_ready", "y_stored"))
        half_landed = [sem(f"expert_half{n}_landed") for n in range(6)]
        piece_hi = sem("piece_hi_ready")
        piece_split = [sem(f"piece{n}_split") for n in range(12)]
        piece_used = [sem(f"parts{n}_used") for n in range(4)]
        dense_split = [sem(f"dense_piece{n}_split") for n in range(4)]
        pool_own, actT_hi, h3T_ready = sem("pool_own"), sem("actT_hi_ready"), sem("h3T_ready")
        conv_stored, conv_back = sem("conv_stored"), sem("conv_back")
        combo_in = [sem(f"combo{n}_in") for n in range(4)]
        stats_settled, turn_may_start, idx_settled = (sem(n) for n in ("stats_settled", "turn_may_start", "idx_settled"))
        zero_ready, y_cleared = sem("zero_ready"), sem("y_cleared")
        combo_used, out_done = sem("combo_used"), sem("out_done")

        st_ms, st_rms, st_r = mini(0, 32), mini(32, 32), mini(64, 32)
        bn6, mv, st_std = mini(96, 24), mini(120, 8), mini(128, 4)
        gn_r = mini(132, 4)
        mx, nmx, den = mini(136, 32), mini(168, 32), mini(200, 32)
        eps = mini(240, 3)
        gidx, gsum, gmax = mini(248, 4), mini(252, 4), mini(256, 4)
        gexp, gm8 = mini(260, 16), mini(276, 8)
        goh = mini(284, 16)
        eid, dl, w01, tden = mini(300, 8), mini(308, 4), mini(312, 8), mini(320, 4)
        cnt, nblk, incl, bstart = mini(324, 32), mini(356, 32), mini(388, 32), mini(420, 32)
        destf, blkf, inf_ = mini(452, 8), mini(460, 8), mini(468, 8)
        plan_col = mini(476, 1)
        c_col = mini(480, 8)
        e_one = mini(488, 4)

        def tiles(w):
            return w.rearrange("(t p) n -> p t n", p=P)

        def row(v, n=None):
            return v.rearrange("(o n) -> o n", o=1)

        def score_use(n):
            return 0 if n == 0 else 4 + 9 * (n - 1)

        def weight_use(n):
            return 4 + 9 * n + (4 if n < MT - 1 else 0)

        x_v = a["x"][0].rearrange("(m p) d -> p m d", p=P)
        out_v = out[0].rearrange("(m p) d -> p m d", p=P)
        w_in = tiles(a["w_in"][0])
        w_ada = a["w_ada"][0].rearrange("(p t) n -> p t n", t=KT)

        block = ctx.enter_context(nc.Block())

        @block.sync
        def _(sp):
            def chunk(stage, j, halves, i=0):
                st = chunks[stage]
                s, n = st.place(j), st.before(j, i)
                if not (isinstance(n, int) and n == 0):
                    sp.wait_ge(weights_used[s], n)
                for dst, src in halves(ring[:, s, :]):
                    sp.dma_start(dst, src).then_inc(weights_landed[s], 16)

            def pair(r, src):
                k, n = src.shape[1], src.shape[2]
                v = r[:, 0:k * n].rearrange("p (k n) -> p k n", k=k)
                return [(v[:, 0:k // 2, :], src[:, 0:k // 2, :]), (v[:, k // 2:k, :], src[:, k // 2:k, :])]

            def both(r, one, two):
                k, n = one.shape[1], one.shape[2]
                v = r[:, 0:2 * k * n].rearrange("p (w k n) -> p w k n", w=2, k=k)
                return [(v[:, 0], one), (v[:, 1], two)]

            sp.dma_start(c_col, a["c"][0].rearrange("(p t) -> p t", t=KT)).then_inc(c_in, 16)
            sp.dma_start(const[:, :], a["const"]).then_inc(const_in, 16)
            sp.dma_start(bada[0:1, :], a["b_ada"]).then_inc(c_in, 16)
            sp.dma_start(x0, x_v).then_inc(x_in, 16)
            sp.dma_start(pre_g, a["pre_norm_g"].partition_broadcast(P)).then_inc(rows_in, 16)
            sp.dma_start(post_g, a["post_norm_g"].partition_broadcast(P)).then_inc(rows_in, 16)
            for j in range(3):
                g = (2, 3, 0, 1, 4, 5)[j]
                chunk("ada", j, lambda r: pair(r, w_ada[:, :, g * 512:(g + 1) * 512]))
            sp.dma_start(pos_i[:, :], a["positions"].partition_broadcast(P)).then_inc(pos_in, 16)
            per_feature = [a["conv_w"][0], a["conv_b"], a["conv_ln_g"], a["conv_ln_b"], row(a["norm_mix_2"]),
                           row(a["norm_cross_2"]), row(a["norm_mem_2"])]
            at = 0
            for v in per_feature:
                sp.dma_start(colrows[at:at + v.shape[0], :], v).then_inc(cols_in, 16)
                at += v.shape[0]
            sp.dma_start(colrows[at:at + 1, 0:512], row(a["out_norm_attn_2"])).then_inc(cols_in, 16)
            sp.dma_start(colrows[at:at + 1, 512:], row(a["out_norm_sgu_2"])).then_inc(cols_in, 16)
            sp.dma_start(sgub_rows[:, :], a["sgu_b_2"]).then_inc(cols_in, 16)
            for j in range(3, 6):
                g = (2, 3, 0, 1, 4, 5)[j]
                chunk("ada", j, lambda r: pair(r, w_ada[:, :, g * 512:(g + 1) * 512]))

            with sp.Fori(0, KT) as t:
                def columns(off):
                    return w_in[:, :, bass.ds(off + t * P, P)]
                chunk("conv", 0, lambda r: both(r, columns(OFF_UV), columns(OFF_UG)), t)
                chunk("conv", 1, lambda r: both(r, columns(OFF_GA), columns(OFF_GB)), t)
                chunk("conv", 2, lambda r: pair(r, columns(OFF_ZC)), t)
            def head_qk(stage, j, h, i=0):
                def qk(r):
                    v = r.rearrange("p (k n) -> p k n", k=KT)
                    return [(v[:, :, 0:HQK], w_in[:, :, bass.ds(OFF_Q + h * HQK, HQK)]),
                            (v[:, :, HQK:], w_in[:, :, bass.ds(OFF_K + h * HQK, HQK)])]
                chunk(stage, j, qk, i)

            def head_vz(stage, h, i=0):
                chunk(stage, 0, lambda r: pair(r, w_in[:, :, bass.ds(OFF_V + h * HV, HV)]), i)
                chunk(stage, 1, lambda r: pair(r, w_in[:, :, bass.ds(OFF_Z + h * HV, HV)]), i)
                sp.wait_ge(decay_used, (h + 1) * MT)
                sp.wait_ge(gated_conv_ready, KT)
                sp.dma_start(decay, a["decay"][bass.ds(h, 1), :, :].rearrange("o p n -> p (o n)")).then_inc(decay_in, 16)

            head_qk("qk0", 0, 0)
            with sp.Fori(0, HEADS - 1) as h:
                head_vz("heads", h, h)
                head_qk("heads", 2, h + 1, h)
            head_vz("head_last", HEADS - 1)
            sp.wait_ge(zero_ready, 1)
            sp.dma_start(y_rows.rearrange("(k p) d -> p k d", p=P),
                         zeros.unsqueeze(1).to_broadcast([P, (MAX_BLOCKS + 2) * SLOTS // P, D])).then_inc(y_cleared, 16)
            w_ret, w_conv = tiles(a["w_ret_out"][0]), tiles(a["w_conv_out"][0])
            sp.wait_ge(gates_stored, (KT + 1) * 16)
            with sp.Fori(0, KT) as t:
                for j in range(2):
                    chunk("mix", j, lambda r: pair(r, w_ret[:, j * KT:(j + 1) * KT, bass.ds(t * P, P)]), t)
                chunk("mix", 2, lambda r: pair(r, w_conv[:, :, bass.ds(t * P, P)]), t)
                sp.wait_ge(gates_used, t + 1)
                sp.dma_start(sig_ab, gates_dram[bass.ds(t, 1)].rearrange("o p g n -> p (o g) n")).then_inc(gates_in, 16)

            def project(stage, w, widths=None):
                at = 0
                for j, n in enumerate(widths or [512] * (w.shape[2] // 512)):
                    chunk(stage, j, lambda r: pair(r, w[:, :, at:at + n]))
                    at += n

            project("out", tiles(a["w_out"][0]))
            project("in2", tiles(a["w_in_2"]), (512, 256, 512, 512))
            sp.wait_ge(actT_ready, 2 * KT)
            for dst, v in ((qn_row, "q_norm_2"), (kn_row, "k_norm_2"), (sgun_row, "sgu_norm_2"), (sink_row, "attn_sinks_2")):
                sp.dma_start(dst, row(a[v]).partition_broadcast(P)).then_inc(gains_in, 16)
            project("out2", tiles(a["w_out_2"]))
            sp.wait_ge(pv_done, 1)
            sp.dma_start(sgu_w, a["sgu_w_2"].rearrange("g i j -> i g j")).then_inc(sguw_in, 16)
            sp.wait_ge(actT_ready, 3 * KT)
            sp.dma_start(mem, a["mem_2"][0].rearrange("(m p) d -> p m d", p=P)).then_inc(mem_in, 16)
            for dst, v in ((cqn_row, "cq_norm_2"), (ckn_row, "ck_norm_2")):
                sp.dma_start(dst, row(a[v]).partition_broadcast(P)).then_inc(mem_in, 16)
            for stage, w in (("xk", "w_ck_2"), ("xv", "w_cv_2"), ("xq", "w_cq_2"), ("xout", "w_co_2")):
                project(stage, tiles(a[w]))
            sp.wait_ge(x_ready, 3)
            sp.dma_start(ffn_row, row(a["norm_ffn_2"]).partition_broadcast(P)).then_inc(ffn_in, 16)
            sp.dma_start(wr[:, :, 0:GROUPS], tiles(a["w_router_group_2"])).then_inc(ffn_in, 16)
            for g in range(GROUPS):
                lo = GROUPS + g * PER_GROUP
                sp.dma_start(wr[:, :, lo:lo + PER_GROUP], tiles(a["w_router_expert_2"][g])).then_inc(ffn_in, 16)
            sp.wait_ge(row_ready, 3 * MT)
            sp.dma_start(h3_rows.rearrange("(m p) d -> p m d", p=P), h3_tok).then_inc(h3_stored, 16)

            sp.wait_ge(plan_ready, 2)
            steps = sp.snap(sp.value_load(n_steps[0:1, 0:1], min_val=2, max_val=MAX_BLOCKS + 1))
            w1, w3 = (a[n].rearrange("e (t p) f -> e p t f", p=P) for n in ("w1_2", "w3_2"))
            w2 = a["w2_2"].rearrange("e (t p) f -> e p t f", p=P)
            for j in range(3):
                sp.wait_ge(weights_used[j], chunks["moe"].before(j))
            with sp.Fori(0, steps) as b:
                e = sp.snap(sp.value_load(plan_row[0:1, bass.ds(b + 1, 1)], min_val=0, max_val=EXPERTS - 1))
                e_before = sp.snap(sp.value_load(plan_row[0:1, bass.ds(b, 1)], min_val=0, max_val=EXPERTS - 1))
                for j, (w, at) in enumerate(((w1, e), (w3, e), (w2, e_before))):
                    src = w[bass.ds(at, 1)].rearrange("o p t f -> p (o t) f")
                    for n, (dst, half) in enumerate(pair(ring[:, j, :], src)):
                        for c in range(2):
                            sp.wait_ge(piece_split[4 * j + 2 * n + c], b + 1)
                        sp.dma_start(dst, half).then_inc(half_landed[2 * j + n], 16)
            for m in range(MT):
                sp.wait_ge(x_ready, 3 + m + 1)
                sp.dma_start(out_v[:, m, :], x[:, m, :]).then_inc(out_done, 16)
            sp.wait_ge(out_done, MT * 16)

        @block.tensor
        def _(pe):
            def landed(stage, j, i=0):
                st = chunks[stage]
                pe.wait_ge(weights_landed[st.place(j)], (st.before(j, i) + 1) * 32)
                return ring[:, st.place(j), :]

            def bank(stage, k, i=0):
                st = banks[stage]
                n = st.before(k, i)
                if not (isinstance(n, int) and n == 0):
                    pe.wait_ge(bank_drained[st.place(k)], n)
                return ps[:, st.place(k), :]

            def filled(stage, k, last):
                last.then_inc(bank_filled[banks[stage].place(k)], 1)

            def product(o, lhs, rhs):
                for k, (l, r) in enumerate(zip(lhs, rhs)):
                    mm = pe.matmul(o, l, r, start=(k == 0), stop=(k == len(lhs) - 1))
                return mm

            def turn(stage, k, pieces, n=P, i=0):
                o = bank(stage, k, i)
                pe.nop().then_inc(turn_may_start, 1)
                for q, piece in enumerate(pieces):
                    rows = piece.shape[0]
                    f = int(np.prod(piece.shape[1:]))
                    mm = pe.transpose(o[0:f, q * n:q * n + rows], piece, ident[0:rows, 0:rows])
                filled(stage, k, mm)

            def project(stage, srcT, mtiles, widths, rows_wait=None):
                k = 0
                for j, n in enumerate(widths):
                    r = landed(stage, j)
                    w = r[:, 0:KT * n].rearrange("p (k n) -> p k n", k=KT)
                    for m in range(mtiles):
                        o = bank(stage, k)
                        mm = product(o[:, 0:n], [srcT[:, t, m * P:(m + 1) * P] for t in range(KT)],
                                     [w[:, t, :] for t in range(KT)])
                        mm.then_inc(bank_filled[banks[stage].place(k)], 1)
                        k += 1

            def mark(signal):
                pe.matmul(ps[:, 7, 0:1], mark_src[:, :], mark_src[:, 0:1], start=True, stop=True).then_inc(signal, 1)

            def split_product(o, lhs, rhs, start, stop):
                pe.matmul(o, lhs[1], rhs[0], start=start, stop=False)
                pe.matmul(o, lhs[0], rhs[1], start=False, stop=False)
                return pe.matmul(o, lhs[0], rhs[0], start=False, stop=stop)

            def hi_lo(v):
                return [v[:, h] for h in range(2)]

            def split(stage, p, i=0):
                st = pieces[stage]
                pe.wait_ge(dense_split[st.place(p)], st.before(p, i) + 1)
                return parts[:, st.place(p)]

            def used(stage, p):
                mark(piece_used[pieces[stage].place(p)])

            def split_project(stage, widths, first_bank=0, first_piece=0, i=0):
                k, p = first_bank, first_piece
                for n in widths:
                    ks = 1024 // n
                    for q in range(KT // ks):
                        w = split(stage, p, i).rearrange("p h (k n) -> p h k n", k=ks)
                        for m in range(MT):
                            o = bank(stage, k + m, i) if q == 0 else ps[:, banks[stage].place(k + m), :]
                            for c in range(ks):
                                t = q * ks + c
                                mm = split_product(o[:, 0:n], hi_lo(actT[:, :, t, m * P:(m + 1) * P]),
                                                   hi_lo(w[:, :, c, :]), t == 0, t == KT - 1)
                            if q == KT // ks - 1:
                                filled(stage, k + m, mm)
                        used(stage, p)
                        p += 1
                    k += MT

            pe.wait_ge(const_in, 16)
            pe.wait_ge(c_rep_ready, KT)
            pe.wait_ge(c_in, 32)
            for q in range(4):
                mark(piece_used[q])
            for j in range(6):
                g = (2, 3, 0, 1, 4, 5)[j]
                w = landed("ada", j).rearrange("p (k n) -> p k n", k=KT)
                o = bank("ada", j)
                for t in range(KT):
                    pe.matmul(o, c_rep[:, t, :], w[:, t, :], start=(t == 0), stop=False)
                filled("ada", j, pe.matmul(o, cst("ones", 1), bada[0:1, g * 512:(g + 1) * 512], start=False, stop=True))

            pe.wait_ge(cols_in, 16 * 10)
            nrow = TAPS + 7
            o = bank("columns", 0)
            for t in range(KT):
                pe.transpose(o[:, t * nrow:(t + 1) * nrow], colrows[:, t * P:(t + 1) * P], ident[0:nrow, 0:nrow])
            filled("columns", 0, pe.transpose(o[:, KT * nrow:KT * nrow + 8], sgub_rows[:, :], ident[0:8, 0:8]))

            pe.wait_ge(h0_ready, MT)
            for t in range(KT):
                turn("hT", t, [h0[:, m, t * P:(t + 1) * P] for m in range(MT)])

            pe.wait_ge(actT_ready, KT)
            with pe.Fori(0, KT) as i:
                for j in range(5):
                    w = split("conv", j, i).rearrange("p h (k n) -> p h k n", k=KT)
                    o = bank("conv", j, i)
                    for t in range(KT):
                        mm = split_product(o, hi_lo(w[:, :, t, :]), hi_lo(actT[:, :, t, :]), t == 0, t == KT - 1)
                    filled("conv", j, mm)
                    used("conv", j)

            pe.wait_ge(conv_ready, KT)
            filled("ln", 0, product(bank("ln", 0), [cst("mean")] * KT, [convT[:, t, :] for t in range(KT)]))
            o = bank("ln", 1)
            for t in range(KT):
                pe.wait_ge(sq_ready, t + 1)
                mm = pe.matmul(o, cst("mean"), ln_sq[:, t % 2, :], start=(t == 0), stop=(t == KT - 1))
                if t < KT - 1:
                    mm.then_inc(sq_used, 1)
            filled("ln", 1, mm)

            def head_qk(stage, k0, p0, i=0):
                for q in range(4):
                    w = split(stage, p0 + q, i).rearrange("p h (k n) -> p h k n", k=2)
                    for k in range(4):
                        o = ps[:, banks[stage].place(k0 + k), :] if q else bank(stage, k0 + k, i)
                        for c in range(2):
                            mm = split_product(o, hi_lo(w[:, :, c, k * P:(k + 1) * P]), hi_lo(actT[:, :, 2 * q + c, :]),
                                               q == 0 and c == 0, q == 3 and c == 1)
                        if q == 3:
                            filled(stage, k0 + k, mm)
                    used(stage, p0 + q)

            def head_out(stage, h, i=0):
                split_project(stage, (HV, HV), 0, 0, i)
                pe.wait_ge(qk_ready, (h + 1) * 4)
                for j in range(MT):
                    o = bank(stage, 8 + j, i)[:, 0:S - j * P]
                    filled(stage, 8 + j, product(o, [qk_rot[:, 2 + c, j * P:(j + 1) * P] for c in range(2)],
                                                 [qk_rot[:, c, j * P:S] for c in range(2)]))
                pe.wait_ge(v_ready, (h + 1) * MT)
                pe.wait_ge(decayed_ready, (h + 1) * MT)
                for m in range(MT):
                    filled(stage, 12 + m, product(bank(stage, 12 + m, i),
                                                  [decayed[:, j, m * P:(m + 1) * P] for j in range(m + 1)],
                                                  [v_tok[:, j, :] for j in range(m + 1)]))

            def head_turn(stage, k0, h, i=0):
                pe.wait_ge(ret_ready, (h + 1) * MT)
                for e in range(4):
                    turn(stage, k0 + e, [z_tok[:, m, e * P:(e + 1) * P] for m in range(MT)], i=i)

            head_qk("qk0", 0, 0)
            with pe.Fori(0, HEADS - 1) as h:
                head_out("heads", h, h)
                head_qk("heads", 16, 8, h)
                head_turn("heads", 20, h, h)
            head_out("head_last", HEADS - 1)
            head_turn("head_last", 16, HEADS - 1)

            pe.wait_ge(retT_ready, HEADS * 4)
            with pe.Fori(0, KT) as i:
                o = bank("mix", 0, i)
                for j in range(2):
                    w = landed("mix", j, i)[:, 0:KT * P].rearrange("p (k n) -> p k n", k=KT)
                    for t in range(KT):
                        mm = pe.matmul(o, w[:, t, :], retT[:, j * KT + t, :], start=(j + t == 0), stop=(j == 1 and t == KT - 1))
                    if j == 1:
                        filled("mix", 0, mm)
                    mark(weights_used[chunks["mix"].place(j)])
                pe.wait_ge(conv_back, 16)
                w = landed("mix", 2, i)[:, 0:KT * P].rearrange("p (k n) -> p k n", k=KT)
                filled("mix", 1, product(bank("mix", 1, i), [w[:, t, :] for t in range(KT)], [conv_backT[:, t, :] for t in range(KT)]))
                mark(weights_used[chunks["mix"].place(2)])

            pe.wait_ge(merged_ready, KT)
            ws = [landed("out", j).rearrange("p (k n) -> p k n", k=KT) for j in range(2)]
            for k in range(8):
                m = OUT_TILES[k // 2]
                filled("out", k, product(bank("out", k), [mergedT[:, t, m * P:(m + 1) * P] for t in range(KT)],
                                         [ws[k % 2][:, t, :] for t in range(KT)]))

            def turn_rows(stage, src, n):
                pe.wait_ge(row_ready, n * MT)
                for t in range(KT):
                    turn(stage, t, [src[:, m, t * P:(t + 1) * P] for m in range(MT)])

            turn_rows("h2T", n_tok, 1)
            pe.wait_ge(actT_ready, 2 * KT)
            split_project("in2", (512, 256, 512, 512))

            pe.wait_ge(qk2_ready, 2)
            for r in range(4):
                turn("qkT", r, [q_pair[:, m, r * P:(r + 1) * P] for m in range(MT)])
            turn("qkT", 4, [kv_tok[:, m, 0:P] for m in range(MT)])
            pe.wait_ge(qkT_ready, 5)
            def scores(n):
                u = score_use(n)
                for v in range(2):
                    for rp in range(2):
                        o = bank("attn", u + 2 * v + rp).rearrange("p (a k) -> p a k", a=2)
                        for c in range(2):
                            mm = pe.matmul(o[:, c, :], qT[v * AD:(v + 1) * AD, 2 * rp + c, n * P:(n + 1) * P],
                                           kT[v * AD:(v + 1) * AD, n * P:(n + 2) * P], start=True, stop=True)
                        filled("attn", u + 2 * v + rp, mm)

            scores(0)
            for n in range(MT):
                if n < MT - 1:
                    scores(n + 1)
                u = weight_use(n)
                pe.wait_ge(p_ready, AH * (n + 1))
                for hp in range(4):
                    turn("attn", u + hp, [s_tok[n % 2][:, 2 * hp + c, w * P:(w + 1) * P] for c in range(2) for w in range(2)])
                pe.wait_ge(pT_ready, 4 * (n + 1))
                o = bank("attn", u + 4)
                for hd in range(AH):
                    v = hd // 4
                    halves = (0, 1) if n else (1,)
                    for w in halves:
                        mm = pe.matmul(o[:, hd * AD:(hd + 1) * AD], pT[:, 2 * hd + w, :],
                                       kv_tok[:, n - 1 + w, P + v * AD:P + (v + 1) * AD],
                                       start=(w == halves[0]), stop=(w == 1))
                filled("attn", u + 4, mm)

            pe.wait_ge(sguw_in, 16)
            for c in range(2):
                turn("sguw", c, [sgu_w[:, 4 * c + g, :] for g in range(4)])
            pe.wait_ge(sguwT_ready, 2)
            pe.wait_ge(vc_ready, 1)
            for gp in range(4):
                o = bank("sgu", gp).rearrange("p (a c d) -> p a c d", a=2, c=MT)
                for c in range(2):
                    g = 2 * gp + c
                    mm = pe.matmul(o[:, c], sgu_wT[:, g, :], g_tok[:, :, g * AD:(g + 1) * AD], start=True, stop=True)
                filled("sgu", gp, mm)
            turn_rows("mixT", n_tok, 2)
            pe.wait_ge(actT_ready, 3 * KT)
            split_project("out2", (512, 512))

            pe.wait_ge(vc_ready, 1 + MM)
            for c in range(4):
                turn("memT", c, [mem[:, m, (2 * c + q) * P:(2 * c + q + 1) * P] for q in range(2) for m in range(MM)])
            pe.wait_ge(memT_ready, KT)
            project("xk", memT, MM, (512, 512))
            project("xv", memT, MM, (512, 512))
            pe.wait_ge(vc_ready, 1 + MM + MT)
            for t in range(KT):
                turn("hqT", t, [n_tok[:, m, t * P:(t + 1) * P] for m in range(MT)])
            pe.wait_ge(xk_ready, 1)
            for c in range(4):
                turn("xkT", c, [xk_tok[:, m, (2 * c + q) * P:(2 * c + q + 1) * P] for q in range(2) for m in range(MM)])
            pe.wait_ge(actT_ready, 4 * KT)
            split_project("xq", (512, 512))
            for t in range(KT):
                pe.wait_ge(xq_ready, 1 + t // 4)
                turn("xqT", t, [xq_tok[:, m, t * P:(t + 1) * P] for m in range(MT)])
            pe.wait_ge(xkT_ready, 4)
            pe.wait_ge(xqT_ready, KT)
            for m in range(MT):
                for hp in range(2):
                    o = bank("xs", 2 * m + hp).rearrange("p (a k) -> p a k", a=2)
                    for c in range(2):
                        hd = 2 * hp + c
                        mm = product(o[:, c, :], [xqT[:, 2 * hd + q, m * P:(m + 1) * P] for q in range(2)],
                                     [xkT[:, 2 * hd + q, :] for q in range(2)])
                    filled("xs", 2 * m + hp, mm)
            pe.wait_ge(xp_ready, MT * XH)
            for k in range(2 * XH):
                turn("xpT", k, [xp_tok[:, m, k // 2, (k % 2) * P:(k % 2 + 1) * P] for m in range(MT)])
            pe.wait_ge(xpT_ready, KT)
            for t in range(KT):
                filled("xo", t, product(bank("xo", t), [xv_tok[:, w, t * P:(t + 1) * P] for w in range(MM)],
                                        [xpT[:, 2 * (t // 2) + w, :] for w in range(MM)]))
            pe.wait_ge(actT_ready, 5 * KT)
            split_project("xout", (512, 512))

            turn_rows("h3T", h3_tok, 3)
            pe.wait_ge(h3T_ready, KT)
            pe.wait_ge(ffn_in, 16 * (2 + GROUPS))
            o = bank("route", 0)
            nl = GROUPS + EXPERTS
            for m in range(MT):
                mm = product(o[:, m * nl:(m + 1) * nl], [h3T[:, t, m * P:(m + 1) * P] for t in range(KT)],
                             [wr[:, t, :] for t in range(KT)])
            filled("route", 0, mm)
            pe.wait_ge(oh_ready, MT)
            o = bank("route", 1)
            for m in range(MT):
                product(o[:, m * EXPERTS:(m + 1) * EXPERTS], [cst("ones")] * m + [cst("before")],
                        [ohs[:, q, :] for q in range(m + 1)])
            mm = product(o[:, MT * EXPERTS:(MT + 1) * EXPERTS], [cst("ones")] * MT, [ohs[:, q, :] for q in range(MT)])
            filled("route", 1, mm)
            pe.wait_ge(plan_col_ready, 1)
            filled("route", 2, pe.transpose(bank("route", 2)[0:1, 0:P], plan_col, ident))
            pe.wait_ge(slot_oh_ready, 1)
            filled("route", 3, product(bank("route", 3)[0:SLOTS, 0:64], [slot_oh[:, q, :] for q in range(2 * MT)],
                                       [block_oh[:, q, :] for q in range(2 * MT)]))

            def turn_slots(stage, k, rows, n, i=0):
                o = bank(stage, k, i)
                pe.nop().then_inc(turn_may_start, 1)
                for q in range(n):
                    mm = pe.transpose(o[:, q * SLOTS:(q + 1) * SLOTS], rows[0:SLOTS, q * P:(q + 1) * P], ident[0:SLOTS, 0:SLOTS])
                filled(stage, k, mm)

            pe.wait_ge(plan_ready, 2)
            steps = pe.snap(pe.value_load(n_steps[0:1, 0:1], min_val=2, max_val=MAX_BLOCKS + 1))
            pe.wait_ge(xg_in, 16)
            turn_slots("moe0", 0, xg, KT)
            for g in range(3):
                filled("moe0", 1 + g, pe.matmul(bank("moe0", 1 + g), ident, const[:, 0:512], start=True, stop=True))
            with pe.Fori(0, steps) as b:
                st = banks["moe"]
                for j in range(2):
                    o = bank("moe", 1 + j, b)[0:SLOTS, :]
                    if j == 0:
                        pe.wait_ge(bank_drained[st.place(0)], st.before(0, b))
                    for n in range(4):
                        pe.wait_ge(piece_split[4 * j + n], b + 2)
                        for c in range(2):
                            t = 2 * n + c
                            mm = split_product(o, [xgT[:, h, t, :] for h in range(2)],
                                               [parts[:, n, h, c * 512:(c + 1) * 512] for h in range(2)],
                                               n == 0 and c == 0, n == 3 and c == 1)
                        if n == 3:
                            filled("moe", 1 + j, mm)
                        mark(piece_used[n])
                pe.wait_ge(xg_in, (b + 2) * 16)
                turn_slots("moe", 0, xg, KT, b)
                ys = [bank("moe", 4 + g, b)[0:SLOTS, :] for g in range(2)]
                pe.wait_ge(bank_drained[st.place(3)], st.before(3, b))
                for n in range(4):
                    pe.wait_ge(piece_split[8 + n], b + 2)
                    for g in range(2):
                        mm = split_product(ys[g], [hidT[:, h, n, :] for h in range(2)],
                                           [parts[:, n, h, g * 512:(g + 1) * 512] for h in range(2)], n == 0, n == 3)
                        if n == 3:
                            filled("moe", 4 + g, mm)
                    mark(piece_used[n])
                pe.wait_ge(hid_ready, b + 1)
                turn_slots("moe", 3, hid, 4, b)

        @block.scalar
        def _(act):
            own = Chain(act, act_own)

            def full(stage, k, i=0):
                st = banks[stage]
                act.wait_ge(bank_filled[st.place(k)], st.before(k, i) + 1)
                return ps[:, st.place(k), :]

            def drained(stage, k, ins):
                ins.then_inc(bank_drained[banks[stage].place(k)], 1)

            def release(stage, j):
                act.nop().then_inc(weights_used[chunks[stage].place(j)], 1)

            sets = [0]

            def roots(src, dst, eps_col, scale=1.0):
                sets[0] += 1
                act.wait_ge(ms_ready, sets[0])
                act.activation(dst, src, ACT.Sqrt, bias=eps[:, eps_col:eps_col + 1], scale=scale).then_inc(rms_ready, 1)

            roots(st_ms[:, 0:MT], st_rms[:, 0:MT], 0, 1.0 / D)
            act.wait_ge(angles_ready, 1)
            own(act.activation(sinT, angle, ACT.Sin))
            own(act.activation(cosT, turns, ACT.Sin))
            own.wait()
            act.nop().then_inc(rotary_ready, 1)
            def take_T(stage, col):
                for t in range(KT):
                    o = full(stage, t)
                    kw = {} if col is None else {"scale": cols[:, t, col:col + 1]}
                    act.activation(actT[:, 0, t, :], o, ACT.Copy, **kw).then_inc(actT_hi, 1)

            take_T("hT", None)

            act.nop().then_inc(gates_stored, 16)
            with act.Fori(0, KT) as i:
                own.enter(i, 2)
                act.wait_ge(gates_stored, (i + 1) * 16)
                act.activation(sig_u, full("conv", 1, i), ACT.Sigmoid).then_inc(sig_u_ready, 1)
                for g in range(2):
                    own(act.activation(sig_g[:, g, :], full("conv", 2 + g, i), ACT.Sigmoid))
                act.activation(sig_z, full("conv", 4, i), ACT.Sigmoid).then_inc(sig_z_ready, 1)
                own.wait()
                act.wait_ge(sig_u_ready, i + 1)
                for k in (1, 2, 3):
                    drained("conv", k, act.nop())
                act.dma_start(gates_dram[bass.ds(i, 1)].rearrange("o p g n -> p (o g) n"), sig_g).then_inc(gates_stored, 16)
            own.leave(KT)

            for t in range(KT):
                act.wait_ge(cen_ready, t + 1)
                if t >= 2:
                    act.wait_ge(sq_used, t - 1)
                act.activation(ln_sq[:, t % 2, :], convT[:, t, :], ACT.Square).then_inc(sq_ready, 1)
            o = full("ln", 1)
            own(act.activation(ln_std, o, ACT.Sqrt, bias=eps[:, 2:3]))
            own.wait()
            drained("ln", 1, act.nop())
            act.nop().then_inc(ln_std_ready, 1)
            for t in range(KT):
                act.wait_ge(ln_y_ready, t + 1)
                if t >= 2:
                    act.wait_ge(gated_conv_ready, t - 1)
                g, bias = cols[:, t, TAPS + 1:TAPS + 2], cols[:, t, TAPS + 2:TAPS + 3]
                own(act.activation(ln_y[:, t % 2, :], ln_y[:, t % 2, :], ACT.Identity, bias=bias, scale=g))
                own.wait()
                act.activation(ln_s[:, t % 2, :], ln_y[:, t % 2, :], ACT.Sigmoid).then_inc(ln_s_ready, 1)

            act.wait_ge(gated_conv_ready, KT)
            act.dma_start(conv_dram, convT).then_inc(conv_stored, 16)
            act.wait_ge(conv_stored, 16)
            def head(stage, turned, h, i=0):
                for m in range(MT):
                    o = full(stage, m, i)
                    own(act.copy(v_tok[:, m, :], o))
                    own.wait()
                    act.nop().then_inc(v_ready, 1)
                    drained(stage, m, act.nop())
                for m in range(MT):
                    o = full(stage, 4 + m, i)
                    if m >= 2:
                        act.wait_ge(sig_r_used, h * MT + (m - 1))
                    act.activation(sig_r[:, m % 2, :], o, ACT.Sigmoid).then_inc(sig_r_ready, 1)
                act.wait_ge(var_ready, h + 1)
                act.activation(st_std, mv.rearrange("p (m s) -> p m s", s=2)[:, :, 1], ACT.Sqrt,
                               bias=eps[:, 1:2]).then_inc(std_ready, 1)
                for e in range(4):
                    o = full(stage, turned + e, i)
                    own(act.copy(retT[:, bass.ds(h * 4 + e, 1), :], o))
                    own.wait()
                    act.nop().then_inc(retT_ready, 1)
                    drained(stage, turned + e, act.nop())

            with act.Fori(0, HEADS - 1) as h:
                own.enter(h, 8)
                head("heads", 20, h, h)
            own.leave(HEADS - 1)
            head("head_last", 16, HEADS - 1)
            act.wait_ge(retT_ready, HEADS * 4)
            act.dma_start(conv_backT, conv_dram).then_inc(conv_back, 16)

            def take(stage, k, dst, func=ACT.Copy, done=None, n=512, mtiles=None):
                o = full(stage, k)
                if mtiles and k % mtiles == mtiles - 1:
                    release(stage, k // mtiles)
                own(act.activation(dst, o[:, 0:n], func))
                own.wait()
                drained(stage, k, act.nop())
                if done is not None:
                    act.nop().then_inc(done, 1)

            act.wait_ge(merged_ready, KT)
            act.wait_ge(y_cleared, 16)
            act.dma_start(x[:, 1:MT, :], x_v[:, 1:MT, :]).then_inc(x_back, 16)
            act.dma_start(x0_early, x_v[:, 0, :]).then_inc(x_back, 16)
            for k in range(8):
                m = OUT_TILES[k // 2]
                take("out", k, y_tok[:, m, (k % 2) * 512:(k % 2 + 1) * 512], done=y_ready)
                if k >= 6:
                    release("out", k % 2)
                if k % 2:
                    for at in (m, MT + m):
                        roots(st_ms[:, at:at + 1], st_rms[:, at:at + 1], 0, 1.0 / D)

            take_T("h2T", TAPS + 3)
            for k in range(16):
                j, m = k // MT, k % MT
                dst, n = ((q_tok, 512), (kv_tok, 256), (u_tok, 512), (g_tok, 512))[j]
                take("in2", k, dst[:, m, :], ACT.Gelu_apprx_tanh if j >= 2 else ACT.Copy, done=in2_ready, n=n)
                if k in (MT - 1, 2 * MT - 1):
                    cnt_ = MT * (AH if k < MT else 2)
                    roots(st_ms[:, 0:cnt_], st_rms[:, 0:cnt_], 0, 1.0 / AD)
            roots(st_ms[:, 0:MT], st_rms[:, 0:MT], 0, 1.0 / 512)
            for r in range(4):
                take("qkT", r, qT[:, r, :], done=qkT_ready)
            take("qkT", 4, kT[:, P:], done=qkT_ready)
            for n in range(MT):
                act.wait_ge(smax_ready, n + 1)
                half = 16 * (n % 2)
                for hd in range(AH):
                    v = s_tok[n % 2][:, hd, :]
                    act.activation(v, v, ACT.Exp, bias=nmx[:, half + hd:half + hd + 1],
                                   accum_out=den[:, half + hd:half + hd + 1]).then_inc(p_ready, 1)
                sinkx = nmx[:, half + AH:half + 2 * AH]
                act.activation(sinkx, sinkx, ACT.Exp).then_inc(sink_exp, 1)
            for lo in (0, MT):
                roots(st_ms[:, lo:lo + MT], st_rms[:, lo:lo + MT], 0, 1.0 / 512)
            take_T("mixT", TAPS + 6)

            roots(st_ms[:, 0:MM], st_rms[:, 0:MM], 0, 1.0 / D)
            for c in range(4):
                o = full("memT", c).rearrange("p (q n) -> p q n", q=2)
                for q in range(2):
                    own(act.activation(memT[:, 2 * c + q, :], o[:, q, :], ACT.Copy, scale=cols[:, 2 * c + q, TAPS + 5:TAPS + 6]))
                own.wait()
                drained("memT", c, act.nop())
                for q in range(2):
                    act.nop().then_inc(memT_ready, 1)
            roots(st_ms[:, 0:MT], st_rms[:, 0:MT], 0, 1.0 / D)
            for stage, dst in (("xk", xk_tok), ("xv", xv_tok)):
                for k in range(4):
                    take(stage, k, dst[:, k % MM, (k // MM) * 512:(k // MM + 1) * 512], done=xkv_ready, mtiles=MM)
                if stage == "xk":
                    roots(st_ms[:, 0:MM * XH], st_rms[:, 0:MM * XH], 0, 1.0 / XD)
            take_T("hqT", TAPS + 4)
            for c in range(4):
                take("xkT", c, xkT[:, 2 * c:2 * c + 2, :].rearrange("p q n -> p (q n)"), done=xkT_ready)
            for k in range(8):
                take("xq", k, xq_tok[:, k % MT, (k // MT) * 512:(k // MT + 1) * 512], done=xq_in)
                if k % MT == MT - 1:
                    lo = k // MT * 2 * MT
                    roots(st_ms[:, lo:lo + 2 * MT], st_rms[:, lo:lo + 2 * MT], 0, 1.0 / XD)
            for t in range(KT):
                take("xqT", t, xqT[:, t, :], done=xqT_ready)
            for m in range(MT):
                for hp in range(2):
                    act.wait_ge(xmax_ready, 2 * m + hp + 1)
                    o = full("xs", 2 * m + hp).rearrange("p (a k) -> p a k", a=2)
                    for c in range(2):
                        hd = m * XH + 2 * hp + c
                        own(act.activation(xp_tok[:, m, 2 * hp + c, :], o[:, c, :], ACT.Exp, bias=nmx[:, hd:hd + 1],
                                           accum_out=den[:, hd:hd + 1]))
                    own.wait()
                    drained("xs", 2 * m + hp, act.nop())
                act.nop().then_inc(xq_in, 1)
            for k in range(8):
                take("xpT", k, xpT[:, k, :], done=xpT_ready)
            take_T("xo", None)

            roots(st_ms[:, 0:MT], st_rms[:, 0:MT], 0, 1.0 / D)
            for t in range(KT):
                take("h3T", t, h3T[:, t, :], done=h3T_ready)
            act.wait_ge(gexp_in, 1)
            act.activation(gexp, gexp, ACT.Exp).then_inc(gexp_ready, 1)
            act.wait_ge(texp_in, 1)
            act.activation(dl, dl, ACT.Exp).then_inc(texp_ready, 1)
            act.wait_ge(plan_ready, 2)
            steps = act.snap(act.value_load(n_steps[0:1, 0:1], min_val=2, max_val=MAX_BLOCKS + 1))
            act.wait_ge(y_cleared, 16)
            act.nop().then_inc(y_stored, 16)

            def high(n, b):
                j = n // 4
                act.wait_ge(half_landed[2 * j + n % 4 // 2], (b + 1) * 16)
                act.wait_ge(piece_used[pieces["moe"].place(n)], pieces["moe"].before(n, b) + 1)
                act.copy(parts[:, n % 4, 0, :], ring[:, j, n % 4 * 1024:(n % 4 + 1) * 1024]).then_inc(piece_hi, 1)

            def store_rows(b):
                st = banks["moe"]
                act.wait_ge(y_stored, (b + 1) * 16)
                for g in range(2):
                    act.wait_ge(bank_filled[st.place(4 + g)], st.before(4 + g, b))
                    own(act.copy(y_blk[0:SLOTS, g * 512:(g + 1) * 512], ps[0:SLOTS, st.place(4 + g), :]))
                own.wait()
                for g in range(2):
                    drained("moe", 4 + g, act.nop())
                act.dma_start(y_rows[bass.ds(b * SLOTS, SLOTS), :], y_blk[0:SLOTS, :]).then_inc(y_stored, 16)

            act.copy(xgT[:, 0].rearrange("p t n -> p (t n)"), full("moe0", 0)).then_inc(xgT_hi, 1)
            with act.Fori(0, steps) as b:
                own.enter(b, 2)
                for n in range(4):
                    high(n, b)
                store_rows(b)
                st = banks["moe"]
                act.wait_ge(bank_filled[st.place(3)], st.before(3, b))
                act.copy(hidT[:, 0].rearrange("p t n -> p (t n)"), ps[:, st.place(3), 0:4 * SLOTS]).then_inc(hidT_hi, 1)
                for n in range(4, 8):
                    high(n, b)
                act.activation(sg_h[0:SLOTS, :], full("moe", 1, b)[0:SLOTS, :], ACT.Sigmoid).then_inc(sg_h_ready, 1)
                for n in range(8, 12):
                    high(n, b)
                o = full("moe", 0, b)
                act.copy(xgT[:, 0].rearrange("p t n -> p (t n)"), o).then_inc(xgT_hi, 1)
            own.base = act.snap(steps * own.per + own.at)
            own.count = 0
            store_rows(steps)
            act.wait_ge(y_stored, steps * 16 + 32)
            act.nop().then_inc(y_blk_ready, 1)

        @block.vector
        def _(dve):
            own = Chain(dve, dve_own)

            def full(stage, k, i=0):
                st = banks[stage]
                dve.wait_ge(bank_filled[st.place(k)], st.before(k, i) + 1)
                return ps[:, st.place(k), :]

            def drained(stage, k, ins):
                ins.then_inc(bank_drained[banks[stage].place(k)], 1)

            def mean_squares(srcs, dst, junk, ready_n=None):
                for m, s in enumerate(srcs):
                    own(dve.tensor_tensor_reduce(out=junk, in0=s, in1=s, scale=1.0, scalar=0.0, op0=ALU.mult,
                                                 op1=ALU.add, accum_out=dst[:, m:m + 1]))
                    own.wait()
                dve.nop().then_inc(ms_ready, 1)

            def head_squares(src, groups, width, dst, junk):
                own(dve.tensor_tensor(junk, src, src, ALU.mult))
                own.wait()
                own(dve.tensor_reduce(dst, junk.rearrange("p (g d) -> p g d", d=width), AX.X, ALU.add))
                own.wait()

            sets = [0]

            def reciprocals(lo, hi):
                sets[0] += 1
                dve.wait_ge(rms_ready, sets[0])
                own(dve.reciprocal(st_r[:, lo:hi], st_rms[:, lo:hi]))
                own.wait()

            def low_T(stage, n, col):
                for t in range(KT):
                    o = full(stage, t)
                    dve.wait_ge(actT_hi, (n - 1) * KT + t + 1)
                    hi, lo = actT[:, 0, t, :].bitcast(F32), actT[:, 1, t, :]
                    if col is None:
                        own(dve.tensor_tensor(lo, o, hi, ALU.subtract))
                    else:
                        own(dve.scalar_tensor_tensor(out=lo, in0=o, scalar=cols[:, t, col:col + 1], in1=hi,
                                                     op0=ALU.mult, op1=ALU.subtract))
                    own.wait()
                    drained(stage, t, dve.nop())
                    dve.nop().then_inc(actT_ready, 1)

            for n, v in enumerate((RMS_EPS, GN_EPS, LN_EPS)):
                own(dve.memset(eps[:, n:n + 1], v))
            own(dve.memset(mark_src[:, :], 0.0))
            dve.wait_ge(const_in, 16)
            dve.wait_ge(c_in, 32)
            for t in range(KT):
                dve.tensor_scalar(c_rep[:, t, :], cst("ones"), c_col[:, t:t + 1], None, ALU.mult).then_inc(c_rep_ready, 1)
            dve.wait_ge(x_in, 16)
            own.wait()
            mean_squares([x0[:, m, :] for m in range(MT)], st_ms, h0[:, 0, :])

            dve.wait_ge(pos_in, 16)
            own(dve.tensor_copy(angle, pos_i[:, :]))
            own.wait()
            own(dve.tensor_scalar(angle, angle, cst("freq"), None, ALU.mult))
            own.wait()
            magic = float(1.5 * 2 ** 23)
            own(dve.tensor_scalar(turns, angle, float(1 / (2 * np.pi)), magic, ALU.mult, ALU.add))
            own.wait()
            own(dve.tensor_scalar(turns, turns, magic, None, ALU.subtract))
            own.wait()
            left = 2 * np.pi
            for bits in (5, 13, None):
                part = float(np.float32(left)) if bits is None else float(np.floor(left * 2 ** bits) / 2 ** bits)
                left -= part
                own(dve.scalar_tensor_tensor(out=angle, in0=turns, scalar=-part, in1=angle, op0=ALU.mult, op1=ALU.add))
                own.wait()
            lim = 3.1415925
            own(dve.tensor_scalar(angle, angle, lim, -lim, ALU.min, ALU.max))
            own.wait()
            own(dve.scalar_tensor_tensor(out=turns, in0=angle, scalar=-1.0, in1=angle, op0=ALU.mult, op1=ALU.max))
            own.wait()
            own(dve.tensor_scalar(turns, turns, -1.0, float(np.pi / 2), ALU.mult, ALU.add))
            own.wait()
            dve.nop().then_inc(angles_ready, 1)

            dve.wait_ge(rows_in, 32)
            def release(stage, j):
                dve.nop().then_inc(weights_used[chunks[stage].place(j)], 1)

            for j in range(6):
                o = full("ada", j)
                release("ada", j)
                half = slice((j % 2) * 512, (j % 2) * 512 + 512)
                if j < 2:
                    own(dve.scalar_tensor_tensor(out=mod_scale[:, half], in0=o, scalar=1.0, in1=pre_g[:, half],
                                                 op0=ALU.add, op1=ALU.mult))
                elif j < 4:
                    own(dve.tensor_copy(mod_shift[:, half], o))
                else:
                    own(dve.tensor_tensor(gate_post[:, half], o, post_g[:, half], ALU.mult))
                own.wait()
                drained("ada", j, dve.nop())
                if j == 3:
                    reciprocals(0, MT)
                    for m in range(MT):
                        own(dve.scalar_tensor_tensor(out=h0[:, m, :], in0=x0[:, m, :], scalar=st_r[:, m:m + 1],
                                                     in1=mod_scale, op0=ALU.mult, op1=ALU.mult))
                    own.wait()
                    for m in range(MT):
                        dve.tensor_tensor(h0[:, m, :], h0[:, m, :], mod_shift, ALU.add).then_inc(h0_ready, 1)

            o = full("columns", 0)
            nrow = TAPS + 7
            own(dve.tensor_copy(cols[:, :, :], o[:, 0:KT * nrow].rearrange("p (t r) -> p t r", t=KT)))
            own(dve.tensor_copy(sgub[:, :], o[:, KT * nrow:KT * nrow + 8]))
            own.wait()
            drained("columns", 0, dve.nop())

            dve.wait_ge(h0_ready, MT)
            low_T("hT", 1, None)
            dve.wait_ge(rotary_ready, 1)
            own(dve.memset(apad[:, 0:TAPS - 1], 0.0))
            own.wait()
            with dve.Fori(0, KT) as i:
                own.enter(i, 2 + TAPS + 1)
                o = full("conv", 0, i)
                dve.wait_ge(sig_u_ready, i + 1)
                own(dve.tensor_tensor(apad[:, TAPS - 1:], o, sig_u, ALU.mult))
                own.wait()
                drained("conv", 0, dve.nop())
                col = cols[:, bass.ds(i, 1), :].rearrange("p o r -> p (o r)")
                for j in range(TAPS):
                    acc = conv_acc[:, j % 2, :]
                    if j == 0:
                        own(dve.tensor_scalar(acc, apad[:, 0:S], col[:, 0:1], col[:, TAPS:TAPS + 1], ALU.mult, ALU.add))
                    elif j == 1:
                        own(dve.tensor_scalar(acc, apad[:, 1:1 + S], col[:, 1:2], None, ALU.mult))
                    else:
                        own.wait(1)
                        own(dve.scalar_tensor_tensor(out=acc, in0=apad[:, j:j + S], scalar=col[:, j:j + 1], in1=acc,
                                                     op0=ALU.mult, op1=ALU.add))
                own.wait()
                dve.wait_ge(sig_z_ready, i + 1)
                own(dve.tensor_tensor(zconvT[:, bass.ds(i, 1), :], full("conv", 4, i), sig_z, ALU.mult))
                own.wait()
                drained("conv", 4, dve.nop())
                own(dve.tensor_tensor(convT[:, bass.ds(i, 1), :], conv_acc[:, 0, :], conv_acc[:, 1, :], ALU.add))
                own.wait()
                dve.nop().then_inc(conv_ready, 1)
            own.leave(KT)

            o = full("ln", 0)
            for t in range(KT):
                own(dve.tensor_tensor(convT[:, t, :], convT[:, t, :], o, ALU.subtract))
                own.wait()
                dve.nop().then_inc(cen_ready, 1)
            drained("ln", 0, dve.nop())
            dve.wait_ge(ln_std_ready, 1)
            own(dve.reciprocal(ln_rstd, ln_std))
            own.wait()
            for t in range(KT + 1):
                if t < KT:
                    if t >= 2:
                        dve.wait_ge(gated_conv_ready, t - 1)
                    dve.tensor_tensor(ln_y[:, t % 2, :], convT[:, t, :], ln_rstd, ALU.mult).then_inc(ln_y_ready, 1)
                if t:
                    q = t - 1
                    dve.wait_ge(ln_s_ready, q + 1)
                    own(dve.tensor_tensor(convT[:, q, :], ln_y[:, q % 2, :], ln_s[:, q % 2, :], ALU.mult))
                    own.wait()
                    dve.tensor_tensor(convT[:, q, :], convT[:, q, :], zconvT[:, q, :], ALU.mult).then_inc(gated_conv_ready, 1)

            dve.wait_ge(gated_conv_ready, KT)
            dve.wait_ge(gates_stored, (KT + 1) * 16)
            dve.nop().then_inc(decay_used, MT)
            def rotate(stage, k0, i=0):
                for part in range(2):
                    t1, t2 = full(stage, k0 + 2 * part, i), full(stage, k0 + 2 * part + 1, i)
                    own(dve.tensor_tensor(rot[:, 0, :], t1, cosT, ALU.mult))
                    own(dve.tensor_tensor(rot[:, 1, :], t2, sinT, ALU.mult))
                    own(dve.tensor_tensor(rot[:, 2, :], t1, sinT, ALU.mult))
                    own(dve.tensor_tensor(rot[:, 3, :], t2, cosT, ALU.mult))
                    own.wait()
                    for q in range(2):
                        drained(stage, k0 + 2 * part + q, dve.nop())
                    own(dve.tensor_tensor(qk_rot[:, 2 * part, :], rot[:, 0, :], rot[:, 1, :], ALU.subtract))
                    own(dve.tensor_tensor(qk_rot[:, 2 * part + 1, :], rot[:, 2, :], rot[:, 3, :], ALU.add))
                    own.wait()
                    for q in range(2):
                        dve.nop().then_inc(qk_ready, 1)

            def head_rows(stage, h, i=0):
                for m in range(MT):
                    o = full(stage, 4 + m, i)
                    dve.wait_ge(sig_r_ready, h * MT + m + 1)
                    own(dve.tensor_tensor(z_tok[:, m, :], o, sig_r[:, m % 2, :], ALU.mult))
                    own.wait()
                    dve.nop().then_inc(sig_r_used, 1)
                    drained(stage, 4 + m, dve.nop())
                dve.wait_ge(decay_in, (h + 1) * 16)
                for j in range(MT):
                    o = full(stage, 8 + j, i)
                    own(dve.tensor_tensor(decayed[:, j, j * P:S], o[:, 0:S - j * P], decay[:, 0:S - j * P], ALU.mult))
                    own.wait()
                    dve.nop().then_inc(decayed_ready, 1)
                    dve.nop().then_inc(decay_used, 1)
                    drained(stage, 8 + j, dve.nop())
                for m in range(MT):
                    own(dve.bn_stats(bn6[:, 6 * m:6 * m + 6], full(stage, 12 + m, i)))
                own.wait()
                dve.nop().then_inc(stats_settled, 1)
                for m in range(MT):
                    own(dve.bn_aggr(mv[:, 2 * m:2 * m + 2], bn6[:, 6 * m:6 * m + 6]))
                own.wait()
                dve.nop().then_inc(var_ready, 1)
                dve.wait_ge(std_ready, h + 1)
                own(dve.reciprocal(gn_r, st_std))
                own.wait()
                for m in range(MT):
                    o = ps[:, banks[stage].place(12 + m), :]
                    if m >= 2:
                        dve.wait_ge(ret_ready, h * MT + (m - 1))
                    own(dve.tensor_scalar(norm_o[:, m % 2, :], o, mv[:, 2 * m:2 * m + 1], gn_r[:, m:m + 1],
                                          ALU.subtract, ALU.mult))
                    own.wait()
                    drained(stage, 12 + m, dve.nop())
                    dve.tensor_tensor(z_tok[:, m, :], norm_o[:, m % 2, :], z_tok[:, m, :], ALU.mult).then_inc(ret_ready, 1)

            rotate("qk0", 0)
            with dve.Fori(0, HEADS - 1) as h:
                own.enter(h, 12 + 5 * MT + 1)
                head_rows("heads", h, h)
                rotate("heads", 16, h)
            own.leave(HEADS - 1)
            head_rows("head_last", HEADS - 1)

            dve.nop().then_inc(gates_used, 1)
            with dve.Fori(0, KT) as i:
                own.enter(i, 3)
                dve.wait_ge(gates_in, (i + 1) * 16)
                for g, part in enumerate((part_a, part_b)):
                    own(dve.tensor_tensor(part, full("mix", g, i), sig_ab[:, g, :], ALU.mult))
                    own.wait()
                    drained("mix", g, dve.nop())
                dve.nop().then_inc(gates_used, 1)
                own(dve.tensor_tensor(mergedT[:, bass.ds(i, 1), :], part_a, part_b, ALU.add))
                own.wait()
                dve.nop().then_inc(merged_ready, 1)
            own.leave(KT)

            dve.wait_ge(x_back, 32)
            for k, m in enumerate(OUT_TILES):
                dve.wait_ge(y_ready, 2 * (k + 1))
                mean_squares([y_tok[:, m, :]], st_ms[:, m:m + 1], squares)
                reciprocals(m, m + 1)
                own(dve.scalar_tensor_tensor(out=y_tok[:, m, :], in0=y_tok[:, m, :], scalar=st_r[:, m:m + 1],
                                             in1=gate_post, op0=ALU.mult, op1=ALU.mult))
                own.wait()
                own(dve.tensor_tensor(x[:, m, :], x[:, m, :] if m else x0_early, y_tok[:, m, :], ALU.add))
                own.wait()
                mean_squares([x[:, m, :]], st_ms[:, MT + m:MT + m + 1], squares)
                reciprocals(MT + m, MT + m + 1)
                dve.tensor_scalar(n_tok[:, m, :], x[:, m, :], st_r[:, MT + m:MT + m + 1], None, ALU.mult).then_inc(row_ready, 1)
            dve.nop().then_inc(x_ready, 1)

            def norm_rows(dst, done, junk, gain=None):
                mean_squares([x[:, m, :] for m in range(MT)], st_ms, junk)
                reciprocals(0, MT)
                for m in range(MT):
                    if gain is None:
                        dve.tensor_scalar(dst[:, m, :], x[:, m, :], st_r[:, m:m + 1], None, ALU.mult).then_inc(done, 1)
                    else:
                        dve.scalar_tensor_tensor(out=dst[:, m, :], in0=x[:, m, :], scalar=st_r[:, m:m + 1], in1=gain,
                                                 op0=ALU.mult, op1=ALU.mult).then_inc(done, 1)

            low_T("h2T", 2, TAPS + 3)

            dve.wait_ge(gains_in, 64)
            dve.wait_ge(in2_ready, MT)
            dve.wait_ge(row_ready, MT)
            flat = lambda v: v.rearrange("p m d -> p (m d)")
            head_squares(flat(q_tok), 32, AD, st_ms[:, 0:32], flat(sq_junk))
            dve.nop().then_inc(ms_ready, 1)
            reciprocals(0, 32)

            def head_scale(v, nheads, width):
                r = st_r[:, 0:nheads].unsqueeze(2).to_broadcast([P, nheads, width])
                own(dve.tensor_tensor(v, v, r, ALU.mult))
                own.wait()

            head_scale(q_tok.rearrange("p m (h d) -> p (m h) d", d=AD), 32, AD)
            for m in range(MT):
                for v in range(2):
                    heads = q_tok[:, m, v * 256:(v + 1) * 256].rearrange("p (r d) -> p r d", d=AD)
                    pairs = q_pair[:, m, :].rearrange("p (r v d) -> p r v d", r=4, v=2)[:, :, v, :]
                    own(dve.scalar_tensor_tensor(out=pairs, in0=heads, scalar=AD ** -0.5,
                                                 in1=qn_row.unsqueeze(1).to_broadcast([P, 4, AD]),
                                                 op0=ALU.mult, op1=ALU.mult))
            own.wait()
            dve.nop().then_inc(qk2_ready, 1)
            dve.wait_ge(in2_ready, 2 * MT)
            for m in range(MT):
                own(dve.tensor_tensor(sq_junk[:, m, 0:P], kv_tok[:, m, 0:P], kv_tok[:, m, 0:P], ALU.mult))
            own.wait()
            for m in range(MT):
                own(dve.tensor_reduce(st_ms[:, 2 * m:2 * m + 2], sq_junk[:, m, 0:P].rearrange("p (g d) -> p g d", d=AD),
                                      AX.X, ALU.add))
            own.wait()
            dve.nop().then_inc(ms_ready, 1)
            reciprocals(0, 8)
            for m in range(MT):
                for v in range(2):
                    k = kv_tok[:, m, v * AD:(v + 1) * AD]
                    own(dve.scalar_tensor_tensor(out=k, in0=k, scalar=st_r[:, 2 * m + v:2 * m + v + 1], in1=kn_row,
                                                 op0=ALU.mult, op1=ALU.mult))
            own(dve.memset(kT[:, 0:P], 0.0))
            own.wait()
            dve.nop().then_inc(qk2_ready, 1)
            dve.wait_ge(in2_ready, 4 * MT)
            mean_squares([g_tok[:, m, :] for m in range(MT)], st_ms, sq_junk[:, 0, :])
            reciprocals(0, MT)
            for m in range(MT):
                own(dve.scalar_tensor_tensor(out=g_tok[:, m, :], in0=g_tok[:, m, :], scalar=st_r[:, m:m + 1], in1=sgun_row,
                                             op0=ALU.mult, op1=ALU.mult))
            own.wait()
            dve.nop().then_inc(vc_ready, 1)

            def columns(v, n):
                lo = 16 * (n % 2)
                return v[:, lo:lo + AH], v[:, lo + AH:lo + 2 * AH]

            def window_max(n):
                mask = cst("band" if n else "first").unsqueeze(1).to_broadcast([P, 2, 2 * P])
                st = s_tok[n % 2]
                for q in range(4):
                    o = full("attn", score_use(n) + q).rearrange("p (a k) -> p a k", a=2)
                    own(dve.tensor_tensor(st[:, 2 * q:2 * q + 2, :], o, mask, ALU.add))
                    own.wait()
                    drained("attn", score_use(n) + q, dve.nop())
                top_, (neg, sinkx) = columns(mx, n)[0], columns(nmx, n)
                own(dve.tensor_reduce(top_, st, AX.X, ALU.max))
                own.wait()
                own(dve.tensor_tensor(top_, top_, sink_row, ALU.max))
                own.wait()
                own(dve.tensor_scalar(neg, top_, -1.0, None, ALU.mult))
                own(dve.tensor_tensor(sinkx, sink_row, top_, ALU.subtract))
                own.wait()
                dve.nop().then_inc(smax_ready, 1)

            window_max(0)
            for n in range(MT):
                if n < MT - 1:
                    window_max(n + 1)
                u = weight_use(n)
                total, inv = columns(den, n)[0], columns(mx, n)[1]
                dve.wait_ge(sink_exp, n + 1)
                dve.wait_ge(p_ready, AH * (n + 1))
                own(dve.tensor_tensor(total, total, columns(nmx, n)[1], ALU.add))
                own.wait()
                own(dve.reciprocal(inv, total))
                for hp in range(4):
                    own(dve.tensor_copy(pT[:, 4 * hp:4 * hp + 4, :].rearrange("p a k -> p (a k)"), full("attn", u + hp)))
                    own.wait()
                    drained("attn", u + hp, dve.nop())
                    dve.nop().then_inc(pT_ready, 1)
                o = full("attn", u + 4).rearrange("p (h d) -> p h d", d=AD)
                own(dve.tensor_tensor(attn_tok[:, n, :].rearrange("p (h d) -> p h d", d=AD), o,
                                      inv.unsqueeze(2).to_broadcast([P, AH, AD]), ALU.mult))
                own.wait()
                drained("attn", u + 4, dve.nop())
            dve.nop().then_inc(pv_done, 1)
            mean_squares([attn_tok[:, m, :] for m in range(MT)], st_ms, sq_junk[:, 0, :])
            reciprocals(0, MT)
            for m in range(MT):
                own(dve.tensor_scalar(n_tok[:, m, 0:512], attn_tok[:, m, :], st_r[:, m:m + 1], None, ALU.mult))
            own.wait()

            for c in range(2):
                o = full("sguw", c).rearrange("p (g i) -> p g i", g=4)
                own(dve.tensor_tensor(sgu_wT[:, 4 * c:4 * c + 4, :], o, cst("causalT").unsqueeze(1).to_broadcast([P, 4, P]), ALU.mult))
                own.wait()
                drained("sguw", c, dve.nop())
                dve.nop().then_inc(sguwT_ready, 1)
            for gp in range(4):
                o = full("sgu", gp).rearrange("p (a c d) -> p a c d", a=2, c=MT)
                for c in range(2):
                    g = 2 * gp + c
                    u = u_tok[:, :, g * AD:(g + 1) * AD]
                    own(dve.scalar_tensor_tensor(out=u, in0=o[:, c], scalar=sgub[:, g:g + 1], in1=u, op0=ALU.add, op1=ALU.mult))
                own.wait()
                drained("sgu", gp, dve.nop())
            mean_squares([u_tok[:, m, :] for m in range(MT)], st_ms[:, MT:2 * MT], sq_junk[:, 0, :])
            reciprocals(MT, 2 * MT)
            for m in range(MT):
                dve.tensor_scalar(n_tok[:, m, 512:], u_tok[:, m, :], st_r[:, MT + m:MT + m + 1], None, ALU.mult).then_inc(row_ready, 1)

            low_T("mixT", 3, TAPS + 6)

            def add_out(stage):
                for k in range(8):
                    v = x[:, k % MT, (k // MT) * 512:(k // MT + 1) * 512]
                    o = full(stage, k)
                    own(dve.tensor_tensor(v, o, v, ALU.add))
                    own.wait()
                    drained(stage, k, dve.nop())
                dve.nop().then_inc(x_ready, 1)

            add_out("out2")

            dve.wait_ge(mem_in, 48)
            mean_squares([mem[:, m, :] for m in range(MM)], st_ms, x_sq)
            reciprocals(0, MM)
            for m in range(MM):
                own(dve.tensor_scalar(mem[:, m, :], mem[:, m, :], st_r[:, m:m + 1], None, ALU.mult))
                own.wait()
                dve.nop().then_inc(vc_ready, 1)
            own(dve.tensor_scalar(cqn_row, cqn_row, XD ** -0.5, None, ALU.mult))
            norm_rows(n_tok, vc_ready, x_sq)
            dve.wait_ge(xkv_ready, 4)
            for m in range(MM):
                head_squares(xk_tok[:, m, :], XH, XD, st_ms[:, XH * m:XH * (m + 1)], x_sq)
            dve.nop().then_inc(ms_ready, 1)
            reciprocals(0, MM * XH)

            def scale_head(v, col, gain):
                own(dve.scalar_tensor_tensor(out=v, in0=v, scalar=st_r[:, col:col + 1], in1=gain, op0=ALU.mult, op1=ALU.mult))

            for m in range(MM):
                for hd in range(XH):
                    scale_head(xk_tok[:, m, hd * XD:(hd + 1) * XD], m * XH + hd, ckn_row)
            own.wait()
            dve.nop().then_inc(xk_ready, 1)
            low_T("hqT", 4, TAPS + 4)
            for half in range(2):
                dve.wait_ge(xq_in, MT * (half + 1))
                lo = half * 2 * MT
                for m in range(MT):
                    head_squares(xq_tok[:, m, half * 512:(half + 1) * 512], 2, XD, st_ms[:, lo + 2 * m:lo + 2 * m + 2], x_sq[:, 0:512])
                dve.nop().then_inc(ms_ready, 1)
                reciprocals(lo, lo + 2 * MT)
                for m in range(MT):
                    for c in range(2):
                        hd = 2 * half + c
                        scale_head(xq_tok[:, m, hd * XD:(hd + 1) * XD], lo + 2 * m + c, cqn_row)
                own.wait()
                dve.nop().then_inc(xq_ready, 1)
            for m in range(MT):
                for hp in range(2):
                    hd = m * XH + 2 * hp
                    o = full("xs", 2 * m + hp).rearrange("p (a k) -> p a k", a=2)
                    own(dve.tensor_reduce(mx[:, hd:hd + 2], o, AX.X, ALU.max))
                    own.wait()
                    own(dve.tensor_scalar(nmx[:, hd:hd + 2], mx[:, hd:hd + 2], -1.0, None, ALU.mult))
                    own.wait()
                    dve.nop().then_inc(xmax_ready, 1)
            for m in range(MT):
                dve.wait_ge(xq_in, 8 + m + 1)
                own(dve.reciprocal(mx[:, m * XH:(m + 1) * XH], den[:, m * XH:(m + 1) * XH]))
                own.wait()
                for hd in range(XH):
                    v = xp_tok[:, m, hd, :]
                    dve.tensor_scalar(v, v, mx[:, m * XH + hd:m * XH + hd + 1], None, ALU.mult).then_inc(xp_ready, 1)
            low_T("xo", 5, None)
            add_out("xout")

            dve.wait_ge(ffn_in, 16 * (2 + GROUPS))
            own(dve.memset(lg[:, :, GROUPS:8], -3.0e38))
            norm_rows(h3_tok, row_ready, xg, gain=ffn_row)
            o = full("route", 0)[:, 0:MT * (GROUPS + EXPERTS)].rearrange("p (m e) -> p m e", m=MT)
            own(dve.tensor_copy(lg[:, :, 0:GROUPS], o[:, :, 0:GROUPS]))
            own(dve.tensor_copy(lg[:, :, 8:], o[:, :, GROUPS:]))
            own.wait()
            drained("route", 0, dve.nop())
            for m in range(MT):
                own(dve.max(top[:, m, :], lg[:, m, 0:8]))
                own.wait()
                own(dve.max_index(top_i[:, m, :], top[:, m, :], lg[:, m, 0:8]))
                own.wait()
                own(dve.tensor_copy(gidx[:, m:m + 1], top_i[:, m, 0:1]))
                own(dve.tensor_scalar(gexp[:, 4 * m:4 * m + 4], lg[:, m, 0:GROUPS], top[:, m, 0:1], None, ALU.subtract))
                own.wait()
                own(dve.tensor_scalar(goh[:, 4 * m:4 * m + 4], cst("iota")[:, 0:GROUPS], gidx[:, m:m + 1], None, ALU.is_equal))
            own.wait()
            dve.nop().then_inc(gexp_in, 1)
            for g in range(GROUPS):
                for m in range(MT):
                    src, sel = lg[:, m, 8 + 8 * g:16 + 8 * g], goh[:, 4 * m + g:4 * m + g + 1]
                    if g == 0:
                        own(dve.tensor_scalar(loc[:, m, :], src, sel, None, ALU.mult))
                    else:
                        own(dve.scalar_tensor_tensor(out=loc[:, m, :], in0=src, scalar=sel, in1=loc[:, m, :],
                                                     op0=ALU.mult, op1=ALU.add))
                own.wait()
            for m in range(MT):
                own(dve.max(top[:, m, :], loc[:, m, :]))
            own.wait()
            for m in range(MT):
                own(dve.max_index(top_i[:, m, :], top[:, m, :], loc[:, m, :]))
            own(dve.tensor_tensor(dl, top[:, :, 1], top[:, :, 0], ALU.subtract))
            own.wait()
            dve.nop().then_inc(texp_in, 1)
            for q in range(2):
                own(dve.tensor_copy(eid[:, q * MT:(q + 1) * MT], top_i[:, :, q]))
            own.wait()
            for q in range(2):
                own(dve.scalar_tensor_tensor(out=eid[:, q * MT:(q + 1) * MT], in0=gidx, scalar=float(PER_GROUP),
                                             in1=eid[:, q * MT:(q + 1) * MT], op0=ALU.mult, op1=ALU.add))
            own.wait()
            for c in range(2 * MT):
                own(dve.tensor_scalar(oh[:, c, :], cst("iota")[:, 0:EXPERTS], eid[:, c:c + 1], None, ALU.is_equal))
            own.wait()
            for m in range(MT):
                dve.tensor_tensor(ohs[:, m, :], oh[:, m, :], oh[:, MT + m, :], ALU.add).then_inc(oh_ready, 1)
            dve.wait_ge(gexp_ready, 1)
            own(dve.tensor_reduce(gsum, gexp.rearrange("p (m g) -> p m g", g=GROUPS), AX.X, ALU.add))
            dve.wait_ge(texp_ready, 1)
            own(dve.tensor_scalar(tden, dl, 1.0, None, ALU.add))
            own.wait()
            own(dve.tensor_tensor(tden, tden, gsum, ALU.mult))
            own.wait()
            own(dve.reciprocal(w01[:, 0:MT], tden))
            own.wait()
            own(dve.tensor_tensor(w01[:, MT:], w01[:, 0:MT], dl, ALU.mult))
            o = full("route", 1)
            own(dve.tensor_copy(ranks.rearrange("p m e -> p (m e)"), o[:, 0:MT * EXPERTS]))
            own(dve.tensor_copy(cnt, o[:, MT * EXPERTS:(MT + 1) * EXPERTS]))
            own.wait()
            drained("route", 1, dve.nop())
            own(dve.tensor_scalar(nblk, cnt, 0.0, None, ALU.is_gt))
            own.wait()
            for j in range(1, S // SLOTS):
                own(dve.scalar_tensor_tensor(out=nblk, in0=cnt, scalar=float(j * SLOTS), in1=nblk, op0=ALU.is_gt, op1=ALU.add))
                own.wait()
            own(dve.tensor_tensor_scan(incl, cst("ones")[:, 0:EXPERTS], nblk, 0.0, ALU.mult, ALU.add))
            own.wait()
            own(dve.tensor_tensor(bstart, incl, nblk, ALU.subtract))
            own(dve.tensor_scalar(n_steps[:, :], incl[0:1, EXPERTS - 1:EXPERTS], 1.0, None, ALU.add))
            own(dve.tensor_scalar(e_tmp[:, 0, :], incl, cst("token")[:, 0:1], 0.0, ALU.is_le, ALU.add, accum_out=plan_col))
            own.wait()
            own(dve.tensor_scalar(plan_col, plan_col, float(EXPERTS - 1), None, ALU.min))
            own.wait()
            dve.nop().then_inc(plan_col_ready, 1)
            dve.nop().then_inc(plan_ready, 1)
            for m in range(MT):
                own(dve.scalar_tensor_tensor(out=place_e[:, m, :], in0=bstart, scalar=float(SLOTS), in1=ranks[:, m, :],
                                             op0=ALU.mult, op1=ALU.add))
            own.wait()
            for q in range(2):
                own(dve.tensor_tensor(e_tmp[:, q * MT:(q + 1) * MT, :], oh[:, q * MT:(q + 1) * MT, :], place_e, ALU.mult))
            own.wait()
            own(dve.tensor_reduce(destf, e_tmp, AX.X, ALU.add))
            own.wait()
            own(dve.tensor_copy(dest_i[:, 0, :], destf))
            own(dve.tensor_scalar(dest_i[:, 3, :], destf, float(2 * SLOTS), None, ALU.add))
            own.wait()
            own(dve.tensor_scalar(dest_i[:, 1, :], dest_i[:, 0, :], SLOTS.bit_length() - 1, None, ALU.logical_shift_right))
            own(dve.tensor_scalar(dest_i[:, 2, :], dest_i[:, 0, :], SLOTS - 1, None, ALU.bitwise_and))
            own.wait()
            own(dve.tensor_copy(blkf, dest_i[:, 1, :]))
            own(dve.tensor_copy(inf_, dest_i[:, 2, :]))
            own.wait()
            for c in range(2 * MT):
                own(dve.tensor_scalar(slot_oh[:, c, :], cst("iota")[:, 0:SLOTS], inf_[:, c:c + 1], None, ALU.is_equal))
                own(dve.tensor_scalar(block_oh[:, c, :], cst("iota"), blkf[:, c:c + 1],
                                      cst("token")[:, c % MT:c % MT + 1], ALU.is_equal, ALU.mult))
            own.wait()
            dve.nop().then_inc(slot_oh_ready, 1)
            own(dve.memset(plan_row[:, 0:1], 0))
            own(dve.tensor_copy(plan_row[:, 1:], full("route", 2)[0:1, 0:P]))
            own.wait()
            drained("route", 2, dve.nop())
            dve.nop().then_inc(plan_ready, 1)
            own(dve.tensor_copy(slot_tok[:, :], full("route", 3)[0:SLOTS, 0:64]))
            own.wait()
            drained("route", 3, dve.nop())
            dve.nop().then_inc(slots_ready, 1)

            steps = dve.snap(dve.value_load(n_steps[0:1, 0:1], min_val=2, max_val=MAX_BLOCKS + 1))
            moe = Chain(dve, dve_moe)

            def low(n, b):
                dve.wait_ge(piece_hi, b * 12 + (n + 1))
                dve.tensor_tensor(parts[:, n % 4, 1, :], ring[:, n // 4, n % 4 * 1024:(n % 4 + 1) * 1024],
                                  parts[:, n % 4, 0, :].bitcast(F32), ALU.subtract).then_inc(piece_split[n], 1)

            def rest(stage, k, dst, o, i=0):
                n = dst.shape[2] * dst.shape[3]
                d = [dst[:, h].rearrange("p t n -> p (t n)") for h in range(2)]
                drained(stage, k, dve.tensor_tensor(d[1], o[:, 0:n], d[0].bitcast(F32), ALU.subtract))

            for n in range(12):
                dve.nop().then_inc(piece_split[n], 1)
            dve.wait_ge(xgT_hi, 1)
            rest("moe0", 0, xgT, full("moe0", 0))
            with dve.Fori(0, steps) as b:
                moe.enter(b, 2)
                for n in (0, 1, 2):
                    low(n, b)
                dve.wait_ge(hidT_hi, b + 1)
                rest("moe", 3, hidT, ps[:, banks["moe"].place(3), :])
                for n in (4, 5, 6):
                    low(n, b)
                dve.wait_ge(sg_h_ready, b + 1)
                moe(dve.tensor_tensor(t_h[0:SLOTS, :], full("moe", 1, b)[0:SLOTS, :], sg_h[0:SLOTS, :], ALU.mult))
                moe.wait()
                drained("moe", 1, dve.nop())
                for n in (8, 9, 10):
                    low(n, b)
                moe(dve.tensor_tensor(hid[0:SLOTS, :], full("moe", 2, b)[0:SLOTS, :], t_h[0:SLOTS, :], ALU.mult))
                moe.wait()
                drained("moe", 2, dve.nop())
                dve.nop().then_inc(hid_ready, 1)
                o = full("moe", 0, b)
                dve.wait_ge(xgT_hi, b + 2)
                rest("moe", 0, xgT, o, b)
            moe.leave(None)
            for c in range(2 * MT):
                q, m = c % 2, c // 2
                dve.wait_ge(combo_in[c % 4], 16 * (c // 4 + 1))
                if q:
                    dve.wait_ge(combo_used, c)
                ins = dve.scalar_tensor_tensor(out=x[:, m, :], in0=combo[:, c % 4, :], scalar=w01[:, q * MT + m:q * MT + m + 1],
                                               in1=x[:, m, :], op0=ALU.mult, op1=ALU.add)
                ins.then_inc(combo_used, 1)
                if q:
                    dve.wait_ge(combo_used, c + 1)
                    dve.nop().then_inc(x_ready, 1)

        @block.gpsimd
        def _(pool):
            own = Chain(pool, pool_own)
            one = cst("ones")[:, 0:1].to_broadcast([P, 1024])

            def split_chunk(stage, j, first, n, i=0):
                st, pc = chunks[stage], pieces[stage]
                pool.wait_ge(weights_landed[st.place(j)], (st.before(j, i) + 1) * 32)
                for k in range(n):
                    q = pc.place(first + k)
                    w = ring[:, st.place(j), k * 1024:(k + 1) * 1024]
                    pool.wait_ge(piece_used[q], pc.before(first + k, i) + 1)
                    own(pool.tensor_tensor(parts[:, q, 0, :], w, one, ALU.mult))
                    own.wait()
                    pool.tensor_tensor(parts[:, q, 1, :], w, parts[:, q, 0, :].bitcast(F32),
                                       ALU.subtract).then_inc(dense_split[q], 1)
                pool.wait_ge(dense_split[q], pc.before(first + n - 1, i) + 1)
                pool.nop().then_inc(weights_used[st.place(j)], 1)

            pool.wait_ge(const_in, 16)
            with pool.Fori(0, KT) as i:
                own.enter(i, 5)
                for j, (first, n) in enumerate(((0, 2), (2, 2), (4, 1))):
                    split_chunk("conv", j, first, n, i)
            own.leave(KT)
            split_chunk("qk0", 0, 0, 4)
            with pool.Fori(0, HEADS - 1) as h:
                own.enter(h, 12)
                for j in range(3):
                    split_chunk("heads", j, 4 * j, 4, h)
            own.leave(HEADS - 1)
            pool.wait_ge(gated_conv_ready, KT)
            pool.memset(zeros, 0.0).then_inc(zero_ready, 1)
            for j in range(2):
                split_chunk("head_last", j, 4 * j, 4)
            for j, (first, n) in enumerate(((0, 4), (4, 2), (6, 4), (10, 4))):
                split_chunk("in2", j, first, n)
            for stage in ("out2", "xq", "xout"):
                for j in range(2):
                    split_chunk(stage, j, 4 * j, 4)

            pool.wait_ge(h3_stored, 16)
            pool.wait_ge(slots_ready, 1)
            steps = pool.snap(pool.value_load(n_steps[0:1, 0:1], min_val=2, max_val=MAX_BLOCKS + 1))

            def gather(b):
                pool.tensor_copy(idx[:, :], slot_tok[:, bass.ds(b, 1)]).then_inc(idx_ready, 1)
                pool.wait_ge(idx_ready, b + 1)
                pool.nop().then_inc(idx_settled, 1)
                pool.indirect_dma_start(xg[0:SLOTS, :], None, h3_rows,
                                        bass.IndirectOffsetOnAxis(ap=idx[:, 0:1], axis=0)).then_inc(xg_in, 16)

            gather(0)
            with pool.Fori(0, steps) as b:
                st = banks["moe"]
                pool.wait_ge(bank_filled[st.place(0)], st.before(0, b))
                gather(b + 1)
                for n in (3, 7, 11):
                    pool.wait_ge(piece_hi, b * 12 + (n + 1))
                    pool.tensor_tensor(parts[:, n % 4, 1, :], ring[:, n // 4, n % 4 * 1024:(n % 4 + 1) * 1024],
                                       parts[:, n % 4, 0, :].bitcast(F32), ALU.subtract).then_inc(piece_split[n], 1)
            pool.wait_ge(y_blk_ready, 1)
            for c in range(2 * MT):
                q, m = c % 2, c // 2
                if c >= 4:
                    pool.wait_ge(combo_used, c - 3)
                pool.indirect_dma_start(combo[:, c % 4, :], None, y_rows, bass.IndirectOffsetOnAxis(
                    ap=dest_i[:, 3, q * MT + m:q * MT + m + 1].bitcast(U32), axis=0)).then_inc(combo_in[c % 4], 16)


_INS = ["x", "c", "positions", "w_ada", "b_ada", "pre_norm_g", "w_in", "conv_w", "conv_b", "conv_ln_g", "conv_ln_b",
        "w_ret_out", "w_conv_out", "w_out", "post_norm_g", "mem_2", "norm_mix_2", "w_in_2", "q_norm_2", "k_norm_2",
        "attn_sinks_2", "sgu_norm_2", "sgu_w_2", "sgu_b_2", "out_norm_attn_2", "out_norm_sgu_2", "w_out_2",
        "norm_cross_2", "norm_mem_2", "w_cq_2", "w_ck_2", "w_cv_2", "cq_norm_2", "ck_norm_2", "w_co_2", "norm_ffn_2",
        "w_router_group_2", "w_router_expert_2", "w1_2", "w3_2", "w2_2"]


def kernel(**inputs):
    import concourse.bacc as _bacc
    from concourse.bass_utils import run_bass_kernel_spmd as _run

    nc = _bacc.Bacc("TRN2", target_bir_lowering=False, num_devices=1)
    arrays = {name: np.ascontiguousarray(inputs[name]) for name in _INS}
    arrays["const"], arrays["decay"] = const_table(), decay_table()
    args = {name: nc.dram_tensor(f"in_{name}", v.shape, mybir.dt.from_np(v.dtype), kind="ExternalInput").ap()
            for name, v in arrays.items()}
    out = nc.dram_tensor("out_0", (1, S, D), F32, kind="ExternalOutput").ap()
    build(nc, args, out)
    r = _run(nc, [{f"in_{k}": v for k, v in arrays.items()}], core_ids=[0])
    return r.results[0]["out_0"]
```

```python
from contextlib import ExitStack

import concourse.bass as bass
import numpy as np
from concourse import mybir

P = 128
S = 512
D = 1024
MT = S // P
KT = D // P
HEADS, HQK, HV = 4, 256, 512
TAPS = 31
WIN_COLS = (1024, 1024, 2048, 2048, 1024, 1024, 1024, 1024, 1024)
OFF_Q, OFF_K, OFF_V, OFF_Z, OFF_UV, OFF_UG, OFF_ZC, OFF_GA, OFF_GB = [
    sum(WIN_COLS[:n]) for n in range(len(WIN_COLS))]
MEM, MM = 256, 2
AH, AD = 8, 64
XH, XD = 4, 256
GROUPS, PER_GROUP = 4, 8
EXPERTS, FF = GROUPS * PER_GROUP, 512
SLOTS = 64
MAX_BLOCKS = EXPERTS + (2 * S - 1) // SLOTS + 1
RMS_EPS, GN_EPS, LN_EPS = 1e-6, 1e-5, 1e-5
NEG = -1e30
ARENA = 21740

F32 = mybir.dt.float32
F32R = mybir.dt.float32r
BF16 = mybir.dt.bfloat16
I32 = mybir.dt.int32
U32 = mybir.dt.uint32
ACT = mybir.ActivationFunctionType
ALU = mybir.AluOpType
AX = mybir.AxisListType

CONSTS = {}


def const_table():
    p = np.arange(P)
    inv_freq = (np.float32(10000.0) ** (-np.arange(HQK // 2, dtype=np.float32) / np.float32(HQK // 2)))
    dist = p[:, None] + P - np.arange(2 * P)[None, :]
    band = np.where((dist >= 0) & (dist < P), 0.0, NEG)
    first = np.where(np.arange(2 * P)[None, :] >= P, band, NEG)
    parts = [
        ("ident", np.eye(P)),
        ("before", (p[:, None] < p[None, :])),
        ("causalT", (p[:, None] <= p[None, :])),
        ("ones", np.ones((P, P))),
        ("mean", np.full((P, P), 1.0 / D)),
        ("iota", np.broadcast_to(np.arange(64), (P, 64))),
        ("first_blocks", np.where(p < EXPERTS, p, 0)[:, None]),
        ("token", p[:, None] + P * np.arange(MT)[None, :]),
        ("band", band),
        ("first", first),
        ("freq", inv_freq[:, None]),
    ]
    at = 0
    for name, a in parts:
        CONSTS[name] = (at, at + a.shape[1])
        at += a.shape[1]
    return np.concatenate([np.asarray(a, np.float32) for _, a in parts], axis=1)


def decay_table():
    log_g = np.log1p(-np.exp2(-5.0 - np.arange(HEADS)))
    diff = np.arange(S)[None, :] - np.arange(P)[:, None]
    d = np.where(diff >= 0, np.exp(log_g[:, None, None] * np.maximum(diff, 0)), 0.0)
    return (d * HQK ** -0.5).astype(np.float32)


const_table()


class Stage:

    def __init__(self, base, uses):
        self.base = list(base)
        self.places = [k % len(base) for k in range(uses)] if isinstance(uses, int) else list(uses)
        self.per = [self.places.count(b) for b in range(len(base))]

    def place(self, k):
        return self.places[k]

    def before(self, k, i=0):
        b = self.places[k]
        return i * self.per[b] + (self.base[b] + self.places[:k].count(b))


def stages(n, plan):
    base, out = [0] * n, {}
    for name, uses, steps in plan:
        out[name] = st = Stage(base, uses)
        base = [b + steps * p for b, p in zip(base, st.per)]
    return out


class Chain:

    def __init__(self, eng, sem):
        self.eng, self.sem, self.base, self.count = eng, sem, 0, 0

    def __call__(self, instruction):
        instruction.then_inc(self.sem, 1)
        self.count += 1

    def wait(self, but=0):
        self.eng.wait_ge(self.sem, self.base + (self.count - but))

    def enter(self, i, per):
        self.at, self.per = self.base + self.count, per
        self.base, self.count = i * per + self.at, 0

    def leave(self, steps):
        assert self.count == self.per, (self.count, self.per)
        self.base, self.count = (self.at + self.per * steps, 0) if steps else (None, 0)


def from_bank(first, uses):
    return [(first + k) % 7 for k in range(uses)]


BANK_PLAN = [
    ("ada", 6, 1), ("columns", 1, 1), ("hT", KT, 1), ("conv", from_bank(1, 5), KT),
    ("qk0", (6, 0, 3, 4), 1), ("ln", (1, 2), 1), ("heads", 24, HEADS - 1), ("head_last", 20, 1), ("mix0", 8, 1), ("mix1", 8, 1), ("mix2", 8, 1),
    ("out", 8, 1),
    ("h2T", KT, 1), ("in2", from_bank(1, 16), 1), ("qkT", 5, 1), ("sguw", 2, 1), ("attn0", 4, 1),
    ("sgu", from_bank(4, 4), 1), ("attn", MT * 9 - 4, 1),
    ("mixT", KT, 1), ("out2", from_bank(1, 8), 1),
    ("memT", 4, 1), ("xk", 4, 1), ("xv", 4, 1), ("hqT", KT, 1), ("xkT", from_bank(1, 4), 1), ("xq", from_bank(5, 8), 1), ("xqT", KT, 1),
    ("xs", 8, 1), ("xpT", 8, 1), ("xo", from_bank(1, 8), 1), ("xout", from_bank(2, 8), 1),
    ("h3T", KT, 1), ("route", from_bank(1, 4), 1), ("moe0", (0,), 1), ("moe_first", 4, 1),
    ("moe", 6, 1),
]
CHUNK_PLAN = [
    ("ada", 6, 1), ("conv", 3, KT), ("qk0", 1, 1), ("heads", (1, 2, 0), HEADS - 1), ("head_last", (1, 2), 1),
    ("mix", 6, 1), ("out", 2, 1), ("in2", 4, 1),
    ("out2", 2, 1), ("xk", 2, 1), ("xv", 2, 1), ("xq", 2, 1), ("xout", 2, 1), ("moe", 3, 1),
]
PIECE_PLAN = [
    ("conv", (0, 1, 2, 3, 1), KT), ("qk0", 4, 1), ("heads", 12, HEADS - 1), ("head_last", 8, 1), ("mix", 24, 1), ("in2", 14, 1), ("out2", 8, 1), ("xq", 8, 1),
    ("xout", 8, 1), ("moe_first", 8, 1), ("moe", 12, 1),
]


def build(nc, a, out):
    banks, chunks, pieces = stages(7, BANK_PLAN), stages(3, CHUNK_PLAN), stages(4, PIECE_PLAN)
    ctx = ExitStack()
    with ctx:
        def sb(name, shape, dt=F32):
            return ctx.enter_context(nc.sbuf_tensor(name, shape, dt))

        def sem(name):
            return ctx.enter_context(nc.semaphore(name))

        ring = sb("ring", [P, 3, 4096])
        const = sb("const", [P, CONSTS["freq"][1]])
        cols = sb("cols", [P, KT, TAPS + 3 + 4])
        sgub = sb("sgub", [P, 8])
        act_parts = sb("act_parts", [P, 2 * KT * S], F32R)
        actT = act_parts[:, :].rearrange("p (h t n) -> p h t n", h=2, t=KT)
        xgT = act_parts[:, 0:2 * KT * SLOTS].rearrange("p (h t n) -> p h t n", h=2, t=KT)
        hidT = act_parts[:, 2 * KT * SLOTS:2 * (KT + 4) * SLOTS].rearrange("p (h t n) -> p h t n", h=2, t=4)
        parts = sb("parts", [P, 4, 2, 1024], F32R)
        small = sb("small", [P, 512])
        arena = sb("arena", [P, ARENA])

        def cst(name, parts=P):
            lo, hi = CONSTS[name]
            return const[0:parts, lo:hi]

        ident = cst("ident")
        taken = [0]

        def carve(shape, at=None):
            n = int(np.prod(shape))
            lo = taken[0] if at is None else at
            assert lo + n <= ARENA, (lo, n)
            if at is None:
                taken[0] = lo + n
            v = arena[:, lo:lo + n]
            if len(shape) == 2:
                v = v.rearrange("p (a b) -> p a b", a=shape[0])
            if len(shape) == 3:
                v = v.rearrange("p (a b c) -> p a b c", a=shape[0], b=shape[1])
            return v

        def mini(lo, n):
            return small[:, lo:lo + n]

        gate_post = carve([D])
        cosT, sinT = carve([S]), carve([S])
        convT = carve([KT, S])
        zconvT = carve([KT, S])
        first_free = taken[0]
        taken[0] = D + 2 * S
        colrows = carve([D])[0:TAPS + 3 + 4, :]
        sgub_rows = carve([P])[0:8, :]
        pos_i = carve([S]).bitcast(I32)
        x0 = carve([MT, D])
        h0 = carve([MT, D])
        mod_scale, mod_shift = carve([D]), carve([D])
        pre_g, post_g = carve([D]), carve([D])
        c_rep = carve([KT, P])
        bada = carve([3 * D])
        angle, turns = carve([S]), carve([S])
        taken[0] = first_free
        apad = carve([TAPS - 1 + S])
        conv_acc = carve([2, S])
        sig_u, sig_z = carve([S]), carve([S])
        ln_sq = carve([2, S])
        ln_rstd, ln_std = carve([S]), carve([S])
        ln_y = carve([2, S])
        ln_s = carve([2, S])
        sig_g = carve([2, S])
        taken[0] = first_free - 2 * KT * S
        retT = carve([16, S])
        qk_rot = carve([4, S])
        v_tok = carve([MT, HV])
        z_tok = carve([MT, HV])
        decayed = carve([MT, S])
        rot = decayed
        sig_r = carve([2, S])
        norm_o = sig_r
        decay = carve([S])
        zeros = carve([D])
        taken[0] = first_free
        conv_backT = carve([KT, S])
        mergedT = carve([KT, S])
        gates = carve([4, S])
        part_b = carve([S])
        x = carve([MT, D], at=ARENA - MT * D)
        y_tok = carve([MT, D], at=first_free)
        x0_early = carve([D], at=MT * D)
        squares = carve([D], at=MT * D + D)
        OUT_TILES = (1, 2, 3, 0)

        taken[0] = 0
        n_tok = carve([MT, D])
        sq_junk = carve([MT, 512])
        q_tok = carve([MT, 512])
        kv_tok = carve([MT, 256])
        u_tok = carve([MT, 512])
        g_tok = carve([MT, 512])
        attn_tok = carve([MT, 512])
        q_pair = attn_tok
        second_free = taken[0]
        qT = carve([4, S])
        kT = carve([P + S], at=2 * D)
        s_tok = [carve([AH, 2 * P], at=MT * D), carve([AH, 2 * P], at=0)]
        pT = carve([2 * AH, P], at=MT * D + MT * 512)
        sgu_junk = ring[:, 2, 16 * P:20 * P]
        sgu_w = ring[:, 2, 0:8 * P].rearrange("p (g n) -> p g n", g=8)
        sgu_wT = ring[:, 2, 8 * P:16 * P].rearrange("p (g n) -> p g n", g=8)
        gain_rows = carve([AD + AD + 512 + 8], at=2 * D + P + S)
        qn_row, kn_row = gain_rows[:, 0:AD], gain_rows[:, AD:2 * AD]
        sgun_row, sink_row = gain_rows[:, 2 * AD:2 * AD + 512], gain_rows[:, 2 * AD + 512:]
        assert second_free + 4 * S <= ARENA - MT * D
        taken[0] = MT * D
        mem = carve([MM, D])
        memT = carve([KT, MEM])
        xv_tok = carve([MM, D])
        xk_tok = carve([MM, D])
        xkT = carve([KT, MEM])
        cqn_row, ckn_row = carve([XD]), carve([XD])
        x_sq = carve([D])
        assert taken[0] <= ARENA - MT * D
        xq_tok = carve([MT, D], at=MT * D)
        xqT = carve([KT, S], at=0)
        xp_tok = carve([MT, XH, MEM], at=MT * D)
        xpT = carve([KT, S], at=MT * D + 6 * D)
        h3_tok = carve([MT, D], at=0)
        taken[0] = MT * D + 10 * D + 2 * XD + D
        ffn_row = carve([D])
        wr = carve([KT, GROUPS + EXPERTS])
        assert taken[0] <= ARENA - MT * D
        taken[0] = MT * D
        lg = carve([MT, 40])
        oh = carve([2 * MT, EXPERTS])
        ohs = carve([MT, EXPERTS])
        oh_before = carve([MT + 1, EXPERTS])
        loc = carve([MT, 8])
        top = carve([MT, 8])
        ranks = carve([MT, EXPERTS])
        place_e = carve([MT, EXPERTS])
        e_tmp = carve([2 * MT, EXPERTS])
        slot_oh = carve([2 * MT, SLOTS])
        block_oh = carve([2 * MT, 64])
        expert_free = taken[0]
        h3T = carve([KT, S], at=expert_free)
        xg = carve([D])
        sg_h, t_h, hid = carve([FF]), carve([FF]), carve([FF])
        y_blk = carve([D])
        taken[0] = expert_free + KT * S
        combo = carve([4, D])
        assert taken[0] <= MT * D + 10 * D + 2 * XD + D
        assert taken[0] <= ARENA - MT * D
        top_i = sb("top_i", [P, MT, 8], U32)
        dest_i = sb("dest_i", [P, 3, 2 * MT], I32)
        mark_src = sb("mark_src", [P, P], BF16)
        slot_tok = sb("slot_tok", [SLOTS, 64], U32)
        idx = sb("idx", [SLOTS, 1], U32)
        plan_row = sb("plan_row", [1, P], I32)
        n_steps = sb("n_steps", [1, 1], I32)
        conv_dram = nc.dram_tensor("conv_dram", [P, KT, S], F32).ap()
        gates_dram = nc.dram_tensor("gates_dram", [KT, P, 2, S], F32).ap()
        h3_rows = nc.dram_tensor("h3_rows", [S, D], F32).ap()
        y_rows = nc.dram_tensor("y_rows", [MAX_BLOCKS * SLOTS, D], F32).ap()

        ps = ctx.enter_context(nc.psum_tensor("ps", [P, 8, 512], F32))

        bank_filled = [sem(f"bank{b}_filled") for b in range(7)]
        bank_drained = [sem(f"bank{b}_drained") for b in range(7)]
        weights_landed = [sem(f"weights{s}_landed") for s in range(3)]
        weights_used = [sem(f"weights{s}_used") for s in range(3)]
        const_in, cols_in, x_in, c_in, pos_in, rows_in = (sem(n) for n in (
            "const_in", "cols_in", "x_in", "c_in", "pos_in", "rows_in"))
        c_rep_ready, h0_ready = sem("c_rep_ready"), sem("h0_ready")
        act_own, dve_own, dve_moe = (sem(n) for n in ("act_own", "dve_own", "dve_moe"))
        sig_u_ready, sig_z_ready = sem("sig_u_ready"), sem("sig_z_ready")
        angles_ready, rotary_ready = sem("angles_ready"), sem("rotary_ready")
        conv_ready, sq_ready, sq_used, cen_ready = (sem(n) for n in (
            "conv_ready", "ln_sq_ready", "ln_sq_used", "centred"))
        ln_std_ready, ln_y_ready, ln_s_ready, gated_conv_ready = (sem(n) for n in (
            "ln_std_ready", "ln_y_ready", "ln_s_ready", "gated_conv_ready"))
        decay_in, decay_used = sem("decay_in"), sem("decay_used")
        qk_ready, v_ready, sig_r_ready, sig_r_used = (sem(n) for n in (
            "qk_ready", "v_ready", "sig_r_ready", "sig_r_used"))
        decayed_ready, var_ready, std_ready, ret_ready, retT_ready = (sem(n) for n in (
            "decayed_ready", "var_ready", "std_ready", "ret_ready", "retT_ready"))
        gates_stored, gates_in, gates_used, merged_ready = (sem(n) for n in (
            "gates_stored", "gates_in", "gates_used", "merged_ready"))
        y_ready, ms_ready, rms_ready, x_ready = (sem(n) for n in ("y_ready", "ms_ready", "rms_ready", "x_ready"))
        x_back, gains_in, x_tile_ready = sem("x_back"), sem("gains_in"), sem("x_tile_ready")
        row_ready, in2_ready, qk2_ready, qkT_ready = (sem(n) for n in (
            "rows_ready", "in2_ready", "qk2_ready", "qkT_ready"))
        smax_ready, p_ready, pT_ready = (sem(n) for n in ("smax_ready", "p_ready", "pT_ready"))
        sguw_in, sguwT_ready, vc_ready, actT_ready = (sem(n) for n in (
            "sguw_in", "sguwT_ready", "vc_ready", "actT_ready"))
        mem_in, memT_ready, xkv_ready, xk_ready, xkT_ready = (sem(n) for n in (
            "mem_in", "memT_ready", "xkv_ready", "xk_ready", "xkT_ready"))
        xq_in, xq_ready, xqT_ready, xmax_ready, sink_exp, xp_ready, xpT_ready = (sem(n) for n in (
            "xq_in", "xq_ready", "xqT_ready", "xmax_ready", "sink_exp", "xp_ready", "xpT_ready"))
        ffn_in, h3_stored, gexp_in, gexp_ready, texp_in, texp_ready = (sem(n) for n in (
            "ffn_in", "h3_stored", "gexp_in", "gexp_ready", "texp_in", "texp_ready"))
        oh_ready, plan_col_ready, slot_oh_ready, plan_ready, slots_ready = (sem(n) for n in (
            "oh_ready", "plan_col_ready", "slot_oh_ready", "plan_ready", "slots_ready"))
        idx_ready, xg_in, xgT_hi, sg_h_ready, hid_ready, hidT_hi, y_blk_ready, y_stored = (sem(n) for n in (
            "idx_ready", "xg_in", "xgT_hi_ready", "sg_h_ready", "hid_ready", "hidT_hi_ready", "y_blk_ready", "y_stored"))
        half_landed = [sem(f"expert_half{n}_landed") for n in range(6)]
        piece_hi = sem("piece_hi_ready")
        piece_split = [sem(f"piece{n}_split") for n in range(12)]
        piece_used = [sem(f"parts{n}_used") for n in range(4)]
        dense_split = [sem(f"dense_piece{n}_split") for n in range(4)]
        pool_own, actT_hi, h3T_ready = sem("pool_own"), sem("actT_hi_ready"), sem("h3T_ready")
        conv_stored, conv_back = sem("conv_stored"), sem("conv_back")
        combo_in = [sem(f"combo{n}_in") for n in range(4)]
        stats_settled, turn_may_start, idx_settled = (sem(n) for n in ("stats_settled", "turn_may_start", "idx_settled"))
        zero_ready, y_cleared = sem("zero_ready"), sem("y_cleared")
        combo_used, out_done = sem("combo_used"), sem("out_done")

        st_ms, st_rms, st_r = mini(0, 32), mini(32, 32), mini(64, 32)
        bn6, mv, st_std = mini(96, 24), mini(120, 8), mini(128, 4)
        gn_r = mini(132, 4)
        mx, nmx, den = mini(136, 32), mini(168, 32), mini(200, 32)
        eps = mini(240, 3)
        gidx, gsum, gmax = mini(248, 4), mini(252, 4), mini(256, 4)
        gexp = mini(260, 16)
        goh = mini(284, 16)
        eid, dl, w01, tden = mini(300, 8), mini(308, 4), mini(312, 8), mini(320, 4)
        cnt, nblk, incl, bstart = mini(324, 32), mini(356, 32), mini(388, 32), mini(420, 32)
        destf, blkf, inf_ = mini(452, 8), mini(460, 8), mini(468, 8)
        plan_col = mini(476, 1)
        c_col = mini(480, 8)

        def tiles(w):
            return w.rearrange("(t p) n -> p t n", p=P)

        def row(v, n=None):
            return v.rearrange("(o n) -> o n", o=1)

        def score_use(n):
            return ("attn0", 0) if n == 0 else ("attn", 9 * (n - 1))

        def weight_use(n):
            return 9 * n + (4 if n < MT - 1 else 0)

        x_v = a["x"][0].rearrange("(m p) d -> p m d", p=P)
        out_v = out[0].rearrange("(m p) d -> p m d", p=P)
        w_in = tiles(a["w_in"][0])
        w_ada = a["w_ada"][0].rearrange("(p t) n -> p t n", t=KT)

        block = ctx.enter_context(nc.Block())

        @block.sync
        def _(sp):
            def chunk(stage, j, halves, i=0):
                st = chunks[stage]
                s, n = st.place(j), st.before(j, i)
                if not (isinstance(n, int) and n == 0):
                    sp.wait_ge(weights_used[s], n)
                for dst, src in halves(ring[:, s, :]):
                    sp.dma_start(dst, src).then_inc(weights_landed[s], 16)

            def pair(r, src):
                k, n = src.shape[1], src.shape[2]
                v = r[:, 0:k * n].rearrange("p (k n) -> p k n", k=k)
                return [(v[:, 0:k // 2, :], src[:, 0:k // 2, :]), (v[:, k // 2:k, :], src[:, k // 2:k, :])]

            def both(r, one, two):
                k, n = one.shape[1], one.shape[2]
                v = r[:, 0:2 * k * n].rearrange("p (w k n) -> p w k n", w=2, k=k)
                return [(v[:, 0], one), (v[:, 1], two)]

            sp.dma_start(c_col, a["c"][0].rearrange("(p t) -> p t", t=KT)).then_inc(c_in, 16)
            sp.dma_start(const[:, :], a["const"]).then_inc(const_in, 16)
            sp.dma_start(bada[0:1, :], a["b_ada"]).then_inc(c_in, 16)
            GROUP_ORDER = (2, 3, 0, 1, 4, 5)

            def ada(j):
                g = GROUP_ORDER[j]
                chunk("ada", j, lambda r: pair(r, w_ada[:, :, g * 512:(g + 1) * 512]))

            ada(0)
            sp.dma_start(pre_g, a["pre_norm_g"].partition_broadcast(P)).then_inc(rows_in, 16)
            sp.dma_start(post_g, a["post_norm_g"].partition_broadcast(P)).then_inc(rows_in, 16)
            ada(1)
            sp.dma_start(x0, x_v).then_inc(x_in, 16)
            ada(2)
            sp.dma_start(pos_i[:, :], a["positions"].partition_broadcast(P)).then_inc(pos_in, 16)
            per_feature = [a["conv_w"][0], a["conv_b"], a["conv_ln_g"], a["conv_ln_b"], row(a["norm_mix_2"]),
                           row(a["norm_cross_2"]), row(a["norm_mem_2"])]
            at = 0
            for v in per_feature:
                sp.dma_start(colrows[at:at + v.shape[0], :], v).then_inc(cols_in, 16)
                at += v.shape[0]
            sp.dma_start(colrows[at:at + 1, 0:512], row(a["out_norm_attn_2"])).then_inc(cols_in, 16)
            sp.dma_start(colrows[at:at + 1, 512:], row(a["out_norm_sgu_2"])).then_inc(cols_in, 16)
            sp.dma_start(sgub_rows[:, :], a["sgu_b_2"]).then_inc(cols_in, 16)
            for j in range(3, 6):
                ada(j)

            with sp.Fori(0, KT) as t:
                def columns(off):
                    return w_in[:, :, bass.ds(off + t * P, P)]
                chunk("conv", 0, lambda r: both(r, columns(OFF_UV), columns(OFF_UG)), t)
                chunk("conv", 1, lambda r: both(r, columns(OFF_GA), columns(OFF_GB)), t)
                chunk("conv", 2, lambda r: pair(r, columns(OFF_ZC)), t)
            def head_qk(stage, j, h, i=0):
                def qk(r):
                    v = r.rearrange("p (k n) -> p k n", k=KT)
                    return [(v[:, :, 0:HQK], w_in[:, :, bass.ds(OFF_Q + h * HQK, HQK)]),
                            (v[:, :, HQK:], w_in[:, :, bass.ds(OFF_K + h * HQK, HQK)])]
                chunk(stage, j, qk, i)

            def head_vz(stage, h, i=0):
                chunk(stage, 0, lambda r: pair(r, w_in[:, :, bass.ds(OFF_V + h * HV, HV)]), i)
                chunk(stage, 1, lambda r: pair(r, w_in[:, :, bass.ds(OFF_Z + h * HV, HV)]), i)
                sp.wait_ge(decay_used, (h + 1) * MT)
                sp.wait_ge(gated_conv_ready, KT)
                sp.dma_start(decay, a["decay"][bass.ds(h, 1), :, :].rearrange("o p n -> p (o n)")).then_inc(decay_in, 16)

            head_qk("qk0", 0, 0)
            with sp.Fori(0, HEADS - 1) as h:
                head_vz("heads", h, h)
                head_qk("heads", 2, h + 1, h)
            head_vz("head_last", HEADS - 1)
            sp.wait_ge(zero_ready, 1)
            sp.dma_start(y_rows.rearrange("(k p) d -> p k d", p=P),
                         zeros.unsqueeze(1).to_broadcast([P, MAX_BLOCKS * SLOTS // P, D])).then_inc(y_cleared, 16)
            w_ret, w_conv = tiles(a["w_ret_out"][0]), tiles(a["w_conv_out"][0])
            def mix_chunk(j):
                src = (w_ret[:, 0:KT], w_ret[:, KT:], w_conv)[j // 2]
                chunk("mix", j, lambda r: pair(r, src[:, :, j % 2 * 512:(j % 2 + 1) * 512]))

            def mix_gates(j):
                if j:
                    sp.wait_ge(gates_used, j)
                sp.dma_start(gates, gates_dram[j % 2 * 4:j % 2 * 4 + 4, :, j // 2, :].rearrange("t p n -> p t n")).then_inc(gates_in, 16)

            for j in range(3):
                mix_chunk(j)
            sp.wait_ge(gates_stored, (KT + 1) * 16)
            sp.wait_ge(y_cleared, 16)
            sp.wait_ge(retT_ready, HEADS * 4)
            mix_gates(0)
            mix_chunk(3)
            mix_gates(1)
            for j in (4, 5):
                mix_chunk(j)
            for j in (2, 3):
                mix_gates(j)

            def project(stage, w, widths=None):
                at = 0
                for j, n in enumerate(widths or [512] * (w.shape[2] // 512)):
                    chunk(stage, j, lambda r: pair(r, w[:, :, at:at + n]))
                    at += n

            project("out", tiles(a["w_out"][0]))
            project("in2", tiles(a["w_in_2"]), (512, 256, 512, 512))
            sp.wait_ge(actT_ready, 5 * KT)
            for dst, v in ((qn_row, "q_norm_2"), (kn_row, "k_norm_2"), (sgun_row, "sgu_norm_2"), (sink_row, "attn_sinks_2")):
                sp.dma_start(dst, row(a[v]).partition_broadcast(P)).then_inc(gains_in, 16)
            sp.wait_ge(weights_used[2], chunks["moe"].before(2))
            sp.dma_start(sgu_w, a["sgu_w_2"].rearrange("g i j -> i g j")).then_inc(sguw_in, 16)
            project("out2", tiles(a["w_out_2"]))
            sp.wait_ge(actT_ready, 6 * KT)
            sp.dma_start(mem, a["mem_2"][0].rearrange("(m p) d -> p m d", p=P)).then_inc(mem_in, 16)
            for dst, v in ((cqn_row, "cq_norm_2"), (ckn_row, "ck_norm_2")):
                sp.dma_start(dst, row(a[v]).partition_broadcast(P)).then_inc(mem_in, 16)
            sp.dma_start(ffn_row, row(a["norm_ffn_2"]).partition_broadcast(P)).then_inc(ffn_in, 16)
            sp.dma_start(wr[:, :, 0:GROUPS], tiles(a["w_router_group_2"])).then_inc(ffn_in, 16)
            for g in range(GROUPS):
                lo = GROUPS + g * PER_GROUP
                sp.dma_start(wr[:, :, lo:lo + PER_GROUP], tiles(a["w_router_expert_2"][g])).then_inc(ffn_in, 16)
            for stage, w in (("xk", "w_ck_2"), ("xv", "w_cv_2"), ("xq", "w_cq_2"), ("xout", "w_co_2")):
                project(stage, tiles(a[w]))
            experts_w = [a[n].rearrange("e (t p) f -> e p t f", p=P) for n in ("w1_2", "w3_2", "w2_2")]

            def expert_weights(j, expert, before=None):
                src = experts_w[j][bass.ds(expert, 1)].rearrange("o p t f -> p (o t) f")
                for n, (dst, half) in enumerate(pair(ring[:, j, :], src)):
                    for c in range(2):
                        if before is not None:
                            sp.wait_ge(piece_split[4 * j + 2 * n + c], before)
                    sp.dma_start(dst, half).then_inc(half_landed[2 * j + n], 16)

            for j in (2, 0, 1):
                sp.wait_ge(weights_used[j], chunks["moe"].before(j))
                expert_weights(j, 0)
            sp.wait_ge(row_ready, 3 * MT)
            sp.dma_start(h3_rows.rearrange("(m p) d -> p m d", p=P), h3_tok).then_inc(h3_stored, 16)
            for j in range(2):
                expert_weights(j, 1, 1)
            sp.wait_ge(plan_ready, 2)
            steps = sp.snap(sp.value_load(n_steps[0:1, 0:1], min_val=EXPERTS - 1, max_val=MAX_BLOCKS - 1))

            def planned(b):
                return sp.snap(sp.value_load(plan_row[0:1, bass.ds(b, 1)], min_val=0, max_val=EXPERTS - 1))

            with sp.Fori(0, sp.snap(steps - 1)) as r:
                e, e_before = planned(r + 2), planned(r + 1)
                for j in range(2):
                    expert_weights(j, e, r + 2)
                expert_weights(2, e_before, r + 1)
            expert_weights(2, planned(steps), steps)
            for m in range(MT):
                sp.wait_ge(x_ready, 3 + m + 1)
                sp.dma_start(out_v[:, m, :], x[:, m, :]).then_inc(out_done, 16)
            sp.wait_ge(out_done, MT * 16)

        @block.tensor
        def _(pe):
            def landed(stage, j, i=0):
                st = chunks[stage]
                pe.wait_ge(weights_landed[st.place(j)], (st.before(j, i) + 1) * 32)
                return ring[:, st.place(j), :]

            def bank(stage, k, i=0):
                st = banks[stage]
                n = st.before(k, i)
                if not (isinstance(n, int) and n == 0):
                    pe.wait_ge(bank_drained[st.place(k)], n)
                return ps[:, st.place(k), :]

            def filled(stage, k, last):
                last.then_inc(bank_filled[banks[stage].place(k)], 1)

            def product(o, lhs, rhs):
                for k, (l, r) in enumerate(zip(lhs, rhs)):
                    mm = pe.matmul(o, l, r, start=(k == 0), stop=(k == len(lhs) - 1))
                return mm

            def turn(stage, k, pieces, n=P, i=0):
                o = bank(stage, k, i)
                pe.nop().then_inc(turn_may_start, 1)
                for q, piece in enumerate(pieces):
                    rows = piece.shape[0]
                    f = int(np.prod(piece.shape[1:]))
                    mm = pe.transpose(o[0:f, q * n:q * n + rows], piece, ident[0:rows, 0:rows])
                filled(stage, k, mm)

            def project(stage, srcT, mtiles, widths):
                k = 0
                for j, n in enumerate(widths):
                    r = landed(stage, j)
                    w = r[:, 0:KT * n].rearrange("p (k n) -> p k n", k=KT)
                    for m in range(mtiles):
                        o = bank(stage, k)
                        mm = product(o[:, 0:n], [srcT[:, t, m * P:(m + 1) * P] for t in range(KT)],
                                     [w[:, t, :] for t in range(KT)])
                        mm.then_inc(bank_filled[banks[stage].place(k)], 1)
                        k += 1

            def mark(signal):
                pe.matmul(ps[:, 7, 0:1], mark_src[:, :], mark_src[:, 0:1], start=True, stop=True).then_inc(signal, 1)

            def split_product(o, lhs, rhs, start, stop):
                pe.matmul(o, lhs[1], rhs[0], start=start, stop=False)
                pe.matmul(o, lhs[0], rhs[1], start=False, stop=False)
                return pe.matmul(o, lhs[0], rhs[0], start=False, stop=stop)

            def hi_lo(v):
                return [v[:, h] for h in range(2)]

            def split(stage, p, i=0):
                st = pieces[stage]
                pe.wait_ge(dense_split[st.place(p)], st.before(p, i) + 1)
                return parts[:, st.place(p)]

            def used(stage, p):
                mark(piece_used[pieces[stage].place(p)])

            def split_project(stage, widths, first_bank=0, first_piece=0, i=0, ready=None):
                k, p = first_bank, first_piece
                for n in widths:
                    ks = 1024 // n
                    for q in range(KT // ks):
                        w = split(stage, p, i).rearrange("p h (k n) -> p h k n", k=ks)
                        for m in range(MT):
                            o = bank(stage, k + m, i) if q == 0 else ps[:, banks[stage].place(k + m), :]
                            for c in range(ks):
                                t = q * ks + c
                                if ready is not None and k == first_bank and m == 0:
                                    pe.wait_ge(actT_ready, ready + t + 1)
                                mm = split_product(o[:, 0:n], hi_lo(actT[:, :, t, m * P:(m + 1) * P]),
                                                   hi_lo(w[:, :, c, :]), t == 0, t == KT - 1)
                            if q == KT // ks - 1:
                                filled(stage, k + m, mm)
                        used(stage, p)
                        p += 1
                    k += MT

            pe.wait_ge(const_in, 16)
            pe.wait_ge(c_rep_ready, KT)
            pe.wait_ge(c_in, 32)
            for q in range(4):
                mark(piece_used[q])
            for j in range(6):
                g = (2, 3, 0, 1, 4, 5)[j]
                w = landed("ada", j).rearrange("p (k n) -> p k n", k=KT)
                o = bank("ada", j)
                for t in range(KT):
                    pe.matmul(o, c_rep[:, t, :], w[:, t, :], start=(t == 0), stop=False)
                filled("ada", j, pe.matmul(o, cst("ones", 1), bada[0:1, g * 512:(g + 1) * 512], start=False, stop=True))
                mark(weights_used[chunks["ada"].place(j)])

            pe.wait_ge(cols_in, 16 * 10)
            nrow = TAPS + 7
            o = bank("columns", 0)
            for t in range(KT):
                pe.transpose(o[:, t * nrow:(t + 1) * nrow], colrows[:, t * P:(t + 1) * P], ident[0:nrow, 0:nrow])
            filled("columns", 0, pe.transpose(o[:, KT * nrow:KT * nrow + 8], sgub_rows[:, :], ident[0:8, 0:8]))

            pe.wait_ge(h0_ready, MT)
            for t in range(KT):
                turn("hT", t, [h0[:, m, t * P:(t + 1) * P] for m in range(MT)])

            with pe.Fori(0, KT) as i:
                for j in range(5):
                    w = split("conv", j, i).rearrange("p h (k n) -> p h k n", k=KT)
                    o = bank("conv", j, i)
                    for t in range(KT):
                        if j == 0:
                            pe.wait_ge(actT_ready, t + 1)
                        mm = split_product(o, hi_lo(w[:, :, t, :]), hi_lo(actT[:, :, t, :]), t == 0, t == KT - 1)
                    filled("conv", j, mm)
                    used("conv", j)

            def four_tiles(outs, stage, k0, p0, i=0, ready=None):
                for q in range(4):
                    w = split(stage, p0 + q, i).rearrange("p h (k n) -> p h k n", k=2)
                    for k in range(4):
                        o = ps[:, banks[outs].place(k0 + k), :] if q else bank(outs, k0 + k, i)
                        for c in range(2):
                            if ready is not None and k == 0:
                                pe.wait_ge(actT_ready, ready + 2 * q + c + 1)
                            mm = split_product(o, hi_lo(w[:, :, c, k * P:(k + 1) * P]), hi_lo(actT[:, :, 2 * q + c, :]),
                                               q == 0 and c == 0, q == 3 and c == 1)
                        if q == 3:
                            filled(outs, k0 + k, mm)
                    used(stage, p0 + q)

            def head_qk(stage, k0, p0, i=0):
                four_tiles(stage, stage, k0, p0, i)

            def head_out(stage, h, i=0):
                split_project(stage, (HV, HV), 0, 0, i)
                pe.wait_ge(qk_ready, (h + 1) * 4)
                for j in range(MT):
                    o = bank(stage, 8 + j, i)[:, 0:S - j * P]
                    filled(stage, 8 + j, product(o, [qk_rot[:, 2 + c, j * P:(j + 1) * P] for c in range(2)],
                                                 [qk_rot[:, c, j * P:S] for c in range(2)]))
                pe.wait_ge(v_ready, (h + 1) * MT)
                for m in range(MT):
                    pe.wait_ge(decayed_ready, h * MT + m + 1)
                    filled(stage, 12 + m, product(bank(stage, 12 + m, i),
                                                  [decayed[:, j, m * P:(m + 1) * P] for j in range(m + 1)],
                                                  [v_tok[:, j, :] for j in range(m + 1)]))

            def head_turn(stage, k0, h, i=0):
                pe.wait_ge(ret_ready, (h + 1) * MT)
                for e in range(4):
                    turn(stage, k0 + e, [z_tok[:, m, e * P:(e + 1) * P] for m in range(MT)], i=i)

            head_qk("qk0", 0, 0)
            pe.wait_ge(conv_ready, KT)
            filled("ln", 0, product(bank("ln", 0), [cst("mean")] * KT, [convT[:, t, :] for t in range(KT)]))
            o = bank("ln", 1)
            for t in range(KT):
                pe.wait_ge(sq_ready, t + 1)
                mm = pe.matmul(o, cst("mean"), ln_sq[:, t % 2, :], start=(t == 0), stop=(t == KT - 1))
                if t < KT - 1:
                    mm.then_inc(sq_used, 1)
            filled("ln", 1, mm)

            with pe.Fori(0, HEADS - 1) as h:
                head_out("heads", h, h)
                head_qk("heads", 16, 8, h)
                head_turn("heads", 20, h, h)
            head_out("head_last", HEADS - 1)
            head_turn("head_last", 16, HEADS - 1)

            for n in range(3):
                for j in range(2):
                    four_tiles(f"mix{n}", "mix", 4 * j, 8 * n + 4 * j, ready=(n + 1) * KT)

            pe.wait_ge(merged_ready, KT)
            ws = [landed("out", j).rearrange("p (k n) -> p k n", k=KT) for j in range(2)]
            for k in range(8):
                m = OUT_TILES[k // 2]
                filled("out", k, product(bank("out", k), [mergedT[:, t, m * P:(m + 1) * P] for t in range(KT)],
                                         [ws[k % 2][:, t, :] for t in range(KT)]))

            def turn_rows(stage, src, n):
                pe.wait_ge(row_ready, n * MT)
                for t in range(KT):
                    turn(stage, t, [src[:, m, t * P:(t + 1) * P] for m in range(MT)])

            turn_rows("h2T", n_tok, 1)
            split_project("in2", (512, 256, 512, 512), ready=4 * KT)

            pe.wait_ge(qk2_ready, 2)
            for r in range(4):
                turn("qkT", r, [q_pair[:, m, r * P:(r + 1) * P] for m in range(MT)])
            turn("qkT", 4, [kv_tok[:, m, 0:P] for m in range(MT)])
            pe.wait_ge(sguw_in, 16)
            for c in range(2):
                turn("sguw", c, [sgu_w[:, 4 * c + g, :] for g in range(4)])
            def scores(n):
                stage, u = score_use(n)
                for v in range(2):
                    for rp in range(2):
                        o = bank(stage, u + 2 * v + rp).rearrange("p (a k) -> p a k", a=2)
                        for c in range(2):
                            mm = pe.matmul(o[:, c, :], qT[v * AD:(v + 1) * AD, 2 * rp + c, n * P:(n + 1) * P],
                                           kT[v * AD:(v + 1) * AD, n * P:(n + 2) * P], start=True, stop=True)
                        filled(stage, u + 2 * v + rp, mm)

            pe.wait_ge(qkT_ready, 5)
            scores(0)
            pe.wait_ge(sguwT_ready, 2)
            pe.wait_ge(vc_ready, 1)
            for gp in range(4):
                o = bank("sgu", gp).rearrange("p (a c d) -> p a c d", a=2, c=MT)
                for c in range(2):
                    g = 2 * gp + c
                    mm = pe.matmul(o[:, c], sgu_wT[:, g, :], g_tok[:, :, g * AD:(g + 1) * AD], start=True, stop=True)
                filled("sgu", gp, mm)
            for n in range(MT):
                if n < MT - 1:
                    scores(n + 1)
                u = weight_use(n)
                for hp in range(4):
                    pe.wait_ge(p_ready, AH * n + 2 * (hp + 1))
                    turn("attn", u + hp, [s_tok[n % 2][:, 2 * hp + c, w * P:(w + 1) * P] for c in range(2) for w in range(2)])
                o = bank("attn", u + 4)
                for hd in range(AH):
                    v = hd // 4
                    pe.wait_ge(pT_ready, 4 * n + hd // 2 + 1)
                    halves = (0, 1) if n else (1,)
                    for w in halves:
                        mm = pe.matmul(o[:, hd * AD:(hd + 1) * AD], pT[:, 2 * hd + w, :],
                                       kv_tok[:, n - 1 + w, P + v * AD:P + (v + 1) * AD],
                                       start=(w == halves[0]), stop=(w == 1))
                filled("attn", u + 4, mm)

            turn_rows("mixT", n_tok, 2)
            split_project("out2", (512, 512), ready=5 * KT)

            pe.wait_ge(vc_ready, 1 + MM)
            for c in range(4):
                turn("memT", c, [mem[:, m, (2 * c + q) * P:(2 * c + q + 1) * P] for q in range(2) for m in range(MM)])
            pe.wait_ge(memT_ready, KT)
            project("xk", memT, MM, (512, 512))
            project("xv", memT, MM, (512, 512))
            pe.wait_ge(vc_ready, 1 + MM + MT)
            for t in range(KT):
                turn("hqT", t, [n_tok[:, m, t * P:(t + 1) * P] for m in range(MT)])
            pe.wait_ge(xk_ready, 1)
            for c in range(4):
                turn("xkT", c, [xk_tok[:, m, (2 * c + q) * P:(2 * c + q + 1) * P] for q in range(2) for m in range(MM)])
            split_project("xq", (512, 512), ready=6 * KT)
            for t in range(KT):
                pe.wait_ge(xq_ready, 1 + t // 4)
                turn("xqT", t, [xq_tok[:, m, t * P:(t + 1) * P] for m in range(MT)])
            pe.wait_ge(xkT_ready, 4)
            pe.wait_ge(xqT_ready, KT)
            for m in range(MT):
                for hp in range(2):
                    o = bank("xs", 2 * m + hp).rearrange("p (a k) -> p a k", a=2)
                    for c in range(2):
                        hd = 2 * hp + c
                        mm = product(o[:, c, :], [xqT[:, 2 * hd + q, m * P:(m + 1) * P] for q in range(2)],
                                     [xkT[:, 2 * hd + q, :] for q in range(2)])
                    filled("xs", 2 * m + hp, mm)
            pe.wait_ge(xp_ready, MT * XH)
            for k in range(2 * XH):
                turn("xpT", k, [xp_tok[:, m, k // 2, (k % 2) * P:(k % 2 + 1) * P] for m in range(MT)])
            for t in range(KT):
                pe.wait_ge(xpT_ready, 2 * (t // 2 + 1))
                filled("xo", t, product(bank("xo", t), [xv_tok[:, w, t * P:(t + 1) * P] for w in range(MM)],
                                        [xpT[:, 2 * (t // 2) + w, :] for w in range(MM)]))
            split_project("xout", (512, 512), ready=7 * KT)

            turn_rows("h3T", h3_tok, 3)
            pe.wait_ge(ffn_in, 16 * (2 + GROUPS))
            o = bank("route", 0)
            nl = GROUPS + EXPERTS
            for m in range(MT):
                for t in range(KT):
                    pe.wait_ge(h3T_ready, t + 1)
                    mm = pe.matmul(o[:, m * nl:(m + 1) * nl], h3T[:, t, m * P:(m + 1) * P], wr[:, t, :],
                                   start=(t == 0), stop=(t == KT - 1))
            filled("route", 0, mm)
            pe.wait_ge(oh_ready, 1)
            o = bank("route", 1)
            product(o[:, 0:MT * EXPERTS], [cst("before"), cst("ones")],
                    [v.rearrange("p m e -> p (m e)") for v in (ohs, oh_before[:, 0:MT, :])])
            mm = product(o[:, MT * EXPERTS:(MT + 1) * EXPERTS], [cst("ones")], [oh_before[:, MT, :]])
            filled("route", 1, mm)
            pe.wait_ge(plan_col_ready, 1)
            filled("route", 2, pe.transpose(bank("route", 2)[0:1, 0:P], plan_col, ident))
            pe.wait_ge(slot_oh_ready, 1)
            filled("route", 3, product(bank("route", 3)[0:SLOTS, 0:64], [slot_oh[:, q, :] for q in range(2 * MT)],
                                       [block_oh[:, q, :] for q in range(2 * MT)]))

            def turn_slots(stage, k, rows, n, i=0):
                o = bank(stage, k, i)
                pe.nop().then_inc(turn_may_start, 1)
                for q in range(n):
                    mm = pe.transpose(o[:, q * SLOTS:(q + 1) * SLOTS], rows[0:SLOTS, q * P:(q + 1) * P], ident[0:SLOTS, 0:SLOTS])
                filled(stage, k, mm)

            pe.wait_ge(plan_ready, 2)
            steps = pe.snap(pe.value_load(n_steps[0:1, 0:1], min_val=EXPERTS - 1, max_val=MAX_BLOCKS - 1))
            pe.wait_ge(xg_in, 16)
            turn_slots("moe0", 0, xg, KT)

            def up(stage, b, i=0):
                st = banks[stage]
                pe.wait_ge(bank_drained[st.place(0)], st.before(0, i))
                for j in range(2):
                    o = bank(stage, 1 + j, i)[0:SLOTS, :]
                    for n in range(4):
                        pe.wait_ge(piece_split[4 * j + n], b + 1)
                        for c in range(2):
                            t = 2 * n + c
                            mm = split_product(o, hi_lo(xgT[:, :, t, :]), hi_lo(parts[:, n, :, c * 512:(c + 1) * 512]),
                                               t == 0, t == KT - 1)
                        if n == 3:
                            filled(stage, 1 + j, mm)
                        mark(piece_used[n])
                pe.wait_ge(xg_in, (b + 2) * 16)
                turn_slots(stage, 0, xg, KT, i)

            def down(c):
                st = banks["moe"]
                ys = [bank("moe", 4 + g, c)[0:SLOTS, :] for g in range(2)]
                pe.wait_ge(bank_drained[st.place(3)], st.before(3, c))
                for n in range(4):
                    pe.wait_ge(piece_split[8 + n], c + 1)
                    for g in range(2):
                        mm = split_product(ys[g], hi_lo(hidT[:, :, n, :]), hi_lo(parts[:, n, :, g * 512:(g + 1) * 512]),
                                           n == 0, n == 3)
                        if n == 3:
                            filled("moe", 4 + g, mm)
                    mark(piece_used[n])

            def turn_hidden(stage, b, i=0):
                pe.wait_ge(hid_ready, b + 1)
                turn_slots(stage, 3, hid, 4, i)

            up("moe_first", 0)
            turn_hidden("moe_first", 0)
            with pe.Fori(0, steps) as r:
                up("moe", r + 1, r)
                down(r)
                turn_hidden("moe", r + 1, r)
            down(steps)

        @block.scalar
        def _(act):
            own = Chain(act, act_own)

            def full(stage, k, i=0):
                st = banks[stage]
                act.wait_ge(bank_filled[st.place(k)], st.before(k, i) + 1)
                return ps[:, st.place(k), :]

            def drained(stage, k, ins):
                ins.then_inc(bank_drained[banks[stage].place(k)], 1)

            def release(stage, j):
                act.nop().then_inc(weights_used[chunks[stage].place(j)], 1)

            sets = [0]

            def roots(src, dst, eps_col, scale=1.0):
                sets[0] += 1
                act.wait_ge(ms_ready, sets[0])
                act.activation(dst, src, ACT.Sqrt, bias=eps[:, eps_col:eps_col + 1], scale=scale).then_inc(rms_ready, 1)

            roots(st_ms[:, 0:MT], st_rms[:, 0:MT], 0, 1.0 / D)
            act.wait_ge(angles_ready, 1)
            own(act.activation(sinT, angle, ACT.Sin))
            own(act.activation(cosT, turns, ACT.Sin))
            own.wait()
            act.nop().then_inc(rotary_ready, 1)
            def take_T(stage, col):
                for t in range(KT):
                    o = full(stage, t)
                    kw = {} if col is None else {"scale": cols[:, t, col:col + 1]}
                    act.activation(actT[:, 0, t, :], o, ACT.Copy, **kw).then_inc(actT_hi, 1)

            take_T("hT", None)

            act.nop().then_inc(gates_stored, 16)
            with act.Fori(0, KT) as i:
                own.enter(i, 2)
                act.wait_ge(gates_stored, (i + 1) * 16)
                act.activation(sig_u, full("conv", 1, i), ACT.Sigmoid).then_inc(sig_u_ready, 1)
                for g in range(2):
                    own(act.activation(sig_g[:, g, :], full("conv", 2 + g, i), ACT.Sigmoid))
                act.activation(sig_z, full("conv", 4, i), ACT.Sigmoid).then_inc(sig_z_ready, 1)
                own.wait()
                act.wait_ge(sig_u_ready, i + 1)
                for k in (1, 2, 3):
                    drained("conv", k, act.nop())
                act.dma_start(gates_dram[bass.ds(i, 1)].rearrange("o p g n -> p (o g) n"), sig_g).then_inc(gates_stored, 16)
            own.leave(KT)

            for t in range(KT):
                act.wait_ge(cen_ready, t + 1)
                if t >= 2:
                    act.wait_ge(sq_used, t - 1)
                act.activation(ln_sq[:, t % 2, :], convT[:, t, :], ACT.Square).then_inc(sq_ready, 1)
            o = full("ln", 1)
            own(act.activation(ln_std, o, ACT.Sqrt, bias=eps[:, 2:3]))
            own.wait()
            drained("ln", 1, act.nop())
            act.nop().then_inc(ln_std_ready, 1)
            for t in range(KT):
                act.wait_ge(ln_y_ready, t + 1)
                if t >= 2:
                    act.wait_ge(gated_conv_ready, t - 1)
                g, bias = cols[:, t, TAPS + 1:TAPS + 2], cols[:, t, TAPS + 2:TAPS + 3]
                own(act.activation(ln_y[:, t % 2, :], ln_y[:, t % 2, :], ACT.Identity, bias=bias, scale=g))
                own.wait()
                act.activation(ln_s[:, t % 2, :], ln_y[:, t % 2, :], ACT.Sigmoid).then_inc(ln_s_ready, 1)

            act.wait_ge(gated_conv_ready, KT)
            act.dma_start(conv_dram, convT).then_inc(conv_stored, 16)
            def high_T(srcs):
                for t, v in enumerate(srcs):
                    act.copy(actT[:, 0, t, :], v).then_inc(actT_hi, 1)

            def head(stage, turned, h, i=0, then=None):
                for m in range(MT):
                    o = full(stage, m, i)
                    own(act.copy(v_tok[:, m, :], o))
                    own.wait()
                    act.nop().then_inc(v_ready, 1)
                    drained(stage, m, act.nop())
                for m in range(MT):
                    o = full(stage, 4 + m, i)
                    if m >= 2:
                        act.wait_ge(sig_r_used, h * MT + (m - 1))
                    act.activation(sig_r[:, m % 2, :], o, ACT.Sigmoid).then_inc(sig_r_ready, 1)
                if then:
                    then()
                act.wait_ge(var_ready, h + 1)
                act.activation(st_std, mv.rearrange("p (m s) -> p m s", s=2)[:, :, 1], ACT.Sqrt,
                               bias=eps[:, 1:2]).then_inc(std_ready, 1)
                act.wait_ge(conv_stored, 16)
                for e in range(4):
                    o = full(stage, turned + e, i)
                    own(act.copy(retT[:, bass.ds(h * 4 + e, 1), :], o))
                    own.wait()
                    act.nop().then_inc(retT_ready, 1)
                    drained(stage, turned + e, act.nop())

            with act.Fori(0, HEADS - 1) as h:
                own.enter(h, 8)
                head("heads", 20, h, h)
            own.leave(HEADS - 1)
            head("head_last", 16, HEADS - 1, then=lambda: high_T([retT[:, t, :] for t in range(KT)]))
            act.wait_ge(retT_ready, HEADS * 4)
            act.dma_start(conv_backT, conv_dram).then_inc(conv_back, 16)
            full("mix0", 7)
            high_T([retT[:, KT + t, :] for t in range(KT)])
            act.wait_ge(conv_back, 16)
            full("mix1", 7)
            high_T([conv_backT[:, t, :] for t in range(KT)])

            def take(stage, k, dst, func=ACT.Copy, done=None, n=512, mtiles=None):
                o = full(stage, k)
                if mtiles and k % mtiles == mtiles - 1:
                    release(stage, k // mtiles)
                own(act.activation(dst, o[:, 0:n], func))
                own.wait()
                drained(stage, k, act.nop())
                if done is not None:
                    act.nop().then_inc(done, 1)

            act.wait_ge(merged_ready, KT)
            act.wait_ge(y_cleared, 16)
            act.dma_start(x[:, 1:MT, :], x_v[:, 1:MT, :]).then_inc(x_back, 16)
            act.dma_start(x0_early, x_v[:, 0, :]).then_inc(x_back, 16)
            for k in range(8):
                m = OUT_TILES[k // 2]
                take("out", k, y_tok[:, m, (k % 2) * 512:(k % 2 + 1) * 512], done=y_ready)
                if k >= 6:
                    release("out", k % 2)
                if k % 2:
                    for at in (m, MT + m):
                        roots(st_ms[:, at:at + 1], st_rms[:, at:at + 1], 0, 1.0 / D)

            take_T("h2T", TAPS + 3)
            for k in range(16):
                j, m = k // MT, k % MT
                dst, n = ((q_tok, 512), (kv_tok, 256), (u_tok, 512), (g_tok, 512))[j]
                take("in2", k, dst[:, m, :], ACT.Gelu_apprx_tanh if j >= 2 else ACT.Copy, done=in2_ready, n=n)
                if k in (MT - 1, 2 * MT - 1):
                    cnt_ = MT * (AH if k < MT else 2)
                    roots(st_ms[:, 0:cnt_], st_rms[:, 0:cnt_], 0, 1.0 / AD)
            roots(st_ms[:, 0:MT], st_rms[:, 0:MT], 0, 1.0 / 512)
            for r in range(4):
                take("qkT", r, qT[:, r, :], done=qkT_ready)
            take("qkT", 4, kT[:, P:], done=qkT_ready)
            for n in range(MT):
                act.wait_ge(smax_ready, n + 1)
                half = 16 * (n % 2)
                for hd in range(AH):
                    v = s_tok[n % 2][:, hd, :]
                    act.activation(v, v, ACT.Exp, bias=nmx[:, half + hd:half + hd + 1],
                                   accum_out=den[:, half + hd:half + hd + 1]).then_inc(p_ready, 1)
                sinkx = nmx[:, half + AH:half + 2 * AH]
                act.activation(sinkx, sinkx, ACT.Exp).then_inc(sink_exp, 1)
                if n == 0:
                    roots(st_ms[:, MT:2 * MT], st_rms[:, MT:2 * MT], 0, 1.0 / 512)
            roots(st_ms[:, 0:MT], st_rms[:, 0:MT], 0, 1.0 / 512)
            take_T("mixT", TAPS + 6)

            roots(st_ms[:, 0:MM], st_rms[:, 0:MM], 0, 1.0 / D)
            for c in range(4):
                o = full("memT", c).rearrange("p (q n) -> p q n", q=2)
                for q in range(2):
                    own(act.activation(memT[:, 2 * c + q, :], o[:, q, :], ACT.Copy, scale=cols[:, 2 * c + q, TAPS + 5:TAPS + 6]))
                own.wait()
                drained("memT", c, act.nop())
                for q in range(2):
                    act.nop().then_inc(memT_ready, 1)
            roots(st_ms[:, 0:MT], st_rms[:, 0:MT], 0, 1.0 / D)
            for stage, dst in (("xk", xk_tok), ("xv", xv_tok)):
                for k in range(4):
                    take(stage, k, dst[:, k % MM, (k // MM) * 512:(k // MM + 1) * 512], done=xkv_ready, mtiles=MM)
                if stage == "xk":
                    roots(st_ms[:, 0:MM * XH], st_rms[:, 0:MM * XH], 0, 1.0 / XD)
            take_T("hqT", TAPS + 4)
            for c in range(4):
                take("xkT", c, xkT[:, 2 * c:2 * c + 2, :].rearrange("p q n -> p (q n)"), done=xkT_ready)
            for k in range(8):
                take("xq", k, xq_tok[:, k % MT, (k // MT) * 512:(k // MT + 1) * 512], done=xq_in)
                if k % MT == MT - 1:
                    lo = k // MT * 2 * MT
                    roots(st_ms[:, lo:lo + 2 * MT], st_rms[:, lo:lo + 2 * MT], 0, 1.0 / XD)
            for t in range(KT):
                take("xqT", t, xqT[:, t, :], done=xqT_ready)
            for m in range(MT):
                for hp in range(2):
                    act.wait_ge(xmax_ready, 2 * m + hp + 1)
                    o = full("xs", 2 * m + hp).rearrange("p (a k) -> p a k", a=2)
                    for c in range(2):
                        hd = m * XH + 2 * hp + c
                        own(act.activation(xp_tok[:, m, 2 * hp + c, :], o[:, c, :], ACT.Exp, bias=nmx[:, hd:hd + 1],
                                           accum_out=den[:, hd:hd + 1]))
                    own.wait()
                    drained("xs", 2 * m + hp, act.nop())
                act.nop().then_inc(xq_in, 1)
            for k in range(8):
                take("xpT", k, xpT[:, k, :], done=xpT_ready)
            take_T("xo", None)

            for m in range(MT):
                act.wait_ge(x_tile_ready, m + 1)
                own(act.activation(xg, x[:, m, :], ACT.Square, accum_out=st_ms[:, m:m + 1]))
                own.wait()
            act.activation(st_rms[:, 0:MT], st_ms[:, 0:MT], ACT.Sqrt, bias=eps[:, 0:1], scale=1.0 / D).then_inc(rms_ready, 1)
            for t in range(KT):
                take("h3T", t, h3T[:, t, :], done=h3T_ready)
            def high(n, block, used):
                j = n // 4
                act.wait_ge(half_landed[2 * j + n % 4 // 2], (block + 1) * 16)
                act.wait_ge(piece_used[n % 4], used + 1)
                act.copy(parts[:, n % 4, 0, :], ring[:, j, n % 4 * 1024:(n % 4 + 1) * 1024]).then_inc(piece_hi, 1)

            for n in range(4):
                high(n, 0, pieces["moe_first"].before(n))
            act.wait_ge(gexp_in, 1)
            act.activation(gexp, gexp, ACT.Exp).then_inc(gexp_ready, 1)
            act.wait_ge(texp_in, 1)
            act.activation(dl, dl, ACT.Exp).then_inc(texp_ready, 1)
            act.wait_ge(plan_ready, 2)
            steps = act.snap(act.value_load(n_steps[0:1, 0:1], min_val=EXPERTS - 1, max_val=MAX_BLOCKS - 1))
            act.wait_ge(y_cleared, 16)
            act.nop().then_inc(y_stored, 16)

            def high_hidden(stage, i=0):
                o = full(stage, 3, i)
                act.copy(hidT[:, 0].rearrange("p t n -> p (t n)"), o[:, 0:4 * SLOTS]).then_inc(hidT_hi, 1)

            def high_rows(stage, k, i=0):
                act.copy(xgT[:, 0].rearrange("p t n -> p (t n)"), full(stage, k, i)).then_inc(xgT_hi, 1)

            def up(stage, b, pieces_, i=0):
                for n in pieces_:
                    high(n, b, pieces[stage].before(n, i))
                if 7 in pieces_:
                    act.activation(sg_h[0:SLOTS, :], full(stage, 1, i)[0:SLOTS, :], ACT.Sigmoid).then_inc(sg_h_ready, 1)

            def store_rows(c):
                act.wait_ge(y_stored, (c + 1) * 16)
                for g in range(2):
                    own(act.copy(y_blk[0:SLOTS, g * 512:(g + 1) * 512], full("moe", 4 + g, c)[0:SLOTS, :]))
                own.wait()
                for g in range(2):
                    drained("moe", 4 + g, act.nop())
                act.dma_start(y_rows[bass.ds(c * SLOTS, SLOTS), :], y_blk[0:SLOTS, :]).then_inc(y_stored, 16)

            def down(c):
                for n in range(4):
                    high(8 + n, c, pieces["moe"].before(8 + n, c))

            high_rows("moe0", 0)
            up("moe_first", 0, range(4, 8))
            high_rows("moe_first", 0)
            up("moe", 1, range(4))
            high_hidden("moe_first")
            up("moe", 1, range(4, 8))
            down(0)
            high_rows("moe", 0)
            with act.Fori(0, act.snap(steps - 1)) as r:
                own.enter(r, 2)
                up("moe", r + 2, range(4), r + 1)
                store_rows(r)
                high_hidden("moe", r)
                up("moe", r + 2, range(4, 8), r + 1)
                down(r + 1)
                high_rows("moe", 0, r + 1)
            own.base = act.snap((steps - 1) * own.per + own.at)
            own.count = 0
            store_rows(act.snap(steps - 1))
            high_hidden("moe", act.snap(steps - 1))
            for n in range(4):
                high(8 + n, steps, pieces["moe"].before(n, steps))
            store_rows(steps)
            act.wait_ge(y_stored, steps * 16 + 32)
            act.nop().then_inc(y_blk_ready, 1)

        @block.vector
        def _(dve):
            own = Chain(dve, dve_own)

            def full(stage, k, i=0):
                st = banks[stage]
                dve.wait_ge(bank_filled[st.place(k)], st.before(k, i) + 1)
                return ps[:, st.place(k), :]

            def drained(stage, k, ins):
                ins.then_inc(bank_drained[banks[stage].place(k)], 1)

            def mean_squares(srcs, dst, junk):
                for m, s in enumerate(srcs):
                    own(dve.tensor_tensor_reduce(out=junk, in0=s, in1=s, scale=1.0, scalar=0.0, op0=ALU.mult,
                                                 op1=ALU.add, accum_out=dst[:, m:m + 1]))
                    own.wait()
                dve.nop().then_inc(ms_ready, 1)

            def head_squares(src, groups, width, dst, junk):
                own(dve.tensor_tensor(junk, src, src, ALU.mult))
                own.wait()
                own(dve.tensor_reduce(dst, junk.rearrange("p (g d) -> p g d", d=width), AX.X, ALU.add))
                own.wait()

            sets = [0]

            def reciprocals(lo, hi):
                sets[0] += 1
                dve.wait_ge(rms_ready, sets[0])
                own(dve.reciprocal(st_r[:, lo:hi], st_rms[:, lo:hi]))
                own.wait()

            def low_T(stage, n, col):
                for t in range(KT):
                    o = full(stage, t)
                    dve.wait_ge(actT_hi, (n - 1) * KT + t + 1)
                    hi, lo = actT[:, 0, t, :].bitcast(F32), actT[:, 1, t, :]
                    if col is None:
                        own(dve.tensor_tensor(lo, o, hi, ALU.subtract))
                    else:
                        own(dve.scalar_tensor_tensor(out=lo, in0=o, scalar=cols[:, t, col:col + 1], in1=hi,
                                                     op0=ALU.mult, op1=ALU.subtract))
                    own.wait()
                    drained(stage, t, dve.nop())
                    dve.nop().then_inc(actT_ready, 1)

            for n, v in enumerate((RMS_EPS, GN_EPS, LN_EPS)):
                own(dve.memset(eps[:, n:n + 1], v))
            own(dve.memset(mark_src[:, :], 0.0))
            dve.wait_ge(const_in, 16)
            dve.wait_ge(c_in, 32)
            for t in range(KT):
                dve.tensor_scalar(c_rep[:, t, :], cst("ones"), c_col[:, t:t + 1], None, ALU.mult).then_inc(c_rep_ready, 1)
            dve.wait_ge(x_in, 16)
            own.wait()
            mean_squares([x0[:, m, :] for m in range(MT)], st_ms, h0[:, 0, :])

            dve.wait_ge(pos_in, 16)
            own(dve.tensor_copy(angle, pos_i[:, :]))
            own.wait()
            own(dve.tensor_scalar(angle, angle, cst("freq"), None, ALU.mult))
            own.wait()
            magic = float(1.5 * 2 ** 23)
            own(dve.tensor_scalar(turns, angle, float(1 / (2 * np.pi)), magic, ALU.mult, ALU.add))
            own.wait()
            own(dve.tensor_scalar(turns, turns, magic, None, ALU.subtract))
            own.wait()
            left = 2 * np.pi
            for bits in (5, 13, None):
                part = float(np.float32(left)) if bits is None else float(np.floor(left * 2 ** bits) / 2 ** bits)
                left -= part
                own(dve.scalar_tensor_tensor(out=angle, in0=turns, scalar=-part, in1=angle, op0=ALU.mult, op1=ALU.add))
                own.wait()
            lim = 3.1415925
            own(dve.tensor_scalar(angle, angle, lim, -lim, ALU.min, ALU.max))
            own.wait()
            own(dve.scalar_tensor_tensor(out=turns, in0=angle, scalar=-1.0, in1=angle, op0=ALU.mult, op1=ALU.max))
            own.wait()
            own(dve.tensor_scalar(turns, turns, -1.0, float(np.pi / 2), ALU.mult, ALU.add))
            own.wait()
            dve.nop().then_inc(angles_ready, 1)

            dve.wait_ge(rows_in, 32)
            for j in range(6):
                o = full("ada", j)
                half = slice((j % 2) * 512, (j % 2) * 512 + 512)
                if j < 2:
                    own(dve.scalar_tensor_tensor(out=mod_scale[:, half], in0=o, scalar=1.0, in1=pre_g[:, half],
                                                 op0=ALU.add, op1=ALU.mult))
                elif j < 4:
                    own(dve.tensor_copy(mod_shift[:, half], o))
                else:
                    own(dve.tensor_tensor(gate_post[:, half], o, post_g[:, half], ALU.mult))
                own.wait()
                drained("ada", j, dve.nop())
                if j == 3:
                    reciprocals(0, MT)
                    for m in range(MT):
                        own(dve.scalar_tensor_tensor(out=h0[:, m, :], in0=x0[:, m, :], scalar=st_r[:, m:m + 1],
                                                     in1=mod_scale, op0=ALU.mult, op1=ALU.mult))
                    own.wait()
                    for m in range(MT):
                        dve.tensor_tensor(h0[:, m, :], h0[:, m, :], mod_shift, ALU.add).then_inc(h0_ready, 1)

            o = full("columns", 0)
            nrow = TAPS + 7
            own(dve.tensor_copy(cols[:, :, :], o[:, 0:KT * nrow].rearrange("p (t r) -> p t r", t=KT)))
            own(dve.tensor_copy(sgub[:, :], o[:, KT * nrow:KT * nrow + 8]))
            own.wait()
            drained("columns", 0, dve.nop())

            dve.wait_ge(h0_ready, MT)
            low_T("hT", 1, None)
            dve.wait_ge(rotary_ready, 1)
            own(dve.memset(apad[:, 0:TAPS - 1], 0.0))
            own.wait()
            with dve.Fori(0, KT) as i:
                own.enter(i, 2 + TAPS + 1)
                o = full("conv", 0, i)
                dve.wait_ge(sig_u_ready, i + 1)
                own(dve.tensor_tensor(apad[:, TAPS - 1:], o, sig_u, ALU.mult))
                own.wait()
                drained("conv", 0, dve.nop())
                col = cols[:, bass.ds(i, 1), :].rearrange("p o r -> p (o r)")
                for j in range(TAPS):
                    acc = conv_acc[:, j % 2, :]
                    if j == 0:
                        own(dve.tensor_scalar(acc, apad[:, 0:S], col[:, 0:1], col[:, TAPS:TAPS + 1], ALU.mult, ALU.add))
                    elif j == 1:
                        own(dve.tensor_scalar(acc, apad[:, 1:1 + S], col[:, 1:2], None, ALU.mult))
                    else:
                        own.wait(1)
                        own(dve.scalar_tensor_tensor(out=acc, in0=apad[:, j:j + S], scalar=col[:, j:j + 1], in1=acc,
                                                     op0=ALU.mult, op1=ALU.add))
                own.wait()
                dve.wait_ge(sig_z_ready, i + 1)
                own(dve.tensor_tensor(zconvT[:, bass.ds(i, 1), :], full("conv", 4, i), sig_z, ALU.mult))
                own.wait()
                drained("conv", 4, dve.nop())
                own(dve.tensor_tensor(convT[:, bass.ds(i, 1), :], conv_acc[:, 0, :], conv_acc[:, 1, :], ALU.add))
                own.wait()
                dve.nop().then_inc(conv_ready, 1)
            own.leave(KT)

            def rotate(stage, k0, i=0):
                for part in range(2):
                    t1, t2 = full(stage, k0 + 2 * part, i), full(stage, k0 + 2 * part + 1, i)
                    own(dve.tensor_tensor(rot[:, 0, :], t1, cosT, ALU.mult))
                    own(dve.tensor_tensor(rot[:, 1, :], t2, sinT, ALU.mult))
                    own(dve.tensor_tensor(rot[:, 2, :], t1, sinT, ALU.mult))
                    own(dve.tensor_tensor(rot[:, 3, :], t2, cosT, ALU.mult))
                    own.wait()
                    for q in range(2):
                        drained(stage, k0 + 2 * part + q, dve.nop())
                    own(dve.tensor_tensor(qk_rot[:, 2 * part, :], rot[:, 0, :], rot[:, 1, :], ALU.subtract))
                    own(dve.tensor_tensor(qk_rot[:, 2 * part + 1, :], rot[:, 2, :], rot[:, 3, :], ALU.add))
                    own.wait()
                    for q in range(2):
                        dve.nop().then_inc(qk_ready, 1)

            dve.wait_ge(gates_stored, (KT + 1) * 16)
            rotate("qk0", 0)

            o = full("ln", 0)
            for t in range(KT):
                own(dve.tensor_tensor(convT[:, t, :], convT[:, t, :], o, ALU.subtract))
                own.wait()
                dve.nop().then_inc(cen_ready, 1)
            drained("ln", 0, dve.nop())
            dve.wait_ge(ln_std_ready, 1)
            own(dve.reciprocal(ln_rstd, ln_std))
            own.wait()
            for t in range(KT + 1):
                if t < KT:
                    if t >= 2:
                        dve.wait_ge(gated_conv_ready, t - 1)
                    dve.tensor_tensor(ln_y[:, t % 2, :], convT[:, t, :], ln_rstd, ALU.mult).then_inc(ln_y_ready, 1)
                if t:
                    q = t - 1
                    dve.wait_ge(ln_s_ready, q + 1)
                    own(dve.tensor_tensor(convT[:, q, :], ln_y[:, q % 2, :], ln_s[:, q % 2, :], ALU.mult))
                    own.wait()
                    dve.tensor_tensor(convT[:, q, :], convT[:, q, :], zconvT[:, q, :], ALU.mult).then_inc(gated_conv_ready, 1)

            dve.wait_ge(gated_conv_ready, KT)
            dve.nop().then_inc(decay_used, MT)
            def low_rows(n, srcs):
                for t, v in enumerate(srcs):
                    dve.wait_ge(actT_hi, (n - 1) * KT + t + 1)
                    own(dve.tensor_tensor(actT[:, 1, t, :], v, actT[:, 0, t, :].bitcast(F32), ALU.subtract))
                    own.wait()
                    dve.nop().then_inc(actT_ready, 1)

            def head_rows(stage, h, i=0, then=None):
                for m in range(MT):
                    o = full(stage, 4 + m, i)
                    dve.wait_ge(sig_r_ready, h * MT + m + 1)
                    own(dve.tensor_tensor(z_tok[:, m, :], o, sig_r[:, m % 2, :], ALU.mult))
                    own.wait()
                    dve.nop().then_inc(sig_r_used, 1)
                    drained(stage, 4 + m, dve.nop())
                dve.wait_ge(decay_in, (h + 1) * 16)
                for j in range(MT):
                    o = full(stage, 8 + j, i)
                    own(dve.tensor_tensor(decayed[:, j, j * P:S], o[:, 0:S - j * P], decay[:, 0:S - j * P], ALU.mult))
                    own.wait()
                    dve.nop().then_inc(decayed_ready, 1)
                    dve.nop().then_inc(decay_used, 1)
                    drained(stage, 8 + j, dve.nop())
                if then:
                    then()
                for m in range(MT):
                    own(dve.bn_stats(bn6[:, 6 * m:6 * m + 6], full(stage, 12 + m, i)))
                own.wait()
                dve.nop().then_inc(stats_settled, 1)
                for m in range(MT):
                    own(dve.bn_aggr(mv[:, 2 * m:2 * m + 2], bn6[:, 6 * m:6 * m + 6]))
                own.wait()
                dve.nop().then_inc(var_ready, 1)
                dve.wait_ge(std_ready, h + 1)
                own(dve.reciprocal(gn_r, st_std))
                own.wait()
                for m in range(MT):
                    o = ps[:, banks[stage].place(12 + m), :]
                    if m >= 2:
                        dve.wait_ge(ret_ready, h * MT + (m - 1))
                    own(dve.tensor_scalar(norm_o[:, m % 2, :], o, mv[:, 2 * m:2 * m + 1], gn_r[:, m:m + 1],
                                          ALU.subtract, ALU.mult))
                    own.wait()
                    drained(stage, 12 + m, dve.nop())
                    dve.tensor_tensor(z_tok[:, m, :], norm_o[:, m % 2, :], z_tok[:, m, :], ALU.mult).then_inc(ret_ready, 1)

            with dve.Fori(0, HEADS - 1) as h:
                own.enter(h, 12 + 5 * MT + 1)
                head_rows("heads", h, h)
                rotate("heads", 16, h)
            own.leave(HEADS - 1)
            head_rows("head_last", HEADS - 1, then=lambda: low_rows(2, [retT[:, t, :] for t in range(KT)]))

            for k in range(8):
                own(dve.tensor_copy(mergedT[:, k, :], full("mix0", k)))
                own.wait()
                drained("mix0", k, dve.nop())
            low_rows(3, [retT[:, KT + t, :] for t in range(KT)])
            for k in range(8):
                if k % 4 == 0:
                    dve.wait_ge(gates_in, 16 * (k // 4 + 1))
                own(dve.tensor_tensor(mergedT[:, k, :], full("mix1", k), mergedT[:, k, :], ALU.add))
                own.wait()
                drained("mix1", k, dve.nop())
                own(dve.tensor_tensor(mergedT[:, k, :], mergedT[:, k, :], gates[:, k % 4, :], ALU.mult))
                if k % 4 == 3:
                    own.wait()
                    dve.nop().then_inc(gates_used, 1)
            low_rows(4, [conv_backT[:, t, :] for t in range(KT)])
            for k in range(8):
                if k % 4 == 0:
                    dve.wait_ge(gates_in, 16 * (k // 4 + 3))
                own(dve.tensor_tensor(part_b, full("mix2", k), gates[:, k % 4, :], ALU.mult))
                own.wait()
                drained("mix2", k, dve.nop())
                if k % 4 == 3:
                    dve.nop().then_inc(gates_used, 1)
                own(dve.tensor_tensor(mergedT[:, k, :], mergedT[:, k, :], part_b, ALU.add))
                own.wait()
                dve.nop().then_inc(merged_ready, 1)

            dve.wait_ge(x_back, 32)
            for k, m in enumerate(OUT_TILES):
                dve.wait_ge(y_ready, 2 * (k + 1))
                mean_squares([y_tok[:, m, :]], st_ms[:, m:m + 1], squares)
                reciprocals(m, m + 1)
                own(dve.scalar_tensor_tensor(out=y_tok[:, m, :], in0=y_tok[:, m, :], scalar=st_r[:, m:m + 1],
                                             in1=gate_post, op0=ALU.mult, op1=ALU.mult))
                own.wait()
                own(dve.tensor_tensor(x[:, m, :], x[:, m, :] if m else x0_early, y_tok[:, m, :], ALU.add))
                own.wait()
                mean_squares([x[:, m, :]], st_ms[:, MT + m:MT + m + 1], squares)
                reciprocals(MT + m, MT + m + 1)
                dve.tensor_scalar(n_tok[:, m, :], x[:, m, :], st_r[:, MT + m:MT + m + 1], None, ALU.mult).then_inc(row_ready, 1)
            dve.nop().then_inc(x_ready, 1)

            def norm_rows(dst, done, junk):
                mean_squares([x[:, m, :] for m in range(MT)], st_ms, junk)
                reciprocals(0, MT)
                for m in range(MT):
                    dve.tensor_scalar(dst[:, m, :], x[:, m, :], st_r[:, m:m + 1], None, ALU.mult).then_inc(done, 1)

            low_T("h2T", 5, TAPS + 3)

            dve.wait_ge(gains_in, 64)
            dve.wait_ge(in2_ready, MT)
            dve.wait_ge(row_ready, MT)
            flat = lambda v: v.rearrange("p m d -> p (m d)")
            head_squares(flat(q_tok), 32, AD, st_ms[:, 0:32], flat(sq_junk))
            dve.nop().then_inc(ms_ready, 1)
            reciprocals(0, 32)

            def head_scale(v, nheads, width):
                r = st_r[:, 0:nheads].unsqueeze(2).to_broadcast([P, nheads, width])
                own(dve.tensor_tensor(v, v, r, ALU.mult))
                own.wait()

            head_scale(q_tok.rearrange("p m (h d) -> p (m h) d", d=AD), 32, AD)
            for m in range(MT):
                for v in range(2):
                    heads = q_tok[:, m, v * 256:(v + 1) * 256].rearrange("p (r d) -> p r d", d=AD)
                    pairs = q_pair[:, m, :].rearrange("p (r v d) -> p r v d", r=4, v=2)[:, :, v, :]
                    own(dve.scalar_tensor_tensor(out=pairs, in0=heads, scalar=AD ** -0.5,
                                                 in1=qn_row.unsqueeze(1).to_broadcast([P, 4, AD]),
                                                 op0=ALU.mult, op1=ALU.mult))
            own.wait()
            dve.nop().then_inc(qk2_ready, 1)
            dve.wait_ge(in2_ready, 2 * MT)
            for m in range(MT):
                own(dve.tensor_tensor(sq_junk[:, m, 0:P], kv_tok[:, m, 0:P], kv_tok[:, m, 0:P], ALU.mult))
            own.wait()
            for m in range(MT):
                own(dve.tensor_reduce(st_ms[:, 2 * m:2 * m + 2], sq_junk[:, m, 0:P].rearrange("p (g d) -> p g d", d=AD),
                                      AX.X, ALU.add))
            own.wait()
            dve.nop().then_inc(ms_ready, 1)
            reciprocals(0, 8)
            for m in range(MT):
                for v in range(2):
                    k = kv_tok[:, m, v * AD:(v + 1) * AD]
                    own(dve.scalar_tensor_tensor(out=k, in0=k, scalar=st_r[:, 2 * m + v:2 * m + v + 1], in1=kn_row,
                                                 op0=ALU.mult, op1=ALU.mult))
            own(dve.memset(kT[:, 0:P], 0.0))
            own.wait()
            dve.nop().then_inc(qk2_ready, 1)
            dve.wait_ge(in2_ready, 4 * MT)
            mean_squares([g_tok[:, m, :] for m in range(MT)], st_ms, sq_junk[:, 0, :])
            reciprocals(0, MT)
            for m in range(MT):
                own(dve.scalar_tensor_tensor(out=g_tok[:, m, :], in0=g_tok[:, m, :], scalar=st_r[:, m:m + 1], in1=sgun_row,
                                             op0=ALU.mult, op1=ALU.mult))
            own.wait()
            dve.nop().then_inc(vc_ready, 1)

            for c in range(2):
                o = full("sguw", c).rearrange("p (g i) -> p g i", g=4)
                own(dve.tensor_tensor(sgu_wT[:, 4 * c:4 * c + 4, :], o, cst("causalT").unsqueeze(1).to_broadcast([P, 4, P]), ALU.mult))
                own.wait()
                drained("sguw", c, dve.nop())
                dve.nop().then_inc(sguwT_ready, 1)
            def columns(v, n):
                lo = 16 * (n % 2)
                return v[:, lo:lo + AH], v[:, lo + AH:lo + 2 * AH]

            def window_max(n):
                mask = cst("band" if n else "first").unsqueeze(1).to_broadcast([P, 2, 2 * P])
                st = s_tok[n % 2]
                stage, u = score_use(n)
                for q in range(4):
                    o = full(stage, u + q).rearrange("p (a k) -> p a k", a=2)
                    own(dve.tensor_tensor(st[:, 2 * q:2 * q + 2, :], o, mask, ALU.add))
                    own.wait()
                    drained(stage, u + q, dve.nop())
                top_, (neg, sinkx) = columns(mx, n)[0], columns(nmx, n)
                own(dve.tensor_reduce(top_, st, AX.X, ALU.max))
                own.wait()
                own(dve.tensor_tensor(top_, top_, sink_row, ALU.max))
                own.wait()
                own(dve.tensor_scalar(neg, top_, -1.0, None, ALU.mult))
                own(dve.tensor_tensor(sinkx, sink_row, top_, ALU.subtract))
                own.wait()
                dve.nop().then_inc(smax_ready, 1)

            window_max(0)
            for gp in range(4):
                o = full("sgu", gp).rearrange("p (a c d) -> p a c d", a=2, c=MT)
                for c in range(2):
                    g = 2 * gp + c
                    u = u_tok[:, :, g * AD:(g + 1) * AD]
                    own(dve.scalar_tensor_tensor(out=u, in0=o[:, c], scalar=sgub[:, g:g + 1], in1=u, op0=ALU.add, op1=ALU.mult))
                own.wait()
                drained("sgu", gp, dve.nop())
            mean_squares([u_tok[:, m, :] for m in range(MT)], st_ms[:, MT:2 * MT], sgu_junk)
            reciprocals(MT, 2 * MT)
            for n in range(MT):
                if n < MT - 1:
                    window_max(n + 1)
                u = weight_use(n)
                total, inv = columns(den, n)[0], columns(mx, n)[1]
                dve.wait_ge(sink_exp, n + 1)
                dve.wait_ge(p_ready, AH * (n + 1))
                own(dve.tensor_tensor(total, total, columns(nmx, n)[1], ALU.add))
                own.wait()
                own(dve.reciprocal(inv, total))
                for hp in range(4):
                    own(dve.tensor_copy(pT[:, 4 * hp:4 * hp + 4, :].rearrange("p a k -> p (a k)"), full("attn", u + hp)))
                    own.wait()
                    drained("attn", u + hp, dve.nop())
                    dve.nop().then_inc(pT_ready, 1)
                o = full("attn", u + 4).rearrange("p (h d) -> p h d", d=AD)
                own(dve.tensor_tensor(attn_tok[:, n, :].rearrange("p (h d) -> p h d", d=AD), o,
                                      inv.unsqueeze(2).to_broadcast([P, AH, AD]), ALU.mult))
                own.wait()
                drained("attn", u + 4, dve.nop())
                own(dve.tensor_tensor_reduce(out=sgu_junk, in0=attn_tok[:, n, :], in1=attn_tok[:, n, :], scale=1.0, scalar=0.0,
                                             op0=ALU.mult, op1=ALU.add, accum_out=st_ms[:, n:n + 1]))
                own.wait()
            dve.nop().then_inc(ms_ready, 1)
            reciprocals(0, MT)
            for m in range(MT):
                own(dve.tensor_scalar(n_tok[:, m, 0:512], attn_tok[:, m, :], st_r[:, m:m + 1], None, ALU.mult))
            own.wait()

            for m in range(MT):
                dve.tensor_scalar(n_tok[:, m, 512:], u_tok[:, m, :], st_r[:, MT + m:MT + m + 1], None, ALU.mult).then_inc(row_ready, 1)

            low_T("mixT", 6, TAPS + 6)

            def add_out(stage, tile_done=None):
                for k in range(8):
                    v = x[:, k % MT, (k // MT) * 512:(k // MT + 1) * 512]
                    o = full(stage, k)
                    own(dve.tensor_tensor(v, o, v, ALU.add))
                    own.wait()
                    drained(stage, k, dve.nop())
                    if tile_done is not None and k >= MT:
                        dve.nop().then_inc(tile_done, 1)
                dve.nop().then_inc(x_ready, 1)

            dve.wait_ge(mem_in, 48)
            mean_squares([mem[:, m, :] for m in range(MM)], st_ms, x_sq)
            reciprocals(0, MM)
            for m in range(MM):
                own(dve.tensor_scalar(mem[:, m, :], mem[:, m, :], st_r[:, m:m + 1], None, ALU.mult))
                own.wait()
                dve.nop().then_inc(vc_ready, 1)
            add_out("out2")

            own(dve.tensor_scalar(cqn_row, cqn_row, XD ** -0.5, None, ALU.mult))
            norm_rows(n_tok, vc_ready, x_sq)
            dve.wait_ge(xkv_ready, 4)
            for m in range(MM):
                head_squares(xk_tok[:, m, :], XH, XD, st_ms[:, XH * m:XH * (m + 1)], x_sq)
            dve.nop().then_inc(ms_ready, 1)
            reciprocals(0, MM * XH)

            def scale_head(v, col, gain):
                own(dve.scalar_tensor_tensor(out=v, in0=v, scalar=st_r[:, col:col + 1], in1=gain, op0=ALU.mult, op1=ALU.mult))

            for m in range(MM):
                for hd in range(XH):
                    scale_head(xk_tok[:, m, hd * XD:(hd + 1) * XD], m * XH + hd, ckn_row)
            own.wait()
            dve.nop().then_inc(xk_ready, 1)
            low_T("hqT", 7, TAPS + 4)
            for half in range(2):
                dve.wait_ge(xq_in, MT * (half + 1))
                lo = half * 2 * MT
                for m in range(MT):
                    for c in range(2):
                        v = xq_tok[:, m, (2 * half + c) * XD:(2 * half + c + 1) * XD]
                        k = 2 * m + c
                        own(dve.tensor_tensor_reduce(out=x_sq[:, k % 4 * XD:(k % 4 + 1) * XD], in0=v, in1=v, scale=1.0, scalar=0.0,
                                                     op0=ALU.mult, op1=ALU.add, accum_out=st_ms[:, lo + k:lo + k + 1]))
                    if m % 2:
                        own.wait()
                dve.nop().then_inc(ms_ready, 1)
                reciprocals(lo, lo + 2 * MT)
                for m in range(MT):
                    for c in range(2):
                        hd = 2 * half + c
                        scale_head(xq_tok[:, m, hd * XD:(hd + 1) * XD], lo + 2 * m + c, cqn_row)
                own.wait()
                dve.nop().then_inc(xq_ready, 1)
            for m in range(MT):
                for hp in range(2):
                    hd = m * XH + 2 * hp
                    o = full("xs", 2 * m + hp).rearrange("p (a k) -> p a k", a=2)
                    own(dve.tensor_reduce(mx[:, hd:hd + 2], o, AX.X, ALU.max))
                    own.wait()
                    own(dve.tensor_scalar(nmx[:, hd:hd + 2], mx[:, hd:hd + 2], -1.0, None, ALU.mult))
                    own.wait()
                    dve.nop().then_inc(xmax_ready, 1)
            for m in range(MT):
                dve.wait_ge(xq_in, 8 + m + 1)
                own(dve.reciprocal(mx[:, m * XH:(m + 1) * XH], den[:, m * XH:(m + 1) * XH]))
                own.wait()
                for hd in range(XH):
                    v = xp_tok[:, m, hd, :]
                    dve.tensor_scalar(v, v, mx[:, m * XH + hd:m * XH + hd + 1], None, ALU.mult).then_inc(xp_ready, 1)
            low_T("xo", 8, None)
            add_out("xout", x_tile_ready)

            dve.wait_ge(ffn_in, 16 * (2 + GROUPS))
            own(dve.memset(lg[:, :, GROUPS:8], -3.0e38))
            reciprocals(0, MT)
            for m in range(MT):
                dve.scalar_tensor_tensor(out=h3_tok[:, m, :], in0=x[:, m, :], scalar=st_r[:, m:m + 1], in1=ffn_row,
                                         op0=ALU.mult, op1=ALU.mult).then_inc(row_ready, 1)
            o = full("route", 0)[:, 0:MT * (GROUPS + EXPERTS)].rearrange("p (m e) -> p m e", m=MT)
            own(dve.tensor_copy(lg[:, :, 0:GROUPS], o[:, :, 0:GROUPS]))
            own(dve.tensor_copy(lg[:, :, 8:], o[:, :, GROUPS:]))
            own.wait()
            drained("route", 0, dve.nop())
            for m in range(MT):
                own(dve.max(top[:, m, :], lg[:, m, 0:8]))
            own.wait()
            for m in range(MT):
                own(dve.max_index(top_i[:, m, :], top[:, m, :], lg[:, m, 0:8]))
                own(dve.tensor_scalar(gexp[:, 4 * m:4 * m + 4], lg[:, m, 0:GROUPS], top[:, m, 0:1], None, ALU.subtract))
            own.wait()
            own(dve.tensor_copy(gidx, top_i[:, :, 0]))
            own.wait()
            for m in range(MT):
                own(dve.tensor_scalar(goh[:, 4 * m:4 * m + 4], cst("iota")[:, 0:GROUPS], gidx[:, m:m + 1], None, ALU.is_equal))
            own.wait()
            dve.nop().then_inc(gexp_in, 1)
            for g in range(GROUPS):
                for m in range(MT):
                    src, sel = lg[:, m, 8 + 8 * g:16 + 8 * g], goh[:, 4 * m + g:4 * m + g + 1]
                    if g == 0:
                        own(dve.tensor_scalar(loc[:, m, :], src, sel, None, ALU.mult))
                    else:
                        own(dve.scalar_tensor_tensor(out=loc[:, m, :], in0=src, scalar=sel, in1=loc[:, m, :],
                                                     op0=ALU.mult, op1=ALU.add))
                own.wait()
            for m in range(MT):
                own(dve.max(top[:, m, :], loc[:, m, :]))
            own.wait()
            for m in range(MT):
                own(dve.max_index(top_i[:, m, :], top[:, m, :], loc[:, m, :]))
            own(dve.tensor_tensor(dl, top[:, :, 1], top[:, :, 0], ALU.subtract))
            own.wait()
            dve.nop().then_inc(texp_in, 1)
            for q in range(2):
                own(dve.tensor_copy(eid[:, q * MT:(q + 1) * MT], top_i[:, :, q]))
            own.wait()
            for q in range(2):
                own(dve.scalar_tensor_tensor(out=eid[:, q * MT:(q + 1) * MT], in0=gidx, scalar=float(PER_GROUP),
                                             in1=eid[:, q * MT:(q + 1) * MT], op0=ALU.mult, op1=ALU.add))
            own.wait()
            for c in range(2 * MT):
                own(dve.tensor_scalar(oh[:, c, :], cst("iota")[:, 0:EXPERTS], eid[:, c:c + 1], None, ALU.is_equal))
            own.wait()
            for m in range(MT):
                own(dve.tensor_tensor(ohs[:, m, :], oh[:, m, :], oh[:, MT + m, :], ALU.add))
            own(dve.memset(oh_before[:, 0, :], 0.0))
            for m in range(MT):
                own.wait()
                own(dve.tensor_tensor(oh_before[:, m + 1, :], oh_before[:, m, :], ohs[:, m, :], ALU.add))
            own.wait()
            dve.nop().then_inc(oh_ready, 1)
            dve.wait_ge(gexp_ready, 1)
            own(dve.tensor_reduce(gsum, gexp.rearrange("p (m g) -> p m g", g=GROUPS), AX.X, ALU.add))
            dve.wait_ge(texp_ready, 1)
            own(dve.tensor_scalar(tden, dl, 1.0, None, ALU.add))
            own.wait()
            own(dve.tensor_tensor(tden, tden, gsum, ALU.mult))
            own.wait()
            own(dve.reciprocal(w01[:, 0:MT], tden))
            own.wait()
            own(dve.tensor_tensor(w01[:, MT:], w01[:, 0:MT], dl, ALU.mult))
            def low(n, done):
                dve.wait_ge(piece_hi, done + 1)
                dve.tensor_tensor(parts[:, n % 4, 1, :], ring[:, n // 4, n % 4 * 1024:(n % 4 + 1) * 1024],
                                  parts[:, n % 4, 0, :].bitcast(F32), ALU.subtract).then_inc(piece_split[n], 1)

            for n in range(3):
                low(n, n)
            o = full("route", 1)
            own(dve.tensor_copy(ranks.rearrange("p m e -> p (m e)"), o[:, 0:MT * EXPERTS]))
            own(dve.tensor_copy(cnt, o[:, MT * EXPERTS:(MT + 1) * EXPERTS]))
            own.wait()
            drained("route", 1, dve.nop())
            own(dve.tensor_scalar(nblk, cnt, float(SLOTS), None, ALU.is_gt))
            own.wait()
            for j in range(2, S // SLOTS):
                own(dve.scalar_tensor_tensor(out=nblk, in0=cnt, scalar=float(j * SLOTS), in1=nblk, op0=ALU.is_gt, op1=ALU.add))
                own.wait()
            own(dve.tensor_tensor_scan(incl, cst("ones")[:, 0:EXPERTS], nblk, float(EXPERTS), ALU.mult, ALU.add))
            own.wait()
            own(dve.tensor_tensor(bstart, incl, nblk, ALU.subtract))
            own(dve.tensor_scalar(n_steps[:, :], incl[0:1, EXPERTS - 1:EXPERTS], 1.0, None, ALU.subtract))
            own(dve.tensor_scalar(e_tmp[:, 0, :], incl, cst("token")[:, 0:1], 0.0, ALU.is_le, ALU.add, accum_out=plan_col))
            own.wait()
            own(dve.tensor_tensor(plan_col, plan_col, cst("first_blocks"), ALU.add))
            own.wait()
            own(dve.tensor_scalar(plan_col, plan_col, float(EXPERTS - 1), None, ALU.min))
            own.wait()
            dve.nop().then_inc(plan_col_ready, 1)
            dve.nop().then_inc(plan_ready, 1)
            expert = cst("iota")[:, 0:EXPERTS]
            own(dve.tensor_tensor(bstart, bstart, expert, ALU.subtract))
            own.wait()
            own(dve.tensor_scalar(bstart, bstart, 1.0, float(SLOTS), ALU.subtract, ALU.mult))
            own.wait()
            for m in range(MT):
                own(dve.scalar_tensor_tensor(out=place_e[:, m, :], in0=ranks[:, m, :], scalar=float(SLOTS - 1), in1=bstart,
                                             op0=ALU.is_gt, op1=ALU.mult))
            own.wait()
            for m in range(MT):
                own(dve.scalar_tensor_tensor(out=ranks[:, m, :], in0=expert, scalar=float(SLOTS), in1=ranks[:, m, :],
                                             op0=ALU.mult, op1=ALU.add))
            own.wait()
            own(dve.tensor_tensor(place_e, place_e, ranks, ALU.add))
            own.wait()
            for q in range(2):
                own(dve.tensor_tensor(e_tmp[:, q * MT:(q + 1) * MT, :], oh[:, q * MT:(q + 1) * MT, :], place_e, ALU.mult))
            own.wait()
            own(dve.tensor_reduce(destf, e_tmp, AX.X, ALU.add))
            own.wait()
            own(dve.tensor_copy(dest_i[:, 0, :], destf))
            own.wait()
            own(dve.tensor_scalar(dest_i[:, 1, :], dest_i[:, 0, :], SLOTS.bit_length() - 1, None, ALU.logical_shift_right))
            own(dve.tensor_scalar(dest_i[:, 2, :], dest_i[:, 0, :], SLOTS - 1, None, ALU.bitwise_and))
            own.wait()
            own(dve.tensor_copy(blkf, dest_i[:, 1, :]))
            own(dve.tensor_copy(inf_, dest_i[:, 2, :]))
            own.wait()
            for c in range(2 * MT):
                own(dve.tensor_scalar(slot_oh[:, c, :], cst("iota")[:, 0:SLOTS], inf_[:, c:c + 1], None, ALU.is_equal))
                own(dve.tensor_scalar(block_oh[:, c, :], cst("iota"), blkf[:, c:c + 1],
                                      cst("token")[:, c % MT:c % MT + 1], ALU.is_equal, ALU.mult))
            own.wait()
            dve.nop().then_inc(slot_oh_ready, 1)
            own(dve.tensor_copy(plan_row[:, :], full("route", 2)[0:1, 0:P]))
            own.wait()
            drained("route", 2, dve.nop())
            dve.nop().then_inc(plan_ready, 1)
            own(dve.tensor_copy(slot_tok[:, :], full("route", 3)[0:SLOTS, 0:64]))
            own.wait()
            drained("route", 3, dve.nop())
            dve.nop().then_inc(slots_ready, 1)

            steps = dve.snap(dve.value_load(n_steps[0:1, 0:1], min_val=EXPERTS - 1, max_val=MAX_BLOCKS - 1))
            moe = Chain(dve, dve_moe)

            def rest(stage, k, dst, i=0):
                n = dst.shape[2] * dst.shape[3]
                d = [dst[:, h].rearrange("p t n -> p (t n)") for h in range(2)]
                drained(stage, k, dve.tensor_tensor(d[1], full(stage, k, i)[:, 0:n], d[0].bitcast(F32), ALU.subtract))

            def low_hidden(stage, c, i=0):
                dve.wait_ge(hidT_hi, c + 1)
                rest(stage, 3, hidT, i)

            def gate(stage, b, i=0):
                dve.wait_ge(sg_h_ready, b + 1)
                moe(dve.tensor_tensor(t_h[0:SLOTS, :], full(stage, 1, i)[0:SLOTS, :], sg_h[0:SLOTS, :], ALU.mult))
                moe.wait()
                drained(stage, 1, dve.nop())

            def hidden(stage, b, i=0):
                moe(dve.tensor_tensor(hid[0:SLOTS, :], full(stage, 2, i)[0:SLOTS, :], t_h[0:SLOTS, :], ALU.mult))
                moe.wait()
                drained(stage, 2, dve.nop())
                dve.nop().then_inc(hid_ready, 1)
                dve.wait_ge(xgT_hi, b + 2)
                rest(stage, 0, xgT, i)

            dve.wait_ge(xgT_hi, 1)
            rest("moe0", 0, xgT)
            for n in (4, 5, 6):
                low(n, n)
            gate("moe_first", 0)
            hidden("moe_first", 0)
            for n in (0, 1, 2):
                low(n, 8 + n)
            low_hidden("moe_first", 0)
            for n in (4, 5, 6):
                low(n, 8 + n)
            gate("moe", 1)
            for n in (8, 9, 10):
                low(n, 8 + n)
            hidden("moe", 1)
            with dve.Fori(0, dve.snap(steps - 1)) as r:
                moe.enter(r, 2)
                for n in (0, 1, 2):
                    low(n, r * 12 + (20 + n))
                low_hidden("moe", r + 1, r)
                for n in (4, 5, 6):
                    low(n, r * 12 + (20 + n))
                gate("moe", r + 2, r + 1)
                for n in (8, 9, 10):
                    low(n, r * 12 + (20 + n))
                hidden("moe", r + 2, r + 1)
            moe.leave(None)
            low_hidden("moe", steps, dve.snap(steps - 1))
            for n in (8, 9, 10, 11):
                low(n, steps * 12 + n)
            for c in range(2 * MT):
                q, m = c % 2, c // 2
                dve.wait_ge(combo_in[c % 4], 16 * (c // 4 + 1))
                if q:
                    dve.wait_ge(combo_used, c)
                ins = dve.scalar_tensor_tensor(out=x[:, m, :], in0=combo[:, c % 4, :], scalar=w01[:, q * MT + m:q * MT + m + 1],
                                               in1=x[:, m, :], op0=ALU.mult, op1=ALU.add)
                ins.then_inc(combo_used, 1)
                if q:
                    dve.wait_ge(combo_used, c + 1)
                    dve.nop().then_inc(x_ready, 1)

        @block.gpsimd
        def _(pool):
            own = Chain(pool, pool_own)
            one = cst("ones")[:, 0:1].to_broadcast([P, 1024])

            def split_chunk(stage, j, first, n, i=0):
                st, pc = chunks[stage], pieces[stage]
                pool.wait_ge(weights_landed[st.place(j)], (st.before(j, i) + 1) * 32)
                for k in range(n):
                    q = pc.place(first + k)
                    w = ring[:, st.place(j), k * 1024:(k + 1) * 1024]
                    pool.wait_ge(piece_used[q], pc.before(first + k, i) + 1)
                    own(pool.tensor_tensor(parts[:, q, 0, :], w, one, ALU.mult))
                    own.wait()
                    pool.tensor_tensor(parts[:, q, 1, :], w, parts[:, q, 0, :].bitcast(F32),
                                       ALU.subtract).then_inc(dense_split[q], 1)
                pool.wait_ge(dense_split[q], pc.before(first + n - 1, i) + 1)
                pool.nop().then_inc(weights_used[st.place(j)], 1)

            pool.wait_ge(const_in, 16)
            with pool.Fori(0, KT) as i:
                own.enter(i, 5)
                for j, (first, n) in enumerate(((0, 2), (2, 2), (4, 1))):
                    split_chunk("conv", j, first, n, i)
            own.leave(KT)
            split_chunk("qk0", 0, 0, 4)
            with pool.Fori(0, HEADS - 1) as h:
                own.enter(h, 12)
                for j in range(3):
                    split_chunk("heads", j, 4 * j, 4, h)
            own.leave(HEADS - 1)
            pool.wait_ge(gated_conv_ready, KT)
            pool.memset(zeros, 0.0).then_inc(zero_ready, 1)
            for j in range(2):
                split_chunk("head_last", j, 4 * j, 4)
            for j in range(6):
                split_chunk("mix", j, 4 * j, 4)
            for j, (first, n) in enumerate(((0, 4), (4, 2), (6, 4), (10, 4))):
                split_chunk("in2", j, first, n)
            for stage in ("out2", "xq", "xout"):
                for j in range(2):
                    split_chunk(stage, j, 4 * j, 4)

            def low(n, done):
                pool.wait_ge(piece_hi, done + 1)
                pool.tensor_tensor(parts[:, n % 4, 1, :], ring[:, n // 4, n % 4 * 1024:(n % 4 + 1) * 1024],
                                   parts[:, n % 4, 0, :].bitcast(F32), ALU.subtract).then_inc(piece_split[n], 1)

            low(3, 3)
            pool.wait_ge(h3_stored, 16)
            pool.wait_ge(slots_ready, 1)
            steps = pool.snap(pool.value_load(n_steps[0:1, 0:1], min_val=EXPERTS - 1, max_val=MAX_BLOCKS - 1))

            def gather(b):
                pool.tensor_copy(idx[:, :], slot_tok[:, bass.ds(b, 1)]).then_inc(idx_ready, 1)
                pool.wait_ge(idx_ready, b + 1)
                pool.nop().then_inc(idx_settled, 1)
                pool.indirect_dma_start(xg[0:SLOTS, :], None, h3_rows,
                                        bass.IndirectOffsetOnAxis(ap=idx[:, 0:1], axis=0)).then_inc(xg_in, 16)

            def turned(stage, i=0):
                st = banks[stage]
                pool.wait_ge(bank_filled[st.place(0)], st.before(0, i))

            gather(0)
            turned("moe_first")
            gather(1)
            low(7, 7)
            with pool.Fori(0, steps) as r:
                turned("moe", r)
                gather(r + 2)
                for n in (3, 7, 11):
                    low(n, r * 12 + (8 + n))
            pool.wait_ge(y_blk_ready, 1)
            for c in range(2 * MT):
                q, m = c % 2, c // 2
                if c >= 4:
                    pool.wait_ge(combo_used, c - 3)
                pool.indirect_dma_start(combo[:, c % 4, :], None, y_rows, bass.IndirectOffsetOnAxis(
                    ap=dest_i[:, 0, q * MT + m:q * MT + m + 1].bitcast(U32), axis=0)).then_inc(combo_in[c % 4], 16)


_INS = ["x", "c", "positions", "w_ada", "b_ada", "pre_norm_g", "w_in", "conv_w", "conv_b", "conv_ln_g", "conv_ln_b",
        "w_ret_out", "w_conv_out", "w_out", "post_norm_g", "mem_2", "norm_mix_2", "w_in_2", "q_norm_2", "k_norm_2",
        "attn_sinks_2", "sgu_norm_2", "sgu_w_2", "sgu_b_2", "out_norm_attn_2", "out_norm_sgu_2", "w_out_2",
        "norm_cross_2", "norm_mem_2", "w_cq_2", "w_ck_2", "w_cv_2", "cq_norm_2", "ck_norm_2", "w_co_2", "norm_ffn_2",
        "w_router_group_2", "w_router_expert_2", "w1_2", "w3_2", "w2_2"]


def kernel(**inputs):
    import concourse.bacc as _bacc
    from concourse.bass_utils import run_bass_kernel_spmd as _run

    nc = _bacc.Bacc("TRN2", target_bir_lowering=False, num_devices=1)
    arrays = {name: np.ascontiguousarray(inputs[name]) for name in _INS}
    arrays["const"], arrays["decay"] = const_table(), decay_table()
    args = {name: nc.dram_tensor(f"in_{name}", v.shape, mybir.dt.from_np(v.dtype), kind="ExternalInput").ap()
            for name, v in arrays.items()}
    out = nc.dram_tensor("out_0", (1, S, D), F32, kind="ExternalOutput").ap()
    build(nc, args, out)
    r = _run(nc, [{f"in_{k}": v for k, v in arrays.items()}], core_ids=[0])
    return r.results[0]["out_0"]
```
